# Optimizing a Trainium2 kernel written in Bass

```python
import math
import jax, jax.numpy as jnp
from jax import lax
import numpy as np
import jax
import jax.numpy as jnp

D_MODEL = 1024
BATCH = 1
SEQ = 256
DEPTH = 1

ROPE_THETA = 500000.0
NORM_EPS = 1e-6
BLOCK_Q = 128
MLA_HEADS = 8
MLA_NOPE_DIM = 64
MLA_ROPE_DIM = 32
MLA_QK_DIM = MLA_NOPE_DIM + MLA_ROPE_DIM
MLA_V_DIM = 64
MLA_Q_RANK = 384
MLA_KV_RANK = 256
MLA_WIDTH = MLA_HEADS * MLA_V_DIM
DIFF_HEADS = 4
DIFF_HEAD_DIM = 64
DIFF_V_DIM = 2 * DIFF_HEAD_DIM
DIFF_ROT_DIM = DIFF_HEAD_DIM // 4
DIFF_QK_WIDTH = DIFF_HEADS * 2 * DIFF_HEAD_DIM
DIFF_WIDTH = DIFF_HEADS * DIFF_V_DIM
N_BRANCHES = 2
IN_SIZES = (MLA_Q_RANK, MLA_KV_RANK, MLA_ROPE_DIM, DIFF_QK_WIDTH, DIFF_QK_WIDTH, DIFF_WIDTH, N_BRANCHES * D_MODEL)
IN_WIDTH = MLA_Q_RANK + MLA_KV_RANK + MLA_ROPE_DIM + 2 * DIFF_QK_WIDTH + DIFF_WIDTH + N_BRANCHES * D_MODEL
FFN_HIDDEN = ((-(-8 * D_MODEL // 3) + 255) // 256) * 256


def rmsnorm(x, g):
    xf = x.astype(jnp.float32)
    y = xf * lax.rsqrt(jnp.mean(xf * xf, axis=-1, keepdims=True) + NORM_EPS)
    return (y * g.astype(jnp.float32)).astype(x.dtype)

def apply_rope(x, positions, rot_dim):
    half = rot_dim // 2
    inv_freq = jnp.exp(-math.log(ROPE_THETA) * jnp.arange(half, dtype=jnp.float32) * (2.0 / rot_dim))
    ang = positions.astype(jnp.float32)[..., None] * inv_freq
    ang = ang.reshape(ang.shape[:2] + (1,) * (x.ndim - 3) + (half,))
    cos, sin = jnp.cos(ang), jnp.sin(ang)
    xr = x[..., :rot_dim].astype(jnp.float32)
    x1, x2 = xr[..., :half], xr[..., half:]
    rot = jnp.concatenate([x1 * cos - x2 * sin, x2 * cos + x1 * sin], axis=-1).astype(x.dtype)
    return jnp.concatenate([rot, x[..., rot_dim:]], axis=-1)

def causal_attention(q, k, v):
    B, S, H, Dk = q.shape
    Dv = v.shape[-1]
    nb = S // BLOCK_Q
    scale = Dk ** -0.5
    qb = q.reshape(B, nb, BLOCK_Q, H, Dk).transpose(1, 0, 2, 3, 4)
    kpos = jnp.arange(S)

    def one_block(args):
        qi, i = args
        s = jnp.einsum('bqhd,bkhd->bhqk', qi, k).astype(jnp.float32) * scale
        qpos = i * BLOCK_Q + jnp.arange(BLOCK_Q)
        s = jnp.where(kpos[None, :] <= qpos[:, None], s, -jnp.inf)
        p = jax.nn.softmax(s, axis=-1).astype(v.dtype)
        return jnp.einsum('bhqk,bkhd->bqhd', p, v)

    out = lax.map(one_block, (qb, jnp.arange(nb)))
    return out.transpose(1, 0, 2, 3, 4).reshape(B, S, H, Dv)

def first_inputs(seed: int = 0) -> dict:
    key = jax.random.key(seed)
    ks = jax.random.split(key, 24)

    def dense(k, fan_in, fan_out):
        return jax.random.normal(k, (DEPTH, fan_in, fan_out), jnp.float32) * fan_in ** -0.5

    def gain(k, n):
        return 1.0 + 0.02 * jax.random.normal(k, (DEPTH, n), jnp.float32)

    def small(k, n, s):
        return s * jax.random.normal(k, (DEPTH, n), jnp.float32)

    x = jax.random.normal(ks[0], (BATCH, SEQ, D_MODEL), jnp.float32)
    positions = jnp.broadcast_to(jnp.arange(SEQ, dtype=jnp.int32)[None, :], (BATCH, SEQ))
    return {
        "x": x,
        "positions": positions,
        "norm_mix_g": gain(ks[1], D_MODEL),
        "w_in": dense(ks[2], D_MODEL, IN_WIDTH),
        "b_gate": small(ks[3], N_BRANCHES * D_MODEL, 0.1),
        "mla_q_norm_g": gain(ks[4], MLA_Q_RANK),
        "mla_w_uq": dense(ks[5], MLA_Q_RANK, MLA_HEADS * MLA_QK_DIM),
        "mla_kv_norm_g": gain(ks[6], MLA_KV_RANK),
        "mla_w_ukv": dense(ks[7], MLA_KV_RANK, MLA_HEADS * (MLA_NOPE_DIM + MLA_V_DIM)),
        "diff_lambda_q1": small(ks[8], DIFF_HEAD_DIM, 0.1),
        "diff_lambda_k1": small(ks[9], DIFF_HEAD_DIM, 0.1),
        "diff_lambda_q2": small(ks[10], DIFF_HEAD_DIM, 0.1),
        "diff_lambda_k2": small(ks[11], DIFF_HEAD_DIM, 0.1),
        "diff_subln_g": gain(ks[12], DIFF_V_DIM),
        "w_branch_mla": dense(ks[13], MLA_WIDTH, D_MODEL),
        "w_branch_diff": dense(ks[14], DIFF_WIDTH, D_MODEL),
        "w_out": dense(ks[15], D_MODEL, D_MODEL),
        "norm_ffn_g": gain(ks[16], D_MODEL),
        "w_ffn_gate": dense(ks[17], D_MODEL, FFN_HIDDEN),
        "w_ffn_up": dense(ks[18], D_MODEL, FFN_HIDDEN),
        "w_ffn_down": dense(ks[19], FFN_HIDDEN, D_MODEL),
        "norm_final_g": 1.0 + 0.02 * jax.random.normal(ks[20], (D_MODEL,), jnp.float32),
    }

def first_block(x, positions, norm_mix_g, w_in, b_gate, mla_q_norm_g, mla_w_uq, mla_kv_norm_g, mla_w_ukv,
              diff_lambda_q1, diff_lambda_k1, diff_lambda_q2, diff_lambda_k2, diff_subln_g,
              w_branch_mla, w_branch_diff, w_out, norm_ffn_g, w_ffn_gate, w_ffn_up, w_ffn_down, norm_final_g):
    B, S, _ = x.shape
    split_idx = [int(v) for v in np.cumsum(IN_SIZES)[:-1]]
    for l in range(DEPTH):
        xn = rmsnorm(x, norm_mix_g[l])
        proj = jnp.einsum('bsd,de->bse', xn, w_in[l])
        q_lat, kv_lat, k_rope, dq, dk, dv, gate_pre = jnp.split(proj, split_idx, axis=-1)

        q = jnp.einsum('bsr,re->bse', rmsnorm(q_lat, mla_q_norm_g[l]), mla_w_uq[l])
        q = q.reshape(B, S, MLA_HEADS, MLA_QK_DIM)
        q_nope, q_pe = q[..., :MLA_NOPE_DIM], apply_rope(q[..., MLA_NOPE_DIM:], positions, MLA_ROPE_DIM)
        kv = jnp.einsum('bsr,re->bse', rmsnorm(kv_lat, mla_kv_norm_g[l]), mla_w_ukv[l])
        kv = kv.reshape(B, S, MLA_HEADS, MLA_NOPE_DIM + MLA_V_DIM)
        k_nope, v_mla = kv[..., :MLA_NOPE_DIM], kv[..., MLA_NOPE_DIM:]
        k_pe = apply_rope(k_rope[:, :, None, :], positions, MLA_ROPE_DIM)
        q_mla = jnp.concatenate([q_nope, q_pe], axis=-1)
        k_mla = jnp.concatenate([k_nope, jnp.broadcast_to(k_pe, (B, S, MLA_HEADS, MLA_ROPE_DIM))], axis=-1)
        o_mla = causal_attention(q_mla, k_mla, v_mla).reshape(B, S, MLA_WIDTH)

        dq = apply_rope(dq.reshape(B, S, DIFF_HEADS, 2, DIFF_HEAD_DIM), positions, DIFF_ROT_DIM)
        dk = apply_rope(dk.reshape(B, S, DIFF_HEADS, 2, DIFF_HEAD_DIM), positions, DIFF_ROT_DIM)
        dv = dv.reshape(B, S, DIFF_HEADS, DIFF_V_DIM)
        o1 = causal_attention(dq[..., 0, :], dk[..., 0, :], dv)
        o2 = causal_attention(dq[..., 1, :], dk[..., 1, :], dv)
        lambda_init = 0.8 - 0.6 * math.exp(-0.3 * l)
        lam = (jnp.exp(jnp.sum(diff_lambda_q1[l].astype(jnp.float32) * diff_lambda_k1[l].astype(jnp.float32)))
               - jnp.exp(jnp.sum(diff_lambda_q2[l].astype(jnp.float32) * diff_lambda_k2[l].astype(jnp.float32)))
               + lambda_init).astype(o1.dtype)
        o_diff = rmsnorm(o1 - lam * o2, diff_subln_g[l]) * (1.0 - lambda_init)
        o_diff = o_diff.reshape(B, S, DIFF_WIDTH)

        gates = jax.nn.sigmoid(gate_pre + b_gate[l])
        g_mla, g_diff = gates[..., :D_MODEL], gates[..., D_MODEL:]
        merged = (g_mla * jnp.einsum('bse,ed->bsd', o_mla, w_branch_mla[l])
                  + g_diff * jnp.einsum('bse,ed->bsd', o_diff, w_branch_diff[l]))
        x = x + jnp.einsum('bsd,de->bse', merged, w_out[l])

        hn = rmsnorm(x, norm_ffn_g[l])
        hid = jax.nn.silu(jnp.einsum('bsd,df->bsf', hn, w_ffn_gate[l])) * jnp.einsum('bsd,df->bsf', hn, w_ffn_up[l])
        x = x + jnp.einsum('bsf,fd->bsd', hid, w_ffn_down[l])
    return rmsnorm(x, norm_final_g)


GRID_W = 64
CTX_LEN = 256
D_MIX = D_MODEL
D_POOL = D_MIX // 2
POOL_WINDOWS = (2, 4, 8, 16)
POOL_GW = D_POOL // len(POOL_WINDOWS)
D_ATTN = D_MIX - D_POOL
NA_HEADS = 8
NA_HEAD_DIM = D_ATTN // NA_HEADS
NA_KH_MAX = 8
NA_KW = 16
D_IN = D_POOL + 3 * D_ATTN
PEER_HEADS = 8
PEER_NKEYS = 128
PEER_N_EXPERTS = PEER_NKEYS * PEER_NKEYS
PEER_TOPK = 16
PEER_DKEY = 256
PEER_TOKEN_BLOCK = 128
N_MOD = 6
EPS = 1e-6


def rmsnorm_2(x, g):
    xf = x.astype(jnp.float32)
    y = xf * lax.rsqrt(jnp.mean(xf * xf, axis=-1, keepdims=True) + EPS)
    return (y * g.astype(jnp.float32)).astype(x.dtype)

def modulate(h, shift, scale):
    return h * (1 + scale) + shift

def multiscale_pool(p, w_grp, scale):
    B, L, _ = p.shape
    pf = p.astype(jnp.float32)
    cs = jnp.concatenate([jnp.zeros((B, 1, D_POOL), jnp.float32), jnp.cumsum(pf, axis=1)], axis=1)
    t = jnp.arange(L)
    outs = []
    for g, w in enumerate(POOL_WINDOWS):
        sl = slice(g * POOL_GW, (g + 1) * POOL_GW)
        lo = jnp.clip(t - w // 2, 0, L)
        hi = jnp.clip(t + w // 2, 0, L)
        csg = cs[..., sl]
        cnt = (hi - lo).astype(jnp.float32)[None, :, None]
        outs.append((jnp.take(csg, hi, axis=1) - jnp.take(csg, lo, axis=1)) / cnt - pf[..., sl])
    pooled = jnp.stack(outs, axis=2).astype(p.dtype)
    y = jnp.einsum('blgc,gcd->blgd', pooled, w_grp).reshape(B, L, D_POOL)
    return y * scale

def neighbourhood_attention(q, k, v, k_ctx, v_ctx, rpb):
    B, S, H, Dh = q.shape
    rows = S // GRID_W
    kh = min(NA_KH_MAX, rows)
    n_loc = kh * NA_KW
    qg = q.reshape(B, rows, GRID_W, H, Dh)
    kg = k.reshape(B, rows, GRID_W, H, Dh)
    vg = v.reshape(B, rows, GRID_W, H, Dh)
    col = jnp.arange(GRID_W)
    c0 = jnp.clip(col - NA_KW // 2, 0, GRID_W - NA_KW)
    col_idx = c0[:, None] + jnp.arange(NA_KW)[None, :]
    col_off = col_idx - col[:, None] + (NA_KW - 1)
    scale = Dh ** -0.5

    def row_block(r):
        r0 = jnp.clip(r - kh // 2, 0, rows - kh)
        k_rows = lax.dynamic_slice_in_dim(kg, r0, kh, axis=1)
        v_rows = lax.dynamic_slice_in_dim(vg, r0, kh, axis=1)
        k_win = k_rows[:, :, col_idx]
        v_win = v_rows[:, :, col_idx]
        q_r = lax.dynamic_index_in_dim(qg, r, axis=1, keepdims=False)
        row_off = r0 + jnp.arange(kh) - r + (NA_KH_MAX - 1)
        bias = rpb[:, row_off[None, :, None], col_off[:, None, :]].astype(jnp.float32)
        s_loc = jnp.einsum('bwhd,biwjhd->bhwij', q_r, k_win).astype(jnp.float32) * scale + bias
        s_ctx = jnp.einsum('bwhd,bchd->bhwc', q_r, k_ctx).astype(jnp.float32) * scale
        s_all = jnp.concatenate([s_loc.reshape(B, H, GRID_W, n_loc), s_ctx], axis=-1)
        prob = jax.nn.softmax(s_all, axis=-1)
        p_loc = prob[..., :n_loc].reshape(B, H, GRID_W, kh, NA_KW).astype(v.dtype)
        p_ctx = prob[..., n_loc:].astype(v.dtype)
        return (jnp.einsum('bhwij,biwjhd->bwhd', p_loc, v_win)
                + jnp.einsum('bhwc,bchd->bwhd', p_ctx, v_ctx))

    out = lax.map(row_block, jnp.arange(rows))
    return jnp.moveaxis(out, 0, 1).reshape(B, S, H * Dh)

def context_attention(q, k, v):
    B, C, H, Dh = q.shape
    s = jnp.einsum('bqhd,bkhd->bhqk', q, k).astype(jnp.float32) * (Dh ** -0.5)
    prob = jax.nn.softmax(s, axis=-1).astype(v.dtype)
    return jnp.einsum('bhqk,bkhd->bqhd', prob, v).reshape(B, C, H * Dh)

def peer(h, w_q, sub_keys, u, v):
    B, L, D = h.shape
    tok = h.reshape((B * L) // PEER_TOKEN_BLOCK, PEER_TOKEN_BLOCK, D)
    k = PEER_TOPK

    def block(xb):
        tb = xb.shape[0]
        q = (xb @ w_q).reshape(tb, PEER_HEADS, 2, PEER_DKEY // 2)
        s = jnp.einsum('thpd,hpnd->thpn', q, sub_keys).astype(jnp.float32)
        sv, si = lax.top_k(s, k)
        cand = (sv[:, :, 0, :, None] + sv[:, :, 1, None, :]).reshape(tb, PEER_HEADS, k * k)
        cand_idx = (si[:, :, 0, :, None] * PEER_NKEYS + si[:, :, 1, None, :]).reshape(tb, PEER_HEADS, k * k)
        top_v, top_i = lax.top_k(cand, k)
        experts = jnp.take_along_axis(cand_idx, top_i, axis=-1)
        g = jax.nn.softmax(top_v, axis=-1)
        u_e = u[experts]
        v_e = v[experts]
        a = jax.nn.gelu(jnp.einsum('td,thkd->thk', xb, u_e).astype(jnp.float32), approximate=False)
        return jnp.einsum('thk,thkd->td', (g * a).astype(xb.dtype), v_e)

    return lax.map(block, tok).reshape(B, L, D)

def split_heads(t):
    B, L, _ = t.shape
    return t.reshape(B, L, NA_HEADS, NA_HEAD_DIM)

def second_inputs(seed: int = 0) -> dict:
    key = jax.random.key(seed)
    ks = jax.random.split(key, 18)
    f32 = jnp.float32
    D = D_MODEL

    def nrm(k, shape, s):
        return jax.random.normal(k, shape, f32) * s

    return {
        'x': nrm(ks[0], (BATCH, SEQ, D), 1.0),
        'c': nrm(ks[1], (BATCH, D), 1.0),
        'ctx': nrm(ks[2], (BATCH, CTX_LEN, D), 1.0),
        'c_ctx': nrm(ks[3], (D,), 1.0),
        'ada_w': nrm(ks[4], (DEPTH, D, N_MOD * D), 0.5 * D ** -0.5),
        'ada_b': nrm(ks[5], (DEPTH, N_MOD * D), 0.01),
        'norm1_g': 1.0 + nrm(ks[6], (DEPTH, D), 0.05),
        'w_in': nrm(ks[7], (DEPTH, D, D_IN), D ** -0.5),
        'pool_w': nrm(ks[8], (DEPTH, len(POOL_WINDOWS), POOL_GW, POOL_GW), POOL_GW ** -0.5),
        'pool_scale': 1.0 + nrm(ks[9], (DEPTH, D_POOL), 0.1),
        'na_rpb': nrm(ks[10], (DEPTH, NA_HEADS, 2 * NA_KH_MAX - 1, 2 * NA_KW - 1), 0.2),
        'w_out': nrm(ks[11], (DEPTH, D_MIX, D), D_MIX ** -0.5),
        'norm2_g': 1.0 + nrm(ks[12], (DEPTH, D), 0.05),
        'peer_wq': nrm(ks[13], (DEPTH, D, PEER_HEADS * PEER_DKEY), D ** -0.5),
        'peer_keys': nrm(ks[14], (DEPTH, PEER_HEADS, 2, PEER_NKEYS, PEER_DKEY // 2), (PEER_DKEY // 2) ** -0.5),
        'peer_u': nrm(ks[15], (DEPTH, PEER_N_EXPERTS, D), D ** -0.5),
        'peer_v': nrm(ks[16], (DEPTH, PEER_N_EXPERTS, D), 0.5),
        'final_g': 1.0 + nrm(ks[17], (D,), 0.05),
    }

def second_block(x, c, ctx, c_ctx, ada_w, ada_b, norm1_g, w_in, pool_w, pool_scale, na_rpb, w_out,
              norm2_g, peer_wq, peer_keys, peer_u, peer_v, final_g):
    kv_cols = slice(D_POOL + D_ATTN, D_IN)
    for layer in range(DEPTH):
        last = layer == DEPTH - 1
        mod_x = (jax.nn.silu(c) @ ada_w[layer] + ada_b[layer])[:, None, :]
        mod_c = jax.nn.silu(c_ctx) @ ada_w[layer] + ada_b[layer]
        sh1, sc1, g1, sh2, sc2, g2 = jnp.split(mod_x, N_MOD, axis=-1)
        csh1, csc1, cg1, csh2, csc2, cg2 = jnp.split(mod_c, N_MOD, axis=-1)

        hx = modulate(rmsnorm_2(x, norm1_g[layer]), sh1, sc1)
        hc = modulate(rmsnorm_2(ctx, norm1_g[layer]), csh1, csc1)
        zx = hx @ w_in[layer]
        px = zx[..., :D_POOL]
        qx = split_heads(zx[..., D_POOL:D_POOL + D_ATTN])
        kx = split_heads(zx[..., D_POOL + D_ATTN:D_POOL + 2 * D_ATTN])
        vx = split_heads(zx[..., D_POOL + 2 * D_ATTN:])
        zc_kv = hc @ w_in[layer][:, kv_cols]
        kc = split_heads(zc_kv[..., :D_ATTN])
        vc = split_heads(zc_kv[..., D_ATTN:])

        pool_x = multiscale_pool(px, pool_w[layer], pool_scale[layer])
        attn_x = neighbourhood_attention(qx, kx, vx, kc, vc, na_rpb[layer])
        x = x + g1 * (jnp.concatenate([pool_x, attn_x], axis=-1) @ w_out[layer])

        if not last:
            zc_pq = hc @ w_in[layer][:, :D_POOL + D_ATTN]
            pool_c = multiscale_pool(zc_pq[..., :D_POOL], pool_w[layer], pool_scale[layer])
            attn_c = context_attention(split_heads(zc_pq[..., D_POOL:]), kc, vc)
            ctx = ctx + cg1 * (jnp.concatenate([pool_c, attn_c], axis=-1) @ w_out[layer])

        h2 = modulate(rmsnorm_2(x, norm2_g[layer]), sh2, sc2)
        x = x + g2 * peer(h2, peer_wq[layer], peer_keys[layer], peer_u[layer], peer_v[layer])
        if not last:
            h2c = modulate(rmsnorm_2(ctx, norm2_g[layer]), csh2, csc2)
            ctx = ctx + cg2 * peer(h2c, peer_wq[layer], peer_keys[layer], peer_u[layer], peer_v[layer])

    return rmsnorm_2(x, final_g)


def setup_inputs(seed=0):
    out = dict(first_inputs(seed))
    for name, value in second_inputs(seed + 1).items():
        if name != "x":
            out[name + "_2"] = value
    return out


def reference(
    x, positions, norm_mix_g, w_in, b_gate, mla_q_norm_g, mla_w_uq, mla_kv_norm_g, mla_w_ukv,
    diff_lambda_q1, diff_lambda_k1, diff_lambda_q2, diff_lambda_k2, diff_subln_g, w_branch_mla,
    w_branch_diff, w_out, norm_ffn_g, w_ffn_gate, w_ffn_up, w_ffn_down, norm_final_g, c_2,
    ctx_2, c_ctx_2, ada_w_2, ada_b_2, norm1_g_2, w_in_2, pool_w_2, pool_scale_2, na_rpb_2,
    w_out_2, norm2_g_2, peer_wq_2, peer_keys_2, peer_u_2, peer_v_2, final_g_2,
):
    x = first_block(
        x, positions, norm_mix_g, w_in, b_gate, mla_q_norm_g, mla_w_uq, mla_kv_norm_g,
        mla_w_ukv, diff_lambda_q1, diff_lambda_k1, diff_lambda_q2, diff_lambda_k2, diff_subln_g,
        w_branch_mla, w_branch_diff, w_out, norm_ffn_g, w_ffn_gate, w_ffn_up, w_ffn_down,
        norm_final_g,
    )
    return second_block(
        x, c_2, ctx_2, c_ctx_2, ada_w_2, ada_b_2, norm1_g_2, w_in_2, pool_w_2, pool_scale_2,
        na_rpb_2, w_out_2, norm2_g_2, peer_wq_2, peer_keys_2, peer_u_2, peer_v_2, final_g_2,
    )


_drawn_inputs = setup_inputs


def setup_inputs(seed=0):
    import zlib

    import numpy as np

    out = dict(_drawn_inputs(seed))
    spreads = {}
    factors = {'norm_mix_g': 2.706,
     'b_gate': 2.768,
     'mla_q_norm_g': 8.0,
     'mla_kv_norm_g': 8.0,
     'diff_lambda_k1': 8.0,
     'diff_lambda_q2': 8.0,
     'diff_subln_g': 5.108,
     'norm_ffn_g': 3.403,
     'ada_b_2': 4.395,
     'norm1_g_2': 4.705,
     'pool_scale_2': 2.796,
     'na_rpb_2': 8.0,
     'norm2_g_2': 8.6}
    for name, (base, spread) in spreads.items():
        noise = np.random.default_rng([zlib.crc32(name.encode()), seed]).standard_normal(out[name].shape)
        drawn = base * np.exp(spread * noise) if base else spread * noise
        out[name] = jnp.asarray(drawn.astype(out[name].dtype))
    for name, factor in factors.items():
        out[name] = (out[name] * factor).astype(out[name].dtype)
    return out
```

```python
import math

import numpy as np

import concourse.bass as bass
from concourse import mybir
from concourse.alu_op_type import AluOpType as ALU

F32 = mybir.dt.float32
U32 = mybir.dt.uint32
I32 = mybir.dt.int32
ACT = mybir.ActivationFunctionType
AXX = mybir.AxisListType.X

P = 128
D = 1024
T = 256
NT = T // P
DC = D // P
EPS = 1e-6
THETA = 500000.0
MLA_H, NOPE, ROPE, MLA_V, Q_RANK, KV_RANK = 8, 64, 32, 64, 384, 256
MLA_QK = NOPE + ROPE
DIFF_H, DIFF_D, DIFF_ROT = 4, 64, 16
DIFF_V = 2 * DIFF_D
LAT = Q_RANK + KV_RANK + ROPE
FFN = 2816
LAMBDA_INIT = 0.8 - 0.6 * math.exp(-0.3 * 0)
NA_H, NA_D, GRID_W, NA_KW, NA_KH_MAX = 8, 64, 64, 16, 8
ROWS = T // GRID_W
POOL_WINDOWS = (2, 4, 8, 16)
D_POOL = 512
PE_H, NKEYS, TOPK = 8, 128, 16
MASKED = -1e30
LOWEST = -3.4e38

COLS = {}
_at = 0
for _name, _n in (("norm_mix_g", 8), ("q_norm_g", 3), ("kv_norm_g", 2), ("b_gate", 16), ("norm_ffn_g", 8),
                  ("c", 8), ("c_ctx", 8), ("norm1_g", 8), ("norm2_g", 8), ("pool_scale", 4), ("ada_b", 48)):
    COLS[_name] = (_at, _n)
    _at += _n
N_COLS = _at
K_IDENT, K_ONES, K_IOTA, K_MASK, K_FREQ = 0, 128, 256, 384, 640
HALF_M, HALF_D = ROPE // 2, DIFF_ROT // 2
N_FREQ = HALF_M + HALF_D
N_CONST = K_FREQ + N_FREQ

RING_SLOTS, SLOT = 5, 2048

G_WORDS = NKEYS * T
OFF = dict(
    act_T=0, ctx_T=2048, gates_T=4096,
    dq=8192, dk=9216, dv=10240, lat=11264, qm=12608, kv=14144, km=16192, lat_T=17728,
    qm_T=19008, km_T=21056, dq_T=23104, dk_T=24128, o_mla=25152, o_diff=26176, oa_T=27200, ob_T=28224,
    merged_T=29248,
    hid_T=8192, ada_x=13824, ada_c=19968,
    zx=8192, zc=22016, q_T=12288, k_T=13312, kc_T=14336, mix_T=15360, attn=17408, pooled_T=18432,
    g1row=29248,
    rope_tmp=31296, rope=31808, small=32096,
    pq_T=24064, s=8192, s_work=12288, v12=14336, i12=14848, i12f=15360, cand=16384, cand_work=18432,
    eq=20480, tv=22528, topi=22912, ab=23040,
)


class Lane:

    def __init__(self, name, sem):
        self.name, self.sem, self.count, self.steps = name, sem, 0, []

    def __call__(self, issue, *after, signal=True):
        self.steps.append((issue, frozen(after), signal))
        self.count += signal
        return (self.sem, self.count) if signal else None

    def play(self, eng):
        passed = {}
        for issue, after, signal in self.steps:
            for tick in flat(after):
                sem, value = tick
                if passed.get(id(sem), 0) < value:
                    eng.wait_ge(sem, value)
                    passed[id(sem)] = value
            ins = issue(eng)
            if signal is True:
                ins.then_inc(self.sem, 1)


def frozen(ticks):
    return tuple(frozen(t) for t in ticks) if isinstance(ticks, (list, tuple)) else ticks


def flat(ticks):
    for t in ticks:
        if t is None:
            continue
        if isinstance(t, Block):
            yield from flat((t.released,))
        elif isinstance(t, tuple) and len(t) == 2 and not isinstance(t[1], (tuple, list)) and t[1] is not None:
            yield t
        else:
            yield from flat(t)


class Block:

    def __init__(self, view, arrived):
        self.view, self.arrived, self.released = view, arrived, None


def build(nc, a, out):
    from contextlib import ExitStack
    ctx = ExitStack()
    with ctx:
        sb = lambda name, words, dt=F32: ctx.enter_context(nc.sbuf_tensor("sb_" + name, [P, words], dt))
        sem = lambda name: ctx.enter_context(nc.semaphore(name))
        G = sb("gates", G_WORDS)
        ring = sb("ring", RING_SLOTS * SLOT)
        xres = sb("residual", NT * D)
        h2_T = sb("h2_T", DC * T)
        abuf = sb("abuf", 2048)
        g2row = sb("g2row", D)
        const = sb("const", N_CONST)
        cols = sb("cols", N_COLS)
        stat = sb("stat", 440)
        pick_T = sb("pick_T", 3 * T)
        posi = sb("posi", NT, I32)
        turns = sb("turns", NT * N_FREQ, I32)
        banks = [ctx.enter_context(nc.psum_tensor(f"bank{i}", [P, 512], F32)) for i in range(8)]

        pe, act, dve, pool, sp = (Lane(n, sem(f"{n}_done")) for n in ("pe", "act", "dve", "pool", "sp"))
        slot_sem = [sem(f"slot{i}_arrived") for i in range(RING_SLOTS)]
        s_x, s_const, s_cols, s_pos, s_lam, s_sub, s_out = (
            sem(n) for n in ("x_arrived", "const_arrived", "cols_arrived", "pos_arrived", "lam_arrived",
                             "subln_arrived", "out_stored"))

        def at(name, words, base=None):
            o = OFF[name]
            return G[:, o:o + words]

        slots_used = []

        def load(src, kc, n):
            i = len(slots_used)
            s = i % RING_SLOTS
            flatview = ring[:, s * SLOT:s * SLOT + kc * n]
            view = flatview.rearrange("p (c n) -> p c n", c=kc) if kc > 1 else flatview
            before = slots_used[i - RING_SLOTS] if i >= RING_SLOTS else None
            sp(lambda e: e.dma_start(view, src).then_inc(slot_sem[s], 16), before, signal=0)
            b = Block(view if kc > 1 else flatview.rearrange("p (c n) -> p c n", c=1), (slot_sem[s], 16 * (i // RING_SLOTS + 1)))
            slots_used.append(b)
            return b

        def panel(w, rows, c0, n):
            out_ = []
            for r0 in range(0, rows, 512):
                kc = min(4, (rows - r0) // P)
                out_.append(load(w[r0:r0 + kc * P, c0:c0 + n].rearrange("(c p) n -> p c n", p=P), kc, n))
            return out_

        free = [(b, None) for b in banks]

        def take():
            return free.pop(0)

        def give(b, tick):
            free.append((b, tick))

        n_stat = [0]

        def stat_col(n=1):
            o = n_stat[0]
            n_stat[0] += n
            assert n_stat[0] <= 440
            return stat[:, o:o + n]

        def col(name, c, n=1):
            o, m = COLS[name]
            assert c + n <= m
            return cols[:, o + c:o + c + n]

        ident = const[:, K_IDENT:K_IDENT + P]
        ones = const[:, K_ONES:K_ONES + P]
        iota = const[:, K_IOTA:K_IOTA + P]
        mask = const[:, K_MASK:K_MASK + 2 * P]
        freq = const[:, K_FREQ:K_FREQ + N_FREQ]

        def mm(dst, lhsT, rhs, start, stop, *after, signal=False):
            return pe(lambda e: e.matmul(dst, lhsT, rhs, start=start, stop=stop), *after, signal=signal)

        def turn(dst, src, *after, signal=False):
            n = src.shape[0]
            return pe(lambda e: e.transpose(dst, src, ident[0:n, 0:n]), *after, signal=signal)

        sp(lambda e: e.dma_start(xres[:, :].rearrange("p (t d) -> p t d", t=NT),
                                 a["x"].rearrange("(t p) d -> p t d", p=P)).then_inc(s_x, 16), signal=0)
        x_in = (s_x, 16)
        for dst, src, s in ((const[:, :], a["const"], s_const), (cols[:, :], a["cols"], s_cols), (posi[:, :], a["pos"], s_pos)):
            sp(lambda e, dst=dst, src=src, s=s: e.dma_start(dst, src).then_inc(s, 16), signal=0)
        const_in, cols_in, pos_in = (s_const, 16), (s_cols, 16), (s_pos, 16)
        small = at("small", 384)
        lam_rows = small[:, 0:4 * DIFF_D]
        subln = small[:, 256:256 + DIFF_V]
        sp(lambda e: e.dma_start(lam_rows, a["lam"].partition_broadcast(P)).then_inc(s_lam, 16), signal=0)
        sp(lambda e: e.dma_start(subln, a["subln"].partition_broadcast(P)).then_inc(s_sub, 16), signal=0)
        xr = xres[:, :].rearrange("p (t d) -> p t d", t=NT)

        half = stat_col()
        half_set = pool(lambda e: e.memset(half, -0.5))

        def inverse_rms(total, width, after):
            n = total.shape[1]
            mean, r = stat_col(n), stat_col(n)
            t0 = dve(lambda e: e.tensor_scalar(mean, total, 1.0 / width, EPS, ALU.mult, ALU.add), after)
            hb = half if n == 1 else half.to_broadcast([P, n])
            t1 = pool(lambda e: e.tensor_tensor(r, mean, hb, ALU.pow), t0, half_set)
            return r, t1

        def squares(src, junk, after, lane):
            total = stat_col()
            if lane is act:
                return total, act(lambda e: e.activation(junk, src, ACT.Square, accum_out=total), after)
            return total, dve(lambda e: e.tensor_tensor_reduce(junk, src, src, 1.0, 0.0, ALU.mult, ALU.add, total), after)

        def normed_T(src, dst, gain, shift, after, gain_ready, tmp_free=None):
            xs = abuf[:, :].rearrange("p (t d) -> p t d", t=NT)
            scaled = []
            for t in range(NT):
                lane = (act, dve)[t % 2]
                total, t0 = squares(src[:, t, :], xs[:, t, :], [after, tmp_free], lane)
                r, t1 = inverse_rms(total, D, t0)
                if lane is act:
                    scaled.append(act(lambda e, t=t, r=r: e.activation(xs[:, t, :], src[:, t, :], ACT.Copy, scale=r), t1, t0))
                else:
                    scaled.append(dve(lambda e, t=t, r=r: e.tensor_scalar(xs[:, t, :], src[:, t, :], r, None, ALU.mult), t1, t0))
            done = []
            for c2 in range(DC // 2):
                bank, was = take()
                for j in range(2):
                    for t in range(NT):
                        c = 2 * c2 + j
                        tk = turn(bank[:, j * T + t * P:j * T + (t + 1) * P], xs[:, t, c * P:(c + 1) * P],
                                  was, scaled, const_in, signal=(j == 1 and t == NT - 1))
                ev = []
                for j in range(2):
                    c = 2 * c2 + j
                    srcp, d = bank[:, j * T:(j + 1) * T], dst[:, c, :]
                    g = gain[:, c:c + 1]
                    b = shift[:, c:c + 1] if shift is not None else None
                    if c2 % 2 == 0:
                        if b is None:
                            ev.append(act(lambda e, s=srcp, d=d, g=g: e.activation(d, s, ACT.Copy, scale=g), tk, gain_ready))
                        else:
                            ev.append(act(lambda e, s=srcp, d=d, g=g, b=b: e.activation(d, s, ACT.Identity, bias=b, scale=g), tk, gain_ready))
                    else:
                        if b is None:
                            ev.append(dve(lambda e, s=srcp, d=d, g=g: e.tensor_scalar(d, s, g, None, ALU.mult), tk, gain_ready))
                        else:
                            ev.append(dve(lambda e, s=srcp, d=d, g=g, b=b: e.tensor_scalar(d, s, g, b, ALU.mult, ALU.add), tk, gain_ready))
                give(bank, ev)
                done.append(ev)
            return done

        def chunks(blocks, kc_total):
            for k in range(kc_total):
                b = blocks[k // 4]
                yield k, b.view[:, k % 4, :], b.arrived

        def token_major(x_T, ready, kc, blocks, n, evacuate, free_blocks=True):
            res = []
            for t in range(NT):
                bank, was = take()
                for k, w, arr in chunks(blocks, kc):
                    tk = mm(bank[:, 0:n], x_T[:, k, t * P:(t + 1) * P], w[:, 0:n], k == 0, k == kc - 1,
                            was, ready, arr, signal=(k == kc - 1))
                ev = evacuate(t, bank[:, 0:n], tk)
                give(bank, ev)
                res.append(ev)
            for b in blocks:
                b.released = tk
            return res

        def feature_major(x_T, ready, kc, blocks, n, evacuate):
            res = []
            tiles = n // P
            for m0 in range(0, tiles, 2):
                bank, was = take()
                cnt = min(2, tiles - m0)
                for j in range(cnt):
                    for k, w, arr in chunks(blocks, kc):
                        last = j == cnt - 1 and k == kc - 1
                        tk = mm(bank[:, j * T:(j + 1) * T], w[:, (m0 + j) * P:(m0 + j + 1) * P], x_T[:, k, :],
                                k == 0, k == kc - 1, was, ready, arr, signal=last)
                ev = evacuate(m0, bank[:, 0:cnt * T].rearrange("p (j t) -> p j t", j=cnt), tk)
                give(bank, ev)
                res.append(ev)
            for b in blocks:
                b.released = tk
            return res

        flip = [0]

        def copy(dst, src, *after):
            flip[0] += 1
            if flip[0] % 2:
                return act(lambda e: e.activation(dst, src, ACT.Copy), *after)
            return dve(lambda e: e.tensor_copy(dst, src), *after)

        def turned(src, dst_of, blocks_of_cols, ready, *after):
            ticks = []
            for i0 in range(0, len(blocks_of_cols), 2):
                group = blocks_of_cols[i0:i0 + 2]
                bank, was = take()
                for j, (c0, n) in enumerate(group):
                    for t in range(NT):
                        tk = turn(bank[0:n, j * T + t * P:j * T + (t + 1) * P], src[:, t, c0:c0 + n], was, ready, *after,
                                  signal=(j == len(group) - 1 and t == NT - 1))
                n = group[0][1]
                ev = copy(dst_of(i0, len(group))[0:n], bank[0:n, 0:len(group) * T].rearrange("p (j t) -> p j t", t=T), tk)
                give(bank, ev)
                ticks.append(ev)
            return ticks

        sb_ring = [h2_T[:, i * 512:(i + 1) * 512] for i in range(4)]
        pt_ring = [abuf[:, i * 512:(i + 1) * 512] for i in range(2)]

        def attention(items, ready):
            N = len(items)
            out_ticks = []
            buf_free, pt_free = [ready] * 4, [ready] * 2
            for i in range(N + 3):
                if i < N:
                    it = items[i]
                    pair = [take() for _ in range(it["banks"])]
                    tk = it["scores"]([b for b, _ in pair], [was for _, was in pair] + [ready])
                    buf = sb_ring[i % 4][:, 0:it["n"]]
                    it["buf"] = buf
                    msk = it["masked"]([b for b, _ in pair], buf, [tk, buf_free[i % 4]])
                    for (b, _), m_ in zip(pair, msk):
                        give(b, m_)
                    nmax, tot, inv = stat_ring(i)
                    t1 = dve(lambda e, buf=buf, nmax=nmax: e.tensor_reduce(nmax, buf, AXX, ALU.max, negate=True), msk, stat_free[i % 4])
                    t2 = act(lambda e, buf=buf, nmax=nmax, tot=tot: e.activation(buf, buf, ACT.Exp, bias=nmax, accum_out=tot), t1, msk)
                    it["inv"] = inv
                    it["exp"] = t2
                    it["invt"] = dve(lambda e, inv=inv, tot=tot: e.reciprocal(inv, tot), t2)
                if i >= 2 and i - 2 < N:
                    it = items[i - 2]
                    kc = it["n"] // P
                    bank, was = take()
                    for k in range(kc):
                        tk = turn(bank[:, k * P:(k + 1) * P], it["buf"][:, k * P:(k + 1) * P], was, it["exp"], signal=(k == kc - 1))
                    buf_free[(i - 2) % 4] = tk
                    pt = pt_ring[i % 2][:, 0:it["n"]]
                    it["pt"] = pt
                    it["ptt"] = copy(pt, bank[:, 0:it["n"]], tk, pt_free[i % 2])
                    give(bank, it["ptt"])
                if i >= 3:
                    it = items[i - 3]
                    bank, was = take()
                    kc = it["n"] // P
                    for k in range(kc):
                        tk = mm(bank[:, 0:it["dv"]], it["pt"][:, k * P:(k + 1) * P], it["values"][k], k == 0, k == kc - 1,
                                was, it["ptt"], it.get("values_ready"), signal=(k == kc - 1))
                    pt_free[(i - 3) % 2] = tk
                    ev = it["finish"](bank[:, 0:it["dv"]], it["inv"], [tk, it["invt"]])
                    stat_free[(i - 3) % 4] = ev
                    give(bank, ev)
                    out_ticks.append(ev)
            return out_ticks

        att_stats = stat_col(12)
        stat_free = [None] * 4

        def stat_ring(i):
            o = 3 * (i % 4)
            return att_stats[:, o:o + 1], att_stats[:, o + 1:o + 2], att_stats[:, o + 2:o + 3]

        posf = stat_col(NT)
        t_pos = dve(lambda e: e.tensor_copy(posf, posi[:, :]), pos_in)
        nf = NT * N_FREQ
        rope_w = at("rope", 6 * nf)
        ang, red, tmp, sin_t, cos_t, nturn = (rope_w[:, i * nf:(i + 1) * nf] for i in range(6))
        tk = None
        for t in range(NT):
            tk = dve(lambda e, t=t: e.tensor_scalar(ang[:, t * N_FREQ:(t + 1) * N_FREQ], freq, posf[:, t:t + 1], None, ALU.mult),
                     t_pos, const_in)
        TWO_PI = 2 * math.pi
        c1 = 6.28125
        c2 = float(np.float32(np.round((TWO_PI - c1) * 2**21) / 2**21))
        c3 = TWO_PI - c1 - c2
        tk = dve(lambda e: e.tensor_scalar(turns[:, :], ang, 1.0 / TWO_PI, None, ALU.mult), tk)
        tk = dve(lambda e: e.tensor_copy(nturn, turns[:, :]), tk)
        tk = dve(lambda e: e.scalar_tensor_tensor(red, nturn, -c1, ang, ALU.mult, ALU.add), tk)
        for c in (c2, c3):
            tk = dve(lambda e, c=c: e.scalar_tensor_tensor(red, nturn, -c, red, ALU.mult, ALU.add), tk)

        def wrap(v, tk):
            tk = dve(lambda e: e.tensor_scalar(tmp, v, math.pi, -TWO_PI, ALU.is_gt, ALU.mult), tk)
            tk = dve(lambda e: e.tensor_tensor(v, v, tmp, ALU.add), tk)
            tk = dve(lambda e: e.tensor_scalar(tmp, v, -math.pi, TWO_PI, ALU.is_lt, ALU.mult), tk)
            tk = dve(lambda e: e.tensor_tensor(v, v, tmp, ALU.add), tk)
            return dve(lambda e: e.tensor_scalar(v, v, 3.1415925, -3.1415925, ALU.min, ALU.max), tk)

        tk = wrap(red, tk)
        t_sin = act(lambda e: e.activation(sin_t, red, ACT.Sin), tk)
        tk = dve(lambda e: e.tensor_scalar(ang, red, math.pi / 2, None, ALU.add), tk)
        tk = wrap(ang, tk)
        rope_ready = [act(lambda e: e.activation(cos_t, ang, ACT.Sin), tk), t_sin]

        def rope(v, c0, heads, stride, half_n, f0, after):
            ticks = []
            for t in range(NT):
                w = v[:, t, 0:heads * stride].rearrange("p (h s) -> p h s", s=stride)
                x1, x2 = w[:, :, c0:c0 + half_n], w[:, :, c0 + half_n:c0 + 2 * half_n]
                co = cos_t[:, t * N_FREQ + f0:t * N_FREQ + f0 + half_n].unsqueeze(1).to_broadcast([P, heads, half_n])
                si = sin_t[:, t * N_FREQ + f0:t * N_FREQ + f0 + half_n].unsqueeze(1).to_broadcast([P, heads, half_n])
                n = heads * half_n
                tm = [rope_tmp[:, i * 128:i * 128 + n].rearrange("p (h s) -> p h s", s=half_n) for i in range(4)]
                tt = lambda o, x, y, op, *af: pool(lambda e: e.tensor_tensor(o, x, y, op), *af)
                a0 = tt(tm[0], x1, co, ALU.mult, after, rope_ready, rope_last[0])
                tt(tm[1], x2, si, ALU.mult)
                tt(tm[2], x2, co, ALU.mult)
                a1 = tt(tm[3], x1, si, ALU.mult)
                tt(x1, tm[0], tm[1], ALU.subtract, a1)
                rope_last[0] = tt(x2, tm[2], tm[3], ALU.add, a1)
                ticks.append(rope_last[0])
            return ticks

        rope_tmp = at("rope_tmp", 512)
        rope_last = [None]

        lam_s, lam_e, lam_neg = stat_col(2), stat_col(2), stat_col()
        lam_junk = stat_col(DIFF_D)
        for i in range(2):
            tk = dve(lambda e, i=i: e.tensor_tensor_reduce(lam_junk, lam_rows[:, 2 * i * DIFF_D:(2 * i + 1) * DIFF_D],
                                                           lam_rows[:, (2 * i + 1) * DIFF_D:(2 * i + 2) * DIFF_D],
                                                           1.0, 0.0, ALU.mult, ALU.add, lam_s[:, i:i + 1]), (s_lam, 16), tk)
        tk = act(lambda e: e.activation(lam_e, lam_s, ACT.Exp), tk)
        tk = dve(lambda e: e.tensor_scalar(lam_neg, lam_e[:, 1:2], -LAMBDA_INIT, None, ALU.add), tk)
        lam_ready = dve(lambda e: e.tensor_tensor(lam_neg, lam_neg, lam_e[:, 0:1], ALU.subtract), tk)

        cs = stat_col(2 * DC)
        t_cs = act(lambda e: e.activation(cs, cols[:, COLS["c"][0]:COLS["c"][0] + 2 * DC], ACT.Silu), cols_in)

        act_T = at("act_T", 2048).rearrange("p (c t) -> p c t", c=DC)
        xn = normed_T(xr, act_T, col("norm_mix_g", 0, 8), None, x_in, cols_in)

        lat = at("lat", NT * LAT).rearrange("p (t d) -> p t d", t=NT)
        parts = []
        for c0, n in ((0, 512), (512, LAT - 512)):
            blk = panel(a["w_in"], D, c0, n)
            parts.append(token_major(act_T, xn, DC, blk, n, lambda t, p, tk, c0=c0, n=n: copy(lat[:, t, c0:c0 + n], p, tk)))
        lat_ready = [parts[0], parts[1]]
        kpe = lat[:, :, Q_RANK + KV_RANK:LAT]
        t_kpe = rope(kpe, 0, 1, ROPE, HALF_M, 0, lat_ready)

        lat_T = at("lat_T", 5 * T).rearrange("p (c t) -> p c t", t=T)
        lat_scaled = []
        junk = at("km", 1536)
        for t in range(NT):
            for j, (c0, n) in enumerate(((0, Q_RANK), (Q_RANK, KV_RANK))):
                total, t0 = squares(lat[:, t, c0:c0 + n], junk[:, (2 * t + j) * 384:(2 * t + j) * 384 + n], lat_ready, (act, dve)[j])
                r, t1 = inverse_rms(total, n, t0)
                lat_scaled.append(dve(lambda e, t=t, c0=c0, n=n, r=r: e.tensor_scalar(lat[:, t, c0:c0 + n], lat[:, t, c0:c0 + n], r, None, ALU.mult), t1, t0))
        lat_T_ready = []
        g0 = COLS["q_norm_g"][0]
        for c in range(5):
            bank, was = take()
            for t in range(NT):
                tk = turn(bank[:, t * P:(t + 1) * P], lat[:, t, c * P:(c + 1) * P], was, lat_scaled, signal=(t == NT - 1))
            ev = dve(lambda e, c=c, bank=bank: e.tensor_scalar(lat_T[:, c, :], bank[:, 0:T], cols[:, g0 + c:g0 + c + 1], None, ALU.mult), tk)
            give(bank, ev)
            lat_T_ready.append(ev)

        def token_buf(name, width):
            return at(name, NT * width).rearrange("p (t d) -> p t d", t=NT)

        dq, dk, dv = (token_buf(n, 512) for n in ("dq", "dk", "dv"))
        got = []
        for j, dst in enumerate((dq, dk, dv)):
            blk = panel(a["w_in"], D, LAT + 512 * j, 512)
            got.append(token_major(act_T, xn, DC, blk, 512, lambda t, p, tk, dst=dst: copy(dst[:, t, :], p, tk)))
        t_dq = rope(dq, 0, 8, DIFF_D, HALF_D, HALF_M, got[0])
        t_dk = rope(dk, 0, 8, DIFF_D, HALF_D, HALF_M, got[1])
        dv_ready = got[2]

        qm, kv, km = token_buf("qm", 768), token_buf("kv", 1024), token_buf("km", 768)
        q_up = []
        for c0, n in ((0, 512), (512, 256)):
            blk = panel(a["w_uq"], Q_RANK, c0, n)
            q_up.append(token_major(lat_T[:, 0:3, :], lat_T_ready, 3, blk, n, lambda t, p, tk, c0=c0, n=n: copy(qm[:, t, c0:c0 + n], p, tk)))
        t_qm = rope(qm, NOPE, MLA_H, MLA_QK, HALF_M, 0, q_up)
        kv_blk = load(a["w_ukv"].rearrange("(c p) n -> p c n", p=P), 2, 1024)
        kv_up = []
        for c0 in (0, 512):
            half_blk = Block(kv_blk.view[:, :, c0:c0 + 512], kv_blk.arrived)
            kv_up.append(token_major(lat_T[:, 3:5, :], lat_T_ready, 2, [half_blk], 512, lambda t, p, tk, c0=c0: copy(kv[:, t, c0:c0 + 512], p, tk)))
            kv_blk.released = half_blk.released
        km_ready = []
        for t in range(NT):
            kv_h = kv[:, t, :].rearrange("p (h s) -> p h s", s=2 * NOPE)
            km_h = km[:, t, :].rearrange("p (h s) -> p h s", s=MLA_QK)
            km_ready.append(dve(lambda e, o=km_h, i=kv_h: e.tensor_copy(o[:, :, 0:NOPE], i[:, :, 0:NOPE]), kv_up, lat_scaled))
            km_ready.append(pool(lambda e, o=km_h, t=t: e.tensor_copy(o[:, :, NOPE:MLA_QK], kpe[:, t, :].unsqueeze(1).to_broadcast([P, MLA_H, ROPE])), t_kpe, lat_scaled))

        qm_T = at("qm_T", 2048).rearrange("p (h t) -> p h t", t=T)
        km_T = at("km_T", 2048).rearrange("p (h t) -> p h t", t=T)
        dq_T = at("dq_T", 1024).rearrange("p (h t) -> p h t", t=T)
        dk_T = at("dk_T", 1024).rearrange("p (h t) -> p h t", t=T)
        att_ready = []
        for src, dst, blocks_, rdy in ((qm, qm_T, [(h * MLA_QK, MLA_QK) for h in range(MLA_H)], t_qm),
                                       (km, km_T, [(h * MLA_QK, MLA_QK) for h in range(MLA_H)], km_ready),
                                       (dq, dq_T, [(h * P, P) for h in range(DIFF_H)], t_dq),
                                       (dk, dk_T, [(h * P, P) for h in range(DIFF_H)], t_dk)):
            att_ready.append(turned(src, lambda i, n, dst=dst: dst[:, i:i + n, :], blocks_, rdy))

        gates_T = at("gates_T", 4096).rearrange("p (c t) -> p c t", t=T)
        gates_ready = []
        for j in range(4):
            blk = panel(a["w_in"], D, LAT + 1536 + 512 * j, 512)

            def ev_gate(m0, p, tk, j=j):
                last = None
                for m in range(p.shape[1]):
                    c = 4 * j + m0 + m
                    last = act(lambda e, c=c, p=p, m=m: e.activation(gates_T[:, c, :], p[:, m, :], ACT.Sigmoid, bias=col("b_gate", c)), tk, cols_in)
                return last
            gates_ready.append(feature_major(act_T, xn, DC, blk, 512, ev_gate))

        o_mla, o_diff = token_buf("o_mla", 512), token_buf("o_diff", 512)
        items = []

        def causal_item(qT, kT, lo, hi, qb, scale, values, dv_n, finish, vready):
            n = (qb + 1) * P
            m = mask[:, 2 * P - n:2 * P]

            def scores(bank, after):
                return mm(bank[0][:, 0:n], qT[lo:hi, qb * P:(qb + 1) * P], kT[lo:hi, 0:n], True, True, after, att_ready, signal=True)

            def masked(bank, buf, after):
                return [dve(lambda e: e.scalar_tensor_tensor(buf, bank[0][:, 0:n], scale, m, ALU.mult, ALU.add), after)]
            return dict(n=n, banks=1, scores=scores, masked=masked, values=values, dv=dv_n, finish=finish, values_ready=vready)

        for h in range(MLA_H):
            for qb in range(NT):
                vals = [kv[:, k, h * 128 + NOPE:h * 128 + 128] for k in range(qb + 1)]

                def fin(p, inv, after, h=h, qb=qb):
                    return act(lambda e: e.activation(o_mla[:, qb, h * 64:(h + 1) * 64], p, ACT.Copy, scale=inv), after)
                items.append(causal_item(qm_T[:, h, :], km_T[:, h, :], 0, MLA_QK, qb, MLA_QK ** -0.5, vals, MLA_V, fin, None))
        o1buf = [small_o1 for small_o1 in (rope_tmp[:, 0:128], rope_tmp[:, 128:256])]
        diff_ticks = {}
        for h in range(DIFF_H):
            for qb in range(NT):
                for comp in range(2):
                    vals = [dv[:, k, h * P:(h + 1) * P] for k in range(qb + 1)]
                    ob = o1buf[(h * NT + qb) % 2]

                    def fin(p, inv, after, h=h, qb=qb, comp=comp, ob=ob):
                        dst = o_diff[:, qb, h * P:(h + 1) * P]
                        if comp == 0:
                            tk = act(lambda e: e.activation(dst, p, ACT.Copy, scale=inv), after)
                            diff_ticks[h, qb] = tk
                            return tk
                        t0 = act(lambda e: e.activation(ob, p, ACT.Copy, scale=inv), after, diff_ticks.get(("free", id(ob))), t_qm, t_dk)
                        t1 = dve(lambda e: e.scalar_tensor_tensor(dst, ob, lam_neg, dst, ALU.mult, ALU.add), t0, lam_ready, diff_ticks[h, qb])
                        diff_ticks["free", id(ob)] = t1
                        diff_ticks[h, qb] = t1
                        return [t0, t1]
                    items.append(causal_item(dq_T[:, h, :], dk_T[:, h, :], comp * 64, comp * 64 + 64, qb, DIFF_D ** -0.5,
                                             vals, DIFF_V, fin, dv_ready))
        att_done = attention(items, [xn])

        tot = stat_col(NT * DIFF_H)
        tks = []
        for t in range(NT):
            for h in range(DIFF_H):
                i = t * DIFF_H + h
                v = o_diff[:, t, h * P:(h + 1) * P]
                tks.append(dve(lambda e, v=v, i=i: e.tensor_tensor_reduce(rope_tmp[:, 256:384], v, v, 1.0, 0.0, ALU.mult, ALU.add, tot[:, i:i + 1]),
                               att_done, tks[-1:] if tks else None))
        r, t1 = inverse_rms(tot, DIFF_V, tks)
        t_r = dve(lambda e: e.tensor_scalar(r, r, 1.0 - LAMBDA_INIT, None, ALU.mult), t1)
        odn = []
        for t in range(NT):
            for h in range(DIFF_H):
                i = t * DIFF_H + h
                v = o_diff[:, t, h * P:(h + 1) * P]
                odn.append(dve(lambda e, v=v, i=i: e.scalar_tensor_tensor(v, v, r[:, i:i + 1], subln, ALU.mult, ALU.mult), t_r, (s_sub, 16)))

        oa_T = at("oa_T", 1024).rearrange("p (c t) -> p c t", t=T)
        ob_T = at("ob_T", 1024).rearrange("p (c t) -> p c t", t=T)
        blocks4 = [(c * P, P) for c in range(4)]
        oa_ready = turned(o_mla, lambda i, n: oa_T[:, i:i + n, :], blocks4, att_done)
        ob_ready = turned(o_diff, lambda i, n: ob_T[:, i:i + n, :], blocks4, odn)

        merged_T = at("merged_T", 2048).rearrange("p (c t) -> p c t", t=T)
        merged_ready = []
        for j in range(2):
            blk = panel(a["w_b_mla"], 512, 512 * j, 512)

            def ev_a(m0, p, tk, j=j):
                c = 4 * j + m0
                return dve(lambda e: e.tensor_tensor(merged_T[:, c:c + 2, :], p, gates_T[:, c:c + 2, :], ALU.mult), tk, gates_ready)
            merged_a = feature_major(oa_T, oa_ready, 4, blk, 512, ev_a)
            blk = panel(a["w_b_diff"], 512, 512 * j, 512)

            def ev_b(m0, p, tk, j=j):
                c = 4 * j + m0
                g = gates_T[:, 8 + c:10 + c, :]
                t0 = dve(lambda e: e.tensor_tensor(g, p, g, ALU.mult), tk, gates_ready)
                t1 = dve(lambda e: e.tensor_tensor(merged_T[:, c:c + 2, :], merged_T[:, c:c + 2, :], g, ALU.add), t0, merged_a)
                merged_ready.append(t1)
                return t0
            feature_major(ob_T, ob_ready, 4, blk, 512, ev_b)

        def add_to_residual(c0):
            def ev(t, p, tk):
                v = xr[:, t, c0:c0 + 512]
                return dve(lambda e: e.tensor_tensor(v, p, v, ALU.add), tk, xn)
            return ev

        x2 = []
        for j in range(2):
            blk = panel(a["w_out"], D, 512 * j, 512)
            x2.append(token_major(merged_T, merged_ready, DC, blk, 512, add_to_residual(512 * j)))

        hn = normed_T(xr, act_T, col("norm_ffn_g", 0, 8), None, x2, cols_in, tmp_free=att_done)
        hid_T = at("hid_T", 22 * T).rearrange("p (c t) -> p c t", t=T)
        ada = {"x": at("ada_x", 6 * D), "c": at("ada_c", 2 * D)}
        ada_tick = {}

        def ada_block(i):
            cb, rb = i // 2, i % 2
            blk = load(a["ada_w"][rb * 512:(rb + 1) * 512, cb * 512:(cb + 1) * 512].rearrange("(c p) n -> p c n", p=P), 4, 512)
            last = []
            for k in range(4):
                for who, base in (("x", 0), ("c", DC)):
                    if who == "c" and cb >= 4:
                        continue
                    acc = ada[who][:, cb * 512:(cb + 1) * 512]
                    s = cs[:, base + rb * 4 + k:base + rb * 4 + k + 1]
                    w = blk.view[:, k, :]
                    if rb == 0 and k == 0:
                        tk = dve(lambda e, acc=acc, w=w, s=s: e.tensor_scalar(acc, w, s, None, ALU.mult), blk.arrived, t_cs, att_done, x2)
                    else:
                        tk = dve(lambda e, acc=acc, w=w, s=s: e.scalar_tensor_tensor(acc, w, s, acc, ALU.mult, ALU.add),
                                 blk.arrived, ada_tick[who, cb])
                    ada_tick[who, cb] = tk
            blk.released = tk

        acc_banks = [take() for _ in range(4)]
        n_ada = 0
        groups = [(f0, min(512, FFN - f0)) for f0 in range(0, FFN, 512)]
        hid_prev = None

        def down(f0, n, ready):
            kc = n // P
            for half_ in range(2):
                blk = load(a["w_down"][f0:f0 + n, half_ * 512:(half_ + 1) * 512].rearrange("(c p) n -> p c n", p=P), kc, 512)
                for t in range(NT):
                    bank, was = acc_banks[2 * half_ + t]
                    for k in range(kc):
                        first, last = f0 == 0 and k == 0, f0 + n == FFN and k == kc - 1
                        tk = mm(bank[:, :], hid_T[:, f0 // P + k, t * P:(t + 1) * P], blk.view[:, k, :], first, last,
                                was, ready, blk.arrived, signal=(k == kc - 1))
                blk.released = tk
            return tk

        for gi, (f0, n) in enumerate(groups):
            ready = []
            for which in ("w_gate", "w_up"):
                blk = panel(a[which], D, f0, n)

                def ev(m0, p, tk, which=which, f0=f0):
                    c = f0 // P + m0
                    dst = hid_T[:, c:c + p.shape[1], :]
                    if which == "w_gate":
                        t0 = act(lambda e: e.activation(dst, p, ACT.Silu), tk, att_done)
                        hid_gate.append(t0)
                        return t0
                    t0 = dve(lambda e: e.tensor_tensor(dst, p, dst, ALU.mult), tk, hid_gate)
                    ready.append(t0)
                    return t0
                if which == "w_gate":
                    hid_gate = []
                feature_major(act_T, hn, DC, blk, n, ev)
            if hid_prev is not None:
                down(*hid_prev)
            hid_prev = (f0, n, ready)
            for _ in range(4):
                if n_ada < 24:
                    ada_block(n_ada)
                    n_ada += 1
        down_tick = down(*hid_prev)
        x3 = []
        for half_ in range(2):
            for t in range(NT):
                bank, _ = acc_banks[2 * half_ + t]
                v = xr[:, t, half_ * 512:(half_ + 1) * 512]
                tk = dve(lambda e, v=v, bank=bank: e.tensor_tensor(v, bank[:, :], v, ALU.add), down_tick, hn)
                give(bank, tk)
                x3.append(tk)

        def row_block(src):
            return load(src.partition_broadcast(P), 1, D)

        def final_norm(src_ready, gain_blk):
            ticks = []
            xs = abuf[:, :].rearrange("p (t d) -> p t d", t=NT)
            for t in range(NT):
                total, t0 = squares(xr[:, t, :], xs[:, t, :], src_ready, (act, dve)[t % 2])
                r, t1 = inverse_rms(total, D, t0)
                ticks.append(dve(lambda e, t=t, r=r: e.scalar_tensor_tensor(xr[:, t, :], xr[:, t, :], r, gain_blk.view[:, 0, :], ALU.mult, ALU.mult),
                                 t1, t0, gain_blk.arrived))
            gain_blk.released = ticks[-1]
            return ticks

        x4 = final_norm([x3, hn], row_block(a["norm_final_g"]))

        mod = sb("mod", 7 * DC)
        mcol = {n: mod[:, i * DC:(i + 1) * DC] for i, n in enumerate(("sh1", "sc1", "csh1", "csc1", "sh2", "sc2", "tmp"))}
        mod_ready = {}
        for name, who, part in (("csh1", "c", 0), ("csc1", "c", 1), ("sh1", "x", 0), ("sc1", "x", 1), ("sh2", "x", 3), ("sc2", "x", 4)):
            tks = []
            for half_ in range(2):
                bank, was = take()
                for j in range(4):
                    o = part * D + (half_ * 4 + j) * P
                    tk = turn(bank[:, j * P:(j + 1) * P], ada[who][:, o:o + P], was, list(ada_tick.values()), signal=(j == 3))
                ev = dve(lambda e, bank=bank, name=name, half_=half_: e.tensor_reduce(
                    mcol[name][:, half_ * 4:half_ * 4 + 4], bank[:, :].rearrange("p (j t) -> p j t", j=4), AXX, ALU.add), tk)
                give(bank, ev)
                tks.append(ev)
            bias = col("ada_b", part * DC, DC)
            tk = dve(lambda e, name=name, bias=bias: e.tensor_tensor(mcol[name], mcol[name], bias, ALU.add), tks)
            if "sc" in name:
                gain = col("norm2_g" if name == "sc2" else "norm1_g", 0, DC)
                tk = dve(lambda e, name=name, gain=gain: e.scalar_tensor_tensor(mcol[name], mcol[name], 1.0, gain, ALU.add, ALU.mult), tk)
            mod_ready[name] = tk
        g1row = at("g1row", D)
        grow_ready = {}
        for part, dst, src in ((2, g1row, a["ada_b_g1"]), (5, g2row[:, :], a["ada_b_g2"])):
            bias = row_block(src)
            tks = []
            for half_ in range(2):
                bank, was = take()
                tk = mm(bank[:, :], ones, ada["x"][:, part * D + half_ * 512:part * D + (half_ + 1) * 512], True, True, was,
                        list(ada_tick.values()), signal=True)
                ev = dve(lambda e, bank=bank, dst=dst, bias=bias, half_=half_: e.tensor_tensor(
                    dst[:, half_ * 512:(half_ + 1) * 512], bank[:, :], bias.view[:, 0, half_ * 512:(half_ + 1) * 512], ALU.add),
                    tk, bias.arrived, list(mod_ready.values()))
                give(bank, ev)
                tks.append(ev)
            bias.released = tks[-1]
            grow_ready[part] = tks

        ctx_T = at("ctx_T", 2048).rearrange("p (c t) -> p c t", c=DC)
        ctx_blk = load(a["ctx"].rearrange("(t p) d -> p t d", p=P), 2, D)
        hc = normed_T(ctx_blk.view, ctx_T, mcol["csc1"], mcol["csh1"], ctx_blk.arrived,
                      [mod_ready["csc1"], mod_ready["csh1"]], tmp_free=x4)
        ctx_blk.released = hc
        hx = normed_T(xr, act_T, mcol["sc1"], mcol["sh1"], x4, [mod_ready["sc1"], mod_ready["sh1"]], tmp_free=hc)

        zx, zc = token_buf("zx", 2048), token_buf("zc", 1024)
        zx_ready, zc_ready = [], []
        for j in (1, 2, 3, 0):
            blk = panel(a["w_in2"], D, 512 * j, 512)
            if j >= 2:
                o = 512 * (j - 2)
                zc_ready.append(token_major(ctx_T, hc, DC, blk, 512, lambda t, p, tk, o=o: copy(zc[:, t, o:o + 512], p, tk, down_tick)))
            zx_ready.append(token_major(act_T, hx, DC, blk, 512, lambda t, p, tk, j=j: copy(zx[:, t, 512 * j:512 * j + 512], p, tk, down_tick)))

        q_T, k_T, kc_T, mix_T = (at(n, w).rearrange("p (c t) -> p c t", t=T) for n, w in
                                 (("q_T", 1024), ("k_T", 1024), ("kc_T", 1024), ("mix_T", 2048)))
        na_ready = []
        clear = [list(grow_ready.values()), down_tick]
        for src, c0, dst, rdy in ((zx, 512, q_T, zx_ready[0]), (zx, 1024, k_T, zx_ready[1]), (zc, 0, kc_T, zc_ready[0])):
            na_ready.append(turned(src, lambda i, n, dst=dst: dst[:, i:i + n, :], [(c0 + c * P, P) for c in range(4)], rdy, clear))

        bias_blk = [load(a["na_bias"][:, i * SLOT:(i + 1) * SLOT], 1, SLOT) for i in range(2)]
        attn = token_buf("attn", 512)
        items = []
        scale = NA_D ** -0.5
        for h in range(NA_H):
            for qb in range(NT):
                lo = (h % 2) * 64
                hb = bias_blk[h // 4]
                bview = hb.view[:, 0, ((h % 4) * NT + qb) * T:((h % 4) * NT + qb + 1) * T]

                def scores(bank, after, h=h, qb=qb, lo=lo):
                    q = q_T[lo:lo + 64, h // 2, qb * P:(qb + 1) * P]
                    mm(bank[0][:, 0:T], q, k_T[lo:lo + 64, h // 2, :], True, True, after, na_ready)
                    return mm(bank[1][:, 0:T], q, kc_T[lo:lo + 64, h // 2, :], True, True, signal=True)

                def masked(bank, buf, after, bview=bview, hb=hb):
                    t0 = dve(lambda e: e.scalar_tensor_tensor(buf[:, 0:T], bank[0][:, 0:T], scale, bview, ALU.mult, ALU.add), after, hb.arrived)
                    hb.released = t0
                    return [t0, act(lambda e: e.activation(buf[:, T:2 * T], bank[1][:, 0:T], ACT.Copy, scale=scale), after)]

                def fin(p, inv, after, h=h, qb=qb):
                    return act(lambda e: e.activation(attn[:, qb, h * 64:(h + 1) * 64], p, ACT.Copy, scale=inv), after)
                vals = [zx[:, k, 1536 + h * 64:1536 + (h + 1) * 64] for k in range(NT)] + [zc[:, k, 512 + h * 64:512 + (h + 1) * 64] for k in range(NT)]
                items.append(dict(n=2 * T, banks=2, scores=scores, masked=masked, values=vals, dv=NA_D, finish=fin, values_ready=[zx_ready[2], zc_ready[1]]))
        attn_done = attention(items, [hx])
        mix_ready = [turned(attn, lambda i, n: mix_T[:, 4 + i:4 + i + n, :], blocks4, attn_done)]

        band_blk = load(a["band"], 1, SLOT)
        pw_blk = load(a["pool_w"], 1, 512)
        band = band_blk.view[:, 0, :].rearrange("p (k g t) -> p k g t", k=NT, g=4)
        pooled_T = at("pooled_T", 1024).rearrange("p (c t) -> p c t", t=T)
        for g in range(4):
            bank, was = take()
            for k in range(NT):
                tk = mm(bank[:, 0:T], zx[:, k, g * P:(g + 1) * P], band[:, k, g, :], k == 0, k == NT - 1,
                        was, zx_ready[3], band_blk.arrived, signal=(k == NT - 1))
            band_blk.released = tk
            ev = copy(pooled_T[:, g, :], bank[:, 0:T], tk, list(grow_ready.values()))
            give(bank, ev)
            bank, was = take()
            tk = mm(bank[:, 0:T], pw_blk.view[:, 0, g * P:(g + 1) * P], pooled_T[:, g, :], True, True, was, ev, pw_blk.arrived, signal=True)
            pw_blk.released = tk
            ev = act(lambda e, g=g, bank=bank: e.activation(mix_T[:, g, :], bank[:, 0:T], ACT.Copy, scale=col("pool_scale", g)), tk, list(grow_ready.values()))
            give(bank, ev)
            mix_ready.append(ev)

        x5 = []
        for j in range(2):
            blk = panel(a["w_out2"], D, 512 * j, 512)

            def ev(t, p, tk, j=j):
                c0 = 512 * j
                tmp_ = h2_T[:, t * 512:(t + 1) * 512]
                t0 = dve(lambda e: e.tensor_tensor(tmp_, p, g1row[:, c0:c0 + 512], ALU.mult), tk, grow_ready[2], attn_done, x5)
                v = xr[:, t, c0:c0 + 512]
                x5.append(pool(lambda e: e.tensor_tensor(v, tmp_, v, ALU.add), t0, hx))
                return t0
            token_major(mix_T, mix_ready, DC, blk, 512, ev)

        h2v = h2_T[:, :].rearrange("p (c t) -> p c t", c=DC)
        h2 = normed_T(xr, h2v, mcol["sc2"], mcol["sh2"], x5, [mod_ready["sc2"], mod_ready["sh2"], attn_done], tmp_free=attn_done)

        pq_T = at("pq_T", 4096).rearrange("p (c t) -> p c t", t=T)
        pq_ready = []
        for j in range(4):
            blk = panel(a["peer_wq"], D, 512 * j, 512)

            def ev(m0, p, tk, j=j):
                tk = copy(pq_T[:, 4 * j + m0:4 * j + m0 + 2, :], p, tk, attn_done)
                pq_ready.append(tk)
                return tk
            feature_major(h2v, h2, DC, blk, 512, ev)

        keys = load(a["keys_T"], 1, 2048)
        s_all = at("s", 4096).rearrange("p (t g n) -> p t g n", t=NT, g=16)
        s_ready = [[], []]
        for t in range(NT):
            for g4 in range(4):
                bank, was = take()
                for j in range(4):
                    g = 4 * g4 + j
                    tk = mm(bank[:, j * P:(j + 1) * P], pq_T[:, g, t * P:(t + 1) * P], keys.view[:, 0, g * P:(g + 1) * P], True, True,
                            was, pq_ready, keys.arrived, signal=(j == 3))
                ev = act(lambda e, t=t, g4=g4, bank=bank: e.activation(s_all[:, t, 4 * g4:4 * g4 + 4, :],
                                                                        bank[:, :].rearrange("p (j n) -> p j n", j=4), ACT.Copy), tk, x5)
                give(bank, ev)
                s_ready[t].append(ev)
        keys.released = tk

        s_work = at("s_work", 2048).rearrange("p (g n) -> p g n", g=16)
        v12 = at("v12", 256).rearrange("p (g k) -> p g k", g=16)
        i12 = at("i12", 256).bitcast(U32).rearrange("p (g k) -> p g k", g=16)
        i12f = at("i12f", 256).rearrange("p (h w k) -> p h w k", h=PE_H, w=2)
        cand = at("cand", 2048).rearrange("p (h k) -> p h k", h=PE_H)
        cand_work = at("cand_work", 2048).rearrange("p (h k) -> p h k", h=PE_H)
        eq = at("eq", 2048).rearrange("p (h k a) -> p h k a", h=PE_H, a=TOPK)
        tv = at("tv", 3 * 128)
        topv = tv[:, 0:128].rearrange("p (h k) -> p h k", h=PE_H)
        topi = at("topi", 128).bitcast(U32)
        ab = at("ab", 2 * 128).bitcast(U32)
        gs = stat_col(2 * PE_H)
        best = stat_col(PE_H)

        def top16(values, work, vals, idx, after):
            n = values.shape[1]
            t0 = [dve(lambda e, g=g: e.max(vals[:, g, 0:8], values[:, g, :]), after) for g in range(n)][-1]
            dve_ = lambda f, *af: dve(f, *af)
            for g in range(n):
                t1 = dve_(lambda e, g=g: e.match_replace(work[:, g, :], vals[:, g, 0:8], values[:, g, :], LOWEST), t0)
            for g in range(n):
                dve_(lambda e, g=g: e.max_index(idx[:, g, 0:8], vals[:, g, 0:8], values[:, g, :]), t0)
            for g in range(n):
                t2 = dve_(lambda e, g=g: e.max(vals[:, g, 8:16], work[:, g, :]), t1)
            for g in range(n):
                t3 = dve_(lambda e, g=g: e.max_index(idx[:, g, 8:16], vals[:, g, 8:16], work[:, g, :]), t2)
            return t3

        picks_ready = []
        last = None
        iota16 = iota[:, 0:TOPK]
        for t in range(NT):
            t0 = top16(s_all[:, t], s_work, v12, i12, [s_ready[t], last, x5])
            t1 = dve(lambda e: e.tensor_copy(i12f, at("i12", 256).bitcast(U32).rearrange("p (h w k) -> p h w k", h=PE_H, w=2)), t0)
            v4 = at("v12", 256).rearrange("p (h w k) -> p h w k", h=PE_H, w=2)
            tks = []
            for h in range(PE_H):
                tks.append(dve(lambda e, h=h: e.tensor_tensor(cand[:, h, :].rearrange("p (a b) -> p a b", a=TOPK),
                                                              v4[:, h, 0, :].unsqueeze(2).to_broadcast([P, TOPK, TOPK]),
                                                              v4[:, h, 1, :].unsqueeze(1).to_broadcast([P, TOPK, TOPK]), ALU.add), t0))
            topi_v = topi[:, :].rearrange("p (h k) -> p h k", h=PE_H)
            t2 = top16(cand, cand_work, topv, topi_v, tks[-1])
            t3 = dve(lambda e: e.tensor_scalar(ab[:, 0:128], topi[:, :], 4, None, ALU.logical_shift_right), t2)
            t3 = dve(lambda e: e.tensor_scalar(ab[:, 128:256], topi[:, :], 15, None, ALU.bitwise_and), t2)
            abf = tv[:, 128:384]
            t4 = dve(lambda e: e.tensor_copy(abf, ab[:, :]), t3, t1)
            pick = abuf[:, 0:384].rearrange("p (w n) -> p w n", w=3)
            for w in range(2):
                av = abf[:, w * 128:(w + 1) * 128].rearrange("p (h k) -> p h k", h=PE_H)
                e0 = dve(lambda e, av=av: e.tensor_tensor(eq.rearrange("p h k a -> p (h k) a"), av.rearrange("p h k -> p (h k)").unsqueeze(2).to_broadcast([P, 128, TOPK]),
                                                          iota16.unsqueeze(1).to_broadcast([P, 128, TOPK]), ALU.is_equal), t4, h2, last)
                e1 = dve(lambda e, w=w: e.tensor_tensor(eq, eq, i12f[:, :, w, :].unsqueeze(2).to_broadcast([P, PE_H, TOPK, TOPK]), ALU.mult), e0)
                t4 = dve(lambda e, w=w: e.tensor_reduce(pick[:, w, :], eq.rearrange("p h k a -> p (h k) a"), AXX, ALU.add), e1)
            mx = best
            u0 = dve(lambda e: e.tensor_copy(mx, topv[:, :, 0]), t2, last)
            u1 = dve(lambda e: e.tensor_tensor(topv, topv, mx.unsqueeze(2).to_broadcast([P, PE_H, TOPK]), ALU.subtract), u0)
            u2 = act(lambda e: e.activation(topv, topv, ACT.Exp), u1)
            u3 = dve(lambda e: e.tensor_reduce(gs[:, 0:PE_H], topv, AXX, ALU.add), u2)
            u4 = dve(lambda e: e.reciprocal(gs[:, PE_H:], gs[:, 0:PE_H]), u3)
            u5 = dve(lambda e: e.tensor_tensor(pick[:, 2, :].rearrange("p (h k) -> p h k", h=PE_H), topv,
                                               gs[:, PE_H:].unsqueeze(2).to_broadcast([P, PE_H, TOPK]), ALU.mult), u4, h2)
            bank, was = take()
            for w in range(3):
                tk = turn(bank[:, w * P:(w + 1) * P], pick[:, w, :], was, t4, u5, signal=(w == 2))
            last = dve(lambda e, t=t, bank=bank: e.tensor_copy(pick_T[:, :].rearrange("p (w t) -> p w t", w=3)[:, :, t * P:(t + 1) * P],
                                                               bank[:, 0:3 * P].rearrange("p (w t) -> p w t", w=3)), tk)
            give(bank, last)
            picks_ready.append(last)

        Gv = G[:, :].rearrange("p (i t) -> p i t", t=T)
        pT = pick_T[:, :].rearrange("p (w t) -> p w t", w=3)
        TG = 4
        hot_free = [picks_ready, picks_ready]
        hot_a = [abuf[:, i * 512:(i + 1) * 512].rearrange("p (t n) -> p t n", n=P) for i in range(2)]
        hot_b = [abuf[:, 1024 + i * 512:1024 + (i + 1) * 512].rearrange("p (t n) -> p t n", n=P) for i in range(2)]
        g_ready = []
        for q in range(T // TG):
            A_, B_ = hot_a[q % 2], hot_b[q % 2]
            bank, was = take()
            for j in range(TG):
                tok = q * TG + j
                dve(lambda e, j=j, tok=tok, A_=A_: e.tensor_scalar(A_[:, j, :], iota, pT[:, 0, tok:tok + 1], None, ALU.is_equal), hot_free[q % 2])
                tk = dve(lambda e, j=j, tok=tok, B_=B_: e.tensor_scalar(B_[:, j, :], iota, pT[:, 1, tok:tok + 1], pT[:, 2, tok:tok + 1], ALU.is_equal, ALU.mult))
            for j in range(TG):
                m = mm(bank[:, j * P:(j + 1) * P], B_[:, j, :], A_[:, j, :], True, True, was, tk, signal=(j == TG - 1))
            hot_free[q % 2] = m
            src = bank[:, :].rearrange("p (t i) -> p i t", t=TG)
            dst = Gv[:, :, q * TG:(q + 1) * TG]
            if q % 4 == 0:
                ev = dve(lambda e, src=src, dst=dst: e.tensor_copy(dst, src), m, picks_ready)
            else:
                ev = act(lambda e, src=src, dst=dst: e.activation(dst, src, ACT.Copy), m, picks_ready)
            give(bank, ev)
            g_ready.append(ev)

        acc = [take() for _ in range(4)]
        a_buf = [abuf[:, i * 512:(i + 1) * 512] for i in range(4)]
        a_free = [m] * 4
        NQ = NKEYS // 4

        def values_of(q, hid):
            for half_ in range(2):
                blk = load(a["peer_v"][q * 512:(q + 1) * 512, half_ * 512:(half_ + 1) * 512].rearrange("(c p) n -> p c n", p=P), 4, 512)
                for t in range(NT):
                    bank, was = acc[2 * half_ + t]
                    for k in range(4):
                        b, tk_h = hid[k // 2]
                        lhsT = b[:, (k % 2) * T + t * P:(k % 2) * T + (t + 1) * P]
                        tk = mm(bank[:, :], lhsT, blk.view[:, k, :], q == 0 and k == 0, q == NQ - 1 and k == 3,
                                was, tk_h, blk.arrived, signal=(k == 3))
                blk.released = tk
            return tk

        pending = None
        for q in range(NQ):
            blk = panel(a["peer_uT"], D, q * 512, 512)
            hid = []

            def ev(m0, p, tk, q=q):
                i = (2 * q + m0 // 2) % 4
                b = a_buf[i]
                bv = b.rearrange("p (j t) -> p j t", j=2)
                t0 = act(lambda e: e.activation(bv, p, ACT.Gelu), tk, a_free[i])
                t1 = dve(lambda e: e.tensor_tensor(bv, bv, Gv[:, 4 * q + m0:4 * q + m0 + 2, :], ALU.mult), t0, g_ready)
                hid.append((b, t1))
                return t0
            feature_major(h2v, h2, DC, blk, 512, ev)
            if pending is not None:
                tk = values_of(*pending)
                for i in range(2):
                    a_free[(2 * pending[0] + i) % 4] = tk
            pending = (q, hid)
        fin_tick = values_of(*pending)

        x6 = []
        for half_ in range(2):
            for t in range(NT):
                bank, _ = acc[2 * half_ + t]
                tmp_ = abuf[:, (2 * half_ + t) * 512:(2 * half_ + t + 1) * 512]
                t0 = dve(lambda e, bank=bank, tmp_=tmp_, half_=half_: e.tensor_tensor(tmp_, bank[:, :], g2row[:, half_ * 512:(half_ + 1) * 512], ALU.mult),
                         fin_tick, grow_ready[5])
                give(bank, t0)
                v = xr[:, t, half_ * 512:(half_ + 1) * 512]
                x6.append(pool(lambda e, v=v, tmp_=tmp_: e.tensor_tensor(v, v, tmp_, ALU.add), t0, h2))
        done = final_norm([x6], row_block(a["final_g"]))
        for t in range(NT):
            act(lambda e, t=t: e.dma_start(out.rearrange("(t p) d -> p t d", p=P)[:, t, :], xr[:, t, :]).then_inc(s_out, 16), done[t], signal=0)
        act(lambda e: e.wait_ge(s_out, 16 * NT), signal=0)

        with nc.Block() as block:
            @block.sync
            def _(eng):
                sp.play(eng)

            @block.scalar
            def _(eng):
                act.play(eng)

            @block.vector
            def _(eng):
                dve.play(eng)

            @block.gpsimd
            def _(eng):
                pool.play(eng)

            @block.tensor
            def _(eng):
                pe.play(eng)


def constants():
    c = np.zeros((P, N_CONST), np.float32)
    c[:, K_IDENT:K_IDENT + P] = np.eye(P)
    c[:, K_ONES:K_ONES + P] = 1
    c[:, K_IOTA:K_IOTA + P] = np.arange(P)
    c[:, K_MASK + P:K_MASK + 2 * P] = np.where(np.arange(P)[None, :] <= np.arange(P)[:, None], 0, MASKED)
    for o, half, rot in ((0, HALF_M, ROPE), (HALF_M, HALF_D, DIFF_ROT)):
        c[:, K_FREQ + o:K_FREQ + o + half] = np.exp(np.float32(-math.log(THETA)) * np.arange(half, dtype=np.float32) * np.float32(2.0 / rot))
    return c


def pooling_band():
    t = np.arange(T)
    band = np.zeros((T, 4, T), np.float64)
    for g, w in enumerate(POOL_WINDOWS):
        lo, hi = np.clip(t - w // 2, 0, T), np.clip(t + w // 2, 0, T)
        inside = (t[:, None] >= lo[None, :]) & (t[:, None] < hi[None, :])
        band[:, g, :] = inside / (hi - lo)[None, :] - np.eye(T)
    return np.ascontiguousarray(band.astype(np.float32).reshape(NT, P, 4, T).transpose(1, 0, 2, 3).reshape(P, -1))


def window_bias(rpb):
    row, colm = np.arange(T) // GRID_W, np.arange(T) % GRID_W
    kh = min(NA_KH_MAX, ROWS)
    r0 = np.clip(row - kh // 2, 0, ROWS - kh)
    c0 = np.clip(colm - NA_KW // 2, 0, GRID_W - NA_KW)
    ok = ((row[None, :] >= r0[:, None]) & (row[None, :] < (r0 + kh)[:, None])
          & (colm[None, :] >= c0[:, None]) & (colm[None, :] < (c0 + NA_KW)[:, None]))
    ro = np.clip(row[None, :] - row[:, None] + NA_KH_MAX - 1, 0, 2 * NA_KH_MAX - 2)
    co = np.clip(colm[None, :] - colm[:, None] + NA_KW - 1, 0, 2 * NA_KW - 2)
    b = rpb[:, ro, co]
    b[:, ~ok] = MASKED
    return np.ascontiguousarray(b.reshape(NA_H, NT, P, T).transpose(2, 0, 1, 3).reshape(P, -1))


def kernel(**inputs):
    import concourse.bacc as bacc
    from concourse.bass_utils import run_bass_kernel_spmd

    v = {k: np.asarray(x) for k, x in inputs.items()}
    by_col = lambda x: x.reshape(-1, P).T
    arrays = {
        "x": v["x"][0],
        "pos": v["positions"].reshape(NT, P).T,
        "const": constants(),
        "cols": np.concatenate([by_col(v[n]) for n in (
            "norm_mix_g", "mla_q_norm_g", "mla_kv_norm_g", "b_gate", "norm_ffn_g", "c_2", "c_ctx_2", "norm1_g_2",
            "norm2_g_2", "pool_scale_2", "ada_b_2")], axis=1),
        "lam": np.concatenate([v[n].reshape(-1) for n in ("diff_lambda_q1", "diff_lambda_k1", "diff_lambda_q2", "diff_lambda_k2")]),
        "subln": v["diff_subln_g"][0],
        "w_in": v["w_in"][0], "w_uq": v["mla_w_uq"][0], "w_ukv": v["mla_w_ukv"][0],
        "w_b_mla": v["w_branch_mla"][0], "w_b_diff": v["w_branch_diff"][0], "w_out": v["w_out"][0],
        "w_gate": v["w_ffn_gate"][0], "w_up": v["w_ffn_up"][0], "w_down": v["w_ffn_down"][0],
        "norm_final_g": v["norm_final_g"],
        "ctx": v["ctx_2"][0], "ada_w": v["ada_w_2"][0],
        "ada_b_g1": v["ada_b_2"][0, 2 * D:3 * D], "ada_b_g2": v["ada_b_2"][0, 5 * D:6 * D],
        "w_in2": v["w_in_2"][0], "na_bias": window_bias(v["na_rpb_2"][0].copy()), "band": pooling_band(),
        "pool_w": v["pool_w_2"][0].transpose(1, 0, 2).reshape(P, -1), "w_out2": v["w_out_2"][0],
        "peer_wq": v["peer_wq_2"][0], "keys_T": v["peer_keys_2"][0].transpose(3, 0, 1, 2).reshape(P, -1),
        "peer_uT": v["peer_u_2"][0].T, "peer_v": v["peer_v_2"][0], "final_g": v["final_g_2"],
    }
    arrays = {k: np.ascontiguousarray(x) for k, x in arrays.items()}
    nc = bacc.Bacc("TRN2", target_bir_lowering=False, num_devices=1)
    aps = {k: nc.dram_tensor(k, x.shape, mybir.dt.from_np(x.dtype), kind="ExternalInput").ap() for k, x in arrays.items()}
    out = nc.dram_tensor("y", (T, D), F32, kind="ExternalOutput").ap()
    build(nc, aps, out)
    r = run_bass_kernel_spmd(nc, [arrays], core_ids=[0])
    return r.results[0]["y"].reshape(1, T, D)
```

```python
import math

import numpy as np

import concourse.bass as bass
from concourse import mybir
from concourse.alu_op_type import AluOpType as ALU

F32 = mybir.dt.float32
F32R = mybir.dt.float32r
U32 = mybir.dt.uint32
I32 = mybir.dt.int32
ACT = mybir.ActivationFunctionType
AXX = mybir.AxisListType.X

P = 128
D = 1024
T = 256
NT = T // P
DC = D // P
EPS = 1e-6
THETA = 500000.0
MLA_H, NOPE, ROPE, MLA_V, Q_RANK, KV_RANK = 8, 64, 32, 64, 384, 256
MLA_QK = NOPE + ROPE
DIFF_H, DIFF_D, DIFF_ROT = 4, 64, 16
DIFF_V = 2 * DIFF_D
LAT = Q_RANK + KV_RANK + ROPE
FFN = 2816
LAMBDA_INIT = 0.8 - 0.6 * math.exp(-0.3 * 0)
NA_H, NA_D, GRID_W, NA_KW, NA_KH_MAX = 8, 64, 64, 16, 8
ROWS = T // GRID_W
POOL_WINDOWS = (2, 4, 8, 16)
D_POOL = 512
PE_H, NKEYS, TOPK = 8, 128, 16
MASKED = -1e30
LOWEST = -3.4e38

COLS = {}
_at = 0
for _name, _n in (("norm_mix_g", 8), ("q_norm_g", 3), ("kv_norm_g", 2), ("b_gate", 16), ("norm_ffn_g", 8),
                  ("c", 8), ("c_ctx", 8), ("norm1_g", 8), ("norm2_g", 8), ("pool_scale", 4), ("ada_b", 48)):
    COLS[_name] = (_at, _n)
    _at += _n
N_COLS = _at
K_IDENT, K_ONES, K_IOTA, K_MASK, K_FREQ = 0, 128, 256, 384, 640
HALF_M, HALF_D = ROPE // 2, DIFF_ROT // 2
N_FREQ = HALF_M + HALF_D
N_CONST = K_FREQ + N_FREQ

RING_SLOTS = 5
BLOCK = 1024
SLOT = 2 * BLOCK
POOL_SHARE = 4
AHEAD = 3
UNIT = 256
HID_BUFS = 3

G_WORDS = NKEYS * T
SBUF_BASE = 16512
OFF = dict(
    gates_T=0, dq=4096, dk=5120, dv=6144, lat=7168, qm=8512, kv=10048, km=12096, lat_hi=13632, lat_lo=14912,
    qm_T=16192, km_T=18240, dq_T=20288, dk_T=21312, o_mla=22336, o_diff=23360,
    xres=24384, xs=26432, score_bufs=26432, prob_T=28480, rope_tmp=29504, rope=30016, small=30304, posi=30688, turns=30696,
    oa_hi=7168, oa_lo=8192, ob_hi=9216, ob_lo=10240, merged=16192, merged_hi=12096, merged_lo=14144,
    ada_x=0, ada_c=6144,
    ctx_hi=8192, ctx_lo=10240, zx=12288, zc=16384, q_T=18432, k_T=19456, kc_T=20480, attn=21504, pooled_T=22528,
    mix_hi=0, mix_lo=2048, g1row=31744, g2row=30720, gated=18432, shifted=28480,
    s=0, s_work=4096, cand_work=6144, pq_T=8192, cand=12288, eq=14336, v12=18432, i12=18688, i12f=18944,
    tv=19200, topi=19584, ab=19712, pick=19968,
    G=0, act_hi=32768, act_lo=34816, ring=36864, hid=36864 + 5 * 2048, const=50176, cols=50840, mod=50968, stat=51024, pick_T=51520,
)


class Lane:

    def __init__(self, name, sem):
        self.name, self.sem, self.count, self.steps = name, sem, 0, []

    def __call__(self, issue, *after, signal=True):
        self.steps.append((issue, frozen(after), signal))
        self.count += signal
        return (self.sem, self.count) if signal else None

    def play(self, eng):
        passed = {}
        for issue, after, signal in self.steps:
            for tick in flat(after):
                sem, value = tick
                if passed.get(id(sem), 0) < value:
                    eng.wait_ge(sem, value)
                    passed[id(sem)] = value
            ins = issue(eng)
            if signal is True:
                ins.then_inc(self.sem, 1)


def frozen(ticks):
    return tuple(frozen(t) for t in ticks) if isinstance(ticks, (list, tuple)) else ticks


def flat(ticks):
    for t in ticks:
        if t is None:
            continue
        if isinstance(t, Block):
            yield from flat((t.released,))
        elif isinstance(t, tuple) and len(t) == 2 and not isinstance(t[1], (tuple, list)) and t[1] is not None:
            yield t
        else:
            yield from flat(t)


class Block:

    def __init__(self, name):
        self.name, self.released = name, None


class Pair:

    def __init__(self, hi, lo):
        self.hi, self.lo = hi, lo


def build(nc, a, out, parked_x, parked_g2):
    from contextlib import ExitStack
    ctx = ExitStack()
    with ctx:
        sem = lambda name: ctx.enter_context(nc.semaphore(name))

        def place(name, words, dt=F32, offset=None):
            o = OFF[name] if offset is None else offset
            return nc.alloc_sbuf_tensor_at("sb_" + name, [P, words], dt, offset=SBUF_BASE + 4 * o)[:, :]

        banks = [ctx.enter_context(nc.psum_tensor(f"bank{i}", [P, 512], F32)) for i in range(8)]
        const, cols, stat, pick_T = place("const", N_CONST), place("cols", N_COLS), place("stat", 490), place("pick_T", 3 * T)
        xres, posi = place("xres", NT * D), place("posi", NT, I32)

        pe, act, dve, pool, sp = (Lane(n, sem(f"{n}_done")) for n in ("pe", "act", "dve", "pool", "sp"))
        slot_sem = [sem(f"slot{i}_arrived") for i in range(RING_SLOTS)]
        s_x, s_const, s_cols, s_pos, s_lam, s_sub, s_park, s_out = (
            sem(n) for n in ("x_arrived", "const_arrived", "cols_arrived", "pos_arrived", "lam_arrived",
                             "subln_arrived", "parked", "out_stored"))

        plan = []

        def by_chunks(w, r0, kc, c0, n):
            return w[r0:r0 + kc * P, c0:c0 + n].rearrange("(c p) n -> p c n", p=P)

        def plan_panel(name, rows, c0, n):
            step = 2 if n > UNIT else 4
            for k0 in range(0, rows // P, step):
                kc = min(step, rows // P - k0)
                plan.append((name, by_chunks(a[name], k0 * P, kc, c0, n), kc, n, True))

        def plan_rows(name, r0):
            for c0 in (0, 512):
                plan.append((name, by_chunks(a[name], r0, 2, c0, 512), 2, 512, True))

        def plan_plain(name, src, kc, n):
            plan.append((name, src, kc, n, False))

        for c0 in (0, LAT // 2):
            plan_panel("w_in", D, c0, LAT // 2)
        for j in range(3):
            plan_panel("w_in", D, LAT + 512 * j, 512)
        for c0 in (0, 384):
            plan_panel("w_uq", Q_RANK, c0, 384)
        for c0 in (0, 512):
            plan_panel("w_ukv", KV_RANK, c0, 512)
        for j in range(8):
            plan_panel("w_in", D, LAT + 1536 + UNIT * j, UNIT)
        for j in range(4):
            plan_panel("w_b_mla", 512, UNIT * j, UNIT)
            plan_panel("w_b_diff", 512, UNIT * j, UNIT)
        for j in range(2):
            plan_panel("w_out", D, 512 * j, 512)
        N_ADA = 6 * D // 512 * 2
        ADA_AT = {u: [i for i in range(N_ADA) if i * 10 // N_ADA == u] for u in range(FFN // UNIT)}
        for u in range(FFN // UNIT):
            plan_panel("w_gate", D, UNIT * u, UNIT)
            plan_panel("w_up", D, UNIT * u, UNIT)
            if u:
                plan_rows("w_down", UNIT * (u - 1))
            for i in ADA_AT[u]:
                plan_plain("ada_w", by_chunks(a["ada_w"], i % 2 * 512, 4, i // 2 * 512, 512), 4, 512)
        plan_rows("w_down", FFN - UNIT)
        for name in ("norm_final_g", "ada_b_g1", "ada_b_g2"):
            plan_plain(name, a[name].partition_broadcast(P), 1, D)
        plan_plain("ctx", a["ctx"].rearrange("(t p) d -> p t d", p=P), 2, D)
        for j in (1, 2, 3):
            plan_panel("w_in2", D, 512 * j, 512)
        for i in range(2):
            plan_plain("na_bias", a["na_bias"][:, i * SLOT:(i + 1) * SLOT], 1, SLOT)
            if i == 0:
                plan_panel("w_in2", D, 0, 512)
        plan_plain("band", a["band"], 1, SLOT)
        plan_plain("pool_w", a["pool_w"], 1, 512)
        for j in range(2):
            plan_panel("w_out2", D, 512 * j, 512)
        for j in range(8):
            plan_panel("peer_wq", D, UNIT * j, UNIT)
        plan_plain("keys_T", a["keys_T"], 1, 2048)
        N_UNITS = NKEYS * NKEYS // UNIT
        V_LAG = HID_BUFS - 1
        for u in range(N_UNITS + V_LAG):
            if u < N_UNITS:
                plan_panel("peer_uT", D, UNIT * u, UNIT)
            if u >= V_LAG:
                plan_rows("peer_v", UNIT * (u - V_LAG))
        plan_plain("parked_x", parked_x.rearrange("(t p) d -> p t d", p=P), 2, D)
        plan_plain("parked_g2", parked_g2, 1, D)
        plan_plain("final_g", a["final_g"].partition_broadcast(P), 1, D)

        ring = [dict(full=place(f"slot{i}", SLOT, F32, OFF["ring"] + i * SLOT),
                     raw=place(f"raw{i}", BLOCK, F32, OFF["ring"] + i * SLOT),
                     lo=place(f"lo{i}", BLOCK, F32R, OFF["ring"] + i * SLOT),
                     hi=place(f"hi{i}", BLOCK, F32R, OFF["ring"] + i * SLOT + BLOCK)) for i in range(RING_SLOTS)]
        issued, taken, n_split = [], [0], [0]
        dram_ready = {}

        def issue(i):
            name, src, kc, n, split = plan[i]
            s = i % RING_SLOTS
            cut = lambda t: t[:, 0:kc * n].rearrange("p (c n) -> p c n", c=kc)
            blk = Block(name)
            before = issued[i - RING_SLOTS] if i >= RING_SLOTS else None
            dst = ring[s]["raw" if split else "full"]
            view = cut(dst) if len(src.shape) == 3 else dst[:, 0:n]
            blk.arrived = (slot_sem[s], 16 * (i // RING_SLOTS + 1))
            sp(lambda e: e.dma_start(view, src).then_inc(slot_sem[s], 16), before, dram_ready.get(name), signal=0)
            if split:
                w = kc * n
                raw, hi, lo = dst[:, 0:w], ring[s]["hi"][:, 0:w], ring[s]["lo"][:, 0:w]
                blk.hi_ready = act(lambda e: e.activation(hi, raw, ACT.Copy), blk.arrived)
                n_split[0] += 1
                lane = pool if n_split[0] % POOL_SHARE == 0 else dve
                blk.lo_ready = lane(lambda e: e.tensor_tensor(lo, raw, hi.bitcast(F32), ALU.subtract), blk.hi_ready, blk.arrived)
                blk.hi, blk.lo = cut(ring[s]["hi"]), cut(ring[s]["lo"])
            else:
                blk.view = cut(dst)
            issued.append(blk)

        def use(name, count=1):
            out_ = []
            for _ in range(count):
                i = taken[0]
                taken[0] += 1
                while len(issued) <= min(i + AHEAD, len(plan) - 1):
                    issue(len(issued))
                assert issued[i].name == name, (issued[i].name, name)
                out_.append(issued[i])
            return out_

        free = [(b, None) for b in banks]

        def take():
            return free.pop(0)

        def give(b, tick):
            free.append((b, tick))

        n_stat = [0]

        def stat_col(n=1):
            o = n_stat[0]
            n_stat[0] += n
            assert n_stat[0] <= 490
            return stat[:, o:o + n]

        def col(name, c, n=1):
            o, m = COLS[name]
            assert c + n <= m
            return cols[:, o + c:o + c + n]

        ident = const[:, K_IDENT:K_IDENT + P]
        ones = const[:, K_ONES:K_ONES + P]
        iota = const[:, K_IOTA:K_IOTA + P]
        mask = const[:, K_MASK:K_MASK + 2 * P]
        freq = const[:, K_FREQ:K_FREQ + N_FREQ]

        def by_chunk(t, w=T):
            return t.rearrange("p (c t) -> p c t", t=w)

        def token_buf(name, width):
            return place(name, NT * width).rearrange("p (t d) -> p t d", t=NT)

        def mm(dst, lhsT, rhs, start, stop, *after, signal=False, shared=False):
            return pe(lambda e: e.matmul(dst, lhsT, rhs, start=start, stop=stop, skip_group_check=shared), *after, signal=signal)

        def turn(dst, src, *after, signal=False):
            n = src.shape[0]
            return pe(lambda e: e.transpose(dst, src, ident[0:n, 0:n]), *after, signal=signal)

        def round_hi(hi, src, *after):
            return act(lambda e: e.activation(hi, src, ACT.Copy), *after)

        def rest_lo(lo, src, hi, *after):
            return dve(lambda e: e.tensor_tensor(lo, src, hi.bitcast(F32), ALU.subtract), *after)

        sp(lambda e: e.dma_start(xres.rearrange("p (t d) -> p t d", t=NT),
                                 a["x"].rearrange("(t p) d -> p t d", p=P)).then_inc(s_x, 16), signal=0)
        x_in = (s_x, 16)
        for dst, src, s in ((const, a["const"], s_const), (cols[:, 0:N_COLS], a["cols"], s_cols), (posi, a["pos"], s_pos)):
            sp(lambda e, dst=dst, src=src, s=s: e.dma_start(dst, src).then_inc(s, 16), signal=0)
        const_in, cols_in, pos_in = (s_const, 16), (s_cols, 16), (s_pos, 16)
        small = place("small", 384)
        lam_rows = small[:, 0:4 * DIFF_D]
        subln = small[:, 256:256 + DIFF_V]
        sp(lambda e: e.dma_start(lam_rows, a["lam"].partition_broadcast(P)).then_inc(s_lam, 16), signal=0)
        sp(lambda e: e.dma_start(subln, a["subln"].partition_broadcast(P)).then_inc(s_sub, 16), signal=0)
        xr = xres.rearrange("p (t d) -> p t d", t=NT)
        xs = token_buf("xs", D)

        half = stat_col()
        half_set = pool(lambda e: e.memset(half, -0.5))

        def inverse_rms(total, width, after):
            n = total.shape[1]
            mean, r = stat_col(n), stat_col(n)
            t0 = dve(lambda e: e.tensor_scalar(mean, total, 1.0 / width, EPS, ALU.mult, ALU.add), after)
            hb = half if n == 1 else half.to_broadcast([P, n])
            t1 = pool(lambda e: e.tensor_tensor(r, mean, hb, ALU.pow), t0, half_set)
            return r, t1

        def squares(src, junk, after, lane):
            total = stat_col()
            if lane is act:
                return total, act(lambda e: e.activation(junk, src, ACT.Square, accum_out=total), after)
            return total, dve(lambda e: e.tensor_tensor_reduce(junk, src, src, 1.0, 0.0, ALU.mult, ALU.add, total), after)

        shifted = place("shifted", 1024)
        shift_free = [None, None]

        def normed_T(src, dst, gain, shift, after, gain_ready, tmp_free=None):
            scaled = []
            for t in range(NT):
                lane = (act, dve)[t % 2]
                total, t0 = squares(src[:, t, :], xs[:, t, :], [after, tmp_free], lane)
                r, t1 = inverse_rms(total, D, t0)
                if lane is act:
                    scaled.append(act(lambda e, t=t, r=r: e.activation(xs[:, t, :], src[:, t, :], ACT.Copy, scale=r), t1, t0))
                else:
                    scaled.append(dve(lambda e, t=t, r=r: e.tensor_scalar(xs[:, t, :], src[:, t, :], r, None, ALU.mult), t1, t0))
            done = []
            for c2 in range(DC // 2):
                bank, was = take()
                for j in range(2):
                    for t in range(NT):
                        c = 2 * c2 + j
                        tk = turn(bank[:, j * T + t * P:j * T + (t + 1) * P], xs[:, t, c * P:(c + 1) * P],
                                  was, scaled, const_in, signal=(j == 1 and t == NT - 1))
                if shift is None:
                    tk = [tk]
                    for j in range(2):
                        c = 2 * c2 + j
                        tk.append(act(lambda e, c=c, j=j, bank=bank: e.activation(dst.hi[:, c, :], bank[:, j * T:(j + 1) * T], ACT.Copy, scale=gain[:, c:c + 1]),
                                      tk[0], gain_ready))
                    for j in range(2):
                        c = 2 * c2 + j
                        lo = dve(lambda e, c=c, j=j, bank=bank: e.scalar_tensor_tensor(
                            dst.lo[:, c, :], bank[:, j * T:(j + 1) * T], gain[:, c:c + 1], dst.hi[:, c, :].bitcast(F32), ALU.mult, ALU.subtract), tk, gain_ready)
                    give(bank, lo)
                else:
                    buf = shifted[:, c2 % 2 * 512:(c2 % 2 + 1) * 512]
                    for j in range(2):
                        c = 2 * c2 + j
                        ev = act(lambda e, c=c, j=j, bank=bank, buf=buf: e.activation(buf[:, j * T:(j + 1) * T], bank[:, j * T:(j + 1) * T], ACT.Identity,
                                                                                    bias=shift[:, c:c + 1], scale=gain[:, c:c + 1]),
                                 tk, gain_ready, shift_free[c2 % 2])
                    give(bank, ev)
                    bv = by_chunk(buf)
                    hi_, lo_ = dst.hi[:, 2 * c2:2 * c2 + 2, :], dst.lo[:, 2 * c2:2 * c2 + 2, :]
                    t0 = dve(lambda e, hi_=hi_, bv=bv: e.tensor_copy(hi_, bv), ev)
                    lo = rest_lo(lo_, bv, hi_, t0)
                    shift_free[c2 % 2] = lo
                done.append([tk, lo])
            return done

        def token_major(x, ready, kc, name, n, evacuate):
            opened = [take() for _ in range(NT)]
            n_blk = (kc + 1) // 2
            ticks = [None] * NT
            for b in range(n_blk):
                blk = use(name)[0]
                k0, kb = 2 * b, min(2, kc - 2 * b)
                for t in range(NT):
                    bank, was = opened[t]
                    for k in range(kb):
                        for part in (x.hi, x.lo):
                            mm(bank[:, 0:n], part[:, k0 + k, t * P:(t + 1) * P], blk.hi[:, k, :], b == 0 and k == 0 and part is x.hi, False,
                               was, ready, blk.hi_ready)
                for t in range(NT):
                    bank, was = opened[t]
                    for k in range(kb):
                        ticks[t] = mm(bank[:, 0:n], x.hi[:, k0 + k, t * P:(t + 1) * P], blk.lo[:, k, :], False, b == n_blk - 1 and k == kb - 1,
                                      blk.lo_ready, signal=(k == kb - 1))
                blk.released = ticks[NT - 1]
            res = []
            for t in range(NT):
                bank, _ = opened[t]
                ev = evacuate(t, bank[:, 0:n], ticks[t])
                give(bank, ev)
                res.append(ev)
            return res

        def feature_major(x, ready, kc, name, evacuate):
            bank, was = take()
            n_blk = (kc + 3) // 4
            for b in range(n_blk):
                blk = use(name)[0]
                k0, kb = 4 * b, min(4, kc - 4 * b)
                for j in range(2):
                    for k in range(kb):
                        for part in (x.hi, x.lo):
                            mm(bank[:, j * T:(j + 1) * T], blk.hi[:, k, j * P:(j + 1) * P], part[:, k0 + k, :],
                               b == 0 and j == 0 and k == 0 and part is x.hi, False, was, ready, blk.hi_ready, shared=True)
                for j in range(2):
                    for k in range(kb):
                        end = j == 1 and k == kb - 1
                        tk = mm(bank[:, j * T:(j + 1) * T], blk.lo[:, k, j * P:(j + 1) * P], x.hi[:, k0 + k, :],
                                False, end and b == n_blk - 1, blk.lo_ready, signal=end, shared=True)
                blk.released = tk
            ev = evacuate(by_chunk(bank[:, 0:2 * T]), tk)
            give(bank, ev)
            return ev

        def rows_onto(acc, hid, ready, name, first, last):
            for half_ in range(2):
                blk = use(name)[0]
                for t in range(NT):
                    bank, was = acc[2 * half_ + t]
                    for k in range(2):
                        for part in (hid.hi, hid.lo):
                            mm(bank[:, :], part[:, k, t * P:(t + 1) * P], blk.hi[:, k, :], first and k == 0 and part is hid.hi, False,
                               was, ready, blk.hi_ready)
                for t in range(NT):
                    bank, _ = acc[2 * half_ + t]
                    for k in range(2):
                        tk = mm(bank[:, :], hid.hi[:, k, t * P:(t + 1) * P], blk.lo[:, k, :], False, last and k == 1,
                                blk.lo_ready, signal=(k == 1))
                blk.released = tk
            return tk

        flip = [0]

        def copy(dst, src, *after):
            flip[0] += 1
            if flip[0] % 2:
                return act(lambda e: e.activation(dst, src, ACT.Copy), *after)
            return dve(lambda e: e.tensor_copy(dst, src), *after)

        def turned(src, dst_of, blocks_of_cols, ready, *after):
            ticks = []
            for i0 in range(0, len(blocks_of_cols), 2):
                group = blocks_of_cols[i0:i0 + 2]
                bank, was = take()
                for j, (c0, n) in enumerate(group):
                    for t in range(NT):
                        tk = turn(bank[0:n, j * T + t * P:j * T + (t + 1) * P], src[:, t, c0:c0 + n], was, ready, *after,
                                  signal=(j == len(group) - 1 and t == NT - 1))
                n = group[0][1]
                dst, got = dst_of(i0, len(group)), by_chunk(bank[0:n, 0:len(group) * T])
                if isinstance(dst, Pair):
                    t0 = round_hi(dst.hi, got, tk)
                    ev = rest_lo(dst.lo, got, dst.hi, t0, tk)
                    ticks.append([t0, ev])
                else:
                    ev = copy(dst[0:n], got, tk)
                    ticks.append(ev)
                give(bank, ev)
            return ticks

        def pair_view(x, i, n):
            return Pair(x.hi[:, i:i + n, :], x.lo[:, i:i + n, :])

        def pair(name, chunks_):
            hi, lo = (place(f"{name}_{w}", chunks_ * T, F32R) for w in ("hi", "lo"))
            return Pair(by_chunk(hi), by_chunk(lo))

        score_bufs, prob_T = place("score_bufs", 2048), place("prob_T", 1024)
        sb_ring = [score_bufs[:, i * 512:(i + 1) * 512] for i in range(4)]
        pt_ring = [prob_T[:, i * 512:(i + 1) * 512] for i in range(2)]
        att_stats = stat_col(12)
        stat_free = [None] * 4

        def attention(items, ready, meanwhile=()):
            N = len(items)
            meanwhile = list(meanwhile)
            steps, run = len(meanwhile), 0
            out_ticks = []
            buf_free, pt_free = [ready] * 4, [ready] * 2
            for i in range(N + 3):
                if i < N:
                    it = items[i]
                    opened = [take() for _ in range(it["banks"])]
                    tk = it["scores"]([b for b, _ in opened], [was for _, was in opened] + [ready])
                    buf = sb_ring[i % 4][:, 0:it["n"]]
                    it["buf"] = buf
                    msk = it["masked"]([b for b, _ in opened], buf, [tk, buf_free[i % 4]])
                    for (b, _), m_ in zip(opened, msk):
                        give(b, m_)
                    nmax, tot, inv = (att_stats[:, 3 * (i % 4) + j:3 * (i % 4) + j + 1] for j in range(3))
                    t1 = dve(lambda e, buf=buf, nmax=nmax: e.tensor_reduce(nmax, buf, AXX, ALU.max, negate=True), msk, stat_free[i % 4])
                    t2 = act(lambda e, buf=buf, nmax=nmax, tot=tot: e.activation(buf, buf, ACT.Exp, bias=nmax, accum_out=tot), t1, msk)
                    it["inv"], it["exp"], it["tot"] = inv, t2, tot
                if i >= 2 and i - 2 < N:
                    it = items[i - 2]
                    kc = it["n"] // P
                    bank, was = take()
                    for k in range(kc):
                        tk = turn(bank[:, k * P:(k + 1) * P], it["buf"][:, k * P:(k + 1) * P], was, it["exp"], signal=(k == kc - 1))
                    buf_free[(i - 2) % 4] = tk
                    pt = pt_ring[i % 2][:, 0:it["n"]]
                    it["pt"] = pt
                    it["ptt"] = copy(pt, bank[:, 0:it["n"]], tk, pt_free[i % 2])
                    give(bank, it["ptt"])
                    it["invt"] = dve(lambda e, inv=it["inv"], tot=it["tot"]: e.reciprocal(inv, tot), it["exp"])
                if i >= 3:
                    it = items[i - 3]
                    bank, was = take()
                    kc = it["n"] // P
                    for k in range(kc):
                        tk = mm(bank[:, 0:P], it["pt"][:, k * P:(k + 1) * P], it["values"][k], k == 0, k == kc - 1,
                                was, it["ptt"], it["values_ready"], signal=(k == kc - 1))
                    pt_free[(i - 3) % 2] = tk
                    ev = it["finish"](bank, it["inv"], [tk, it["invt"]])
                    stat_free[(i - 3) % 4] = ev
                    give(bank, ev)
                    out_ticks.append(ev)
                while meanwhile and run * (N + 1) < (i + 1) * steps:
                    meanwhile.pop(0)()
                    run += 1
            return out_ticks

        posf = stat_col(NT)
        t_pos = dve(lambda e: e.tensor_copy(posf, posi), pos_in)
        nf = NT * N_FREQ
        rope_w = place("rope", 6 * nf)
        turns = place("turns", nf, I32)
        ang, red, tmp, sin_t, cos_t, nturn = (rope_w[:, i * nf:(i + 1) * nf] for i in range(6))
        tk = None
        for t in range(NT):
            tk = dve(lambda e, t=t: e.tensor_scalar(ang[:, t * N_FREQ:(t + 1) * N_FREQ], freq, posf[:, t:t + 1], None, ALU.mult),
                     t_pos, const_in)
        TWO_PI = 2 * math.pi
        c1 = 6.28125
        c2 = float(np.float32(np.round((TWO_PI - c1) * 2**21) / 2**21))
        c3 = TWO_PI - c1 - c2
        tk = dve(lambda e: e.tensor_scalar(turns, ang, 1.0 / TWO_PI, None, ALU.mult), tk)
        tk = dve(lambda e: e.tensor_copy(nturn, turns), tk)
        tk = dve(lambda e: e.scalar_tensor_tensor(red, nturn, -c1, ang, ALU.mult, ALU.add), tk)
        for c in (c2, c3):
            tk = dve(lambda e, c=c: e.scalar_tensor_tensor(red, nturn, -c, red, ALU.mult, ALU.add), tk)

        def wrap(v, tk):
            tk = dve(lambda e: e.tensor_scalar(tmp, v, math.pi, -TWO_PI, ALU.is_gt, ALU.mult), tk)
            tk = dve(lambda e: e.tensor_tensor(v, v, tmp, ALU.add), tk)
            tk = dve(lambda e: e.tensor_scalar(tmp, v, -math.pi, TWO_PI, ALU.is_lt, ALU.mult), tk)
            tk = dve(lambda e: e.tensor_tensor(v, v, tmp, ALU.add), tk)
            return dve(lambda e: e.tensor_scalar(v, v, 3.1415925, -3.1415925, ALU.min, ALU.max), tk)

        tk = wrap(red, tk)
        t_sin = act(lambda e: e.activation(sin_t, red, ACT.Sin), tk)
        tk = dve(lambda e: e.tensor_scalar(ang, red, math.pi / 2, None, ALU.add), tk)
        tk = wrap(ang, tk)
        rope_ready = [act(lambda e: e.activation(cos_t, ang, ACT.Sin), tk), t_sin]

        rope_tmp = place("rope_tmp", 512)
        rope_last = [None]

        def rope(v, c0, heads, stride, half_n, f0, after):
            ticks = []
            for t in range(NT):
                w = v[:, t, 0:heads * stride].rearrange("p (h s) -> p h s", s=stride)
                x1, x2 = w[:, :, c0:c0 + half_n], w[:, :, c0 + half_n:c0 + 2 * half_n]
                co = cos_t[:, t * N_FREQ + f0:t * N_FREQ + f0 + half_n].unsqueeze(1).to_broadcast([P, heads, half_n])
                si = sin_t[:, t * N_FREQ + f0:t * N_FREQ + f0 + half_n].unsqueeze(1).to_broadcast([P, heads, half_n])
                n = heads * half_n
                tm = [rope_tmp[:, i * 128:i * 128 + n].rearrange("p (h s) -> p h s", s=half_n) for i in range(4)]
                tt = lambda o, x, y, op, *af: pool(lambda e: e.tensor_tensor(o, x, y, op), *af)
                tt(tm[0], x1, co, ALU.mult, after, rope_ready, rope_last[0])
                tt(tm[1], x2, si, ALU.mult)
                tt(tm[2], x2, co, ALU.mult)
                a1 = tt(tm[3], x1, si, ALU.mult)
                tt(x1, tm[0], tm[1], ALU.subtract, a1)
                rope_last[0] = tt(x2, tm[2], tm[3], ALU.add, a1)
                ticks.append(rope_last[0])
            return ticks

        lam_s, lam_e, lam_neg = stat_col(2), stat_col(2), stat_col()
        lam_junk = stat_col(DIFF_D)
        for i in range(2):
            tk = dve(lambda e, i=i: e.tensor_tensor_reduce(lam_junk, lam_rows[:, 2 * i * DIFF_D:(2 * i + 1) * DIFF_D],
                                                           lam_rows[:, (2 * i + 1) * DIFF_D:(2 * i + 2) * DIFF_D],
                                                           1.0, 0.0, ALU.mult, ALU.add, lam_s[:, i:i + 1]), (s_lam, 16), tk)
        tk = act(lambda e: e.activation(lam_e, lam_s, ACT.Exp), tk)
        tk = dve(lambda e: e.tensor_scalar(lam_neg, lam_e[:, 1:2], -LAMBDA_INIT, None, ALU.add), tk)
        lam_ready = dve(lambda e: e.tensor_tensor(lam_neg, lam_neg, lam_e[:, 0:1], ALU.subtract), tk)

        cs = stat_col(2 * DC)
        t_cs = act(lambda e: e.activation(cs, cols[:, COLS["c"][0]:COLS["c"][0] + 2 * DC], ACT.Silu), cols_in)

        act_T = pair("act", DC)
        xn = normed_T(xr, act_T, col("norm_mix_g", 0, 8), None, x_in, cols_in)

        lat = token_buf("lat", LAT)
        lat_ready = []
        for c0 in (0, LAT // 2):
            lat_ready.append(token_major(act_T, xn, DC, "w_in", LAT // 2, lambda t, p, tk, c0=c0: copy(lat[:, t, c0:c0 + LAT // 2], p, tk)))
        kpe = lat[:, :, Q_RANK + KV_RANK:LAT]
        t_kpe = rope(kpe, 0, 1, ROPE, HALF_M, 0, lat_ready)

        dq, dk, dv = (token_buf(n, 512) for n in ("dq", "dk", "dv"))
        km = token_buf("km", 768)
        lat_T = pair("lat", 5)
        got = []
        for j, dst in enumerate((dq, dk, dv)):
            got.append(token_major(act_T, xn, DC, "w_in", 512, lambda t, p, tk, dst=dst: copy(dst[:, t, :], p, tk)))
            if j:
                continue
            lat_scaled = []
            for t in range(NT):
                for j2, (c0, n) in enumerate(((0, Q_RANK), (Q_RANK, KV_RANK))):
                    total, t0 = squares(lat[:, t, c0:c0 + n], km[:, t, j2 * 384:j2 * 384 + n], lat_ready, (act, dve)[j2])
                    r, t1 = inverse_rms(total, n, t0)
                    lat_scaled.append(dve(lambda e, t=t, c0=c0, n=n, r=r: e.tensor_scalar(lat[:, t, c0:c0 + n], lat[:, t, c0:c0 + n], r, None, ALU.mult), t1, t0))
            lat_T_ready = []
            g0 = COLS["q_norm_g"][0]
            for c in range(5):
                bank, was = take()
                for t in range(NT):
                    tk = turn(bank[:, t * P:(t + 1) * P], lat[:, t, c * P:(c + 1) * P], was, lat_scaled, signal=(t == NT - 1))
                g = cols[:, g0 + c:g0 + c + 1]
                t0 = act(lambda e, c=c, bank=bank, g=g: e.activation(lat_T.hi[:, c, :], bank[:, 0:T], ACT.Copy, scale=g), tk)
                ev = dve(lambda e, c=c, bank=bank, g=g: e.scalar_tensor_tensor(lat_T.lo[:, c, :], bank[:, 0:T], g, lat_T.hi[:, c, :].bitcast(F32),
                                                                               ALU.mult, ALU.subtract), t0, tk)
                give(bank, ev)
                lat_T_ready.append([t0, ev])
        t_dq = rope(dq, 0, 8, DIFF_D, HALF_D, HALF_M, got[0])
        t_dk = rope(dk, 0, 8, DIFF_D, HALF_D, HALF_M, got[1])
        dv_ready = got[2]

        qm, kv = token_buf("qm", 768), token_buf("kv", 1024)
        q_up = []
        for c0 in (0, 384):
            q_up.append(token_major(pair_view(lat_T, 0, 3), lat_T_ready, 3, "w_uq", 384, lambda t, p, tk, c0=c0: copy(qm[:, t, c0:c0 + 384], p, tk)))
        t_qm = rope(qm, NOPE, MLA_H, MLA_QK, HALF_M, 0, q_up)
        kv_up = []
        for c0 in (0, 512):
            kv_up.append(token_major(pair_view(lat_T, 3, 2), lat_T_ready, 2, "w_ukv", 512, lambda t, p, tk, c0=c0: copy(kv[:, t, c0:c0 + 512], p, tk)))
        km_ready = []
        for t in range(NT):
            kv_h = kv[:, t, :].rearrange("p (h s) -> p h s", s=2 * NOPE)
            km_h = km[:, t, :].rearrange("p (h s) -> p h s", s=MLA_QK)
            km_ready.append(dve(lambda e, o=km_h, i=kv_h: e.tensor_copy(o[:, :, 0:NOPE], i[:, :, 0:NOPE]), kv_up, lat_scaled))
            km_ready.append(pool(lambda e, o=km_h, t=t: e.tensor_copy(o[:, :, NOPE:MLA_QK], kpe[:, t, :].unsqueeze(1).to_broadcast([P, MLA_H, ROPE])), t_kpe, lat_scaled))

        gates_T = by_chunk(place("gates_T", 4096))
        gates_raw = []

        def gate_panel(j):
            def ev(p, tk):
                gates_raw.append(copy(gates_T[:, 2 * j:2 * j + 2, :], p, tk))
                return gates_raw[-1]
            feature_major(act_T, xn, DC, "w_in", ev)

        for j in range(2):
            gate_panel(j)

        qm_T, km_T = (by_chunk(place(n, 2048)) for n in ("qm_T", "km_T"))
        dq_T, dk_T = (by_chunk(place(n, 1024)) for n in ("dq_T", "dk_T"))
        att_ready = []
        for src, dst, blocks_, rdy in ((qm, qm_T, [(h * MLA_QK, MLA_QK) for h in range(MLA_H)], t_qm),
                                       (km, km_T, [(h * MLA_QK, MLA_QK) for h in range(MLA_H)], km_ready),
                                       (dq, dq_T, [(h * P, P) for h in range(DIFF_H)], t_dq),
                                       (dk, dk_T, [(h * P, P) for h in range(DIFF_H)], t_dk)):
            att_ready.append(turned(src, lambda i, n, dst=dst: dst[:, i:i + n, :], blocks_, rdy))

        o_mla, o_diff = token_buf("o_mla", 512), token_buf("o_diff", 512)
        items = []

        def causal_item(qT, kT, lo, hi, qb, scale, values, finish, vready):
            n = (qb + 1) * P
            m = mask[:, 2 * P - n:2 * P]

            def scores(bank, after):
                return mm(bank[0][:, 0:n], qT[lo:hi, qb * P:(qb + 1) * P], kT[lo:hi, 0:n], True, True, after, att_ready, signal=True)

            def masked(bank, buf, after):
                return [dve(lambda e: e.scalar_tensor_tensor(buf, bank[0][:, 0:n], scale, m, ALU.mult, ALU.add), after)]
            return dict(n=n, banks=1, scores=scores, masked=masked, values=values, finish=finish, values_ready=vready)

        for h in range(MLA_H):
            for qb in range(NT):
                vals = [kv[:, k, h * 128:(h + 1) * 128] for k in range(qb + 1)]

                def fin(p, inv, after, h=h, qb=qb):
                    return act(lambda e: e.activation(o_mla[:, qb, h * 64:(h + 1) * 64], p[:, NOPE:NOPE + MLA_V], ACT.Copy, scale=inv), after)
                items.append(causal_item(qm_T[:, h, :], km_T[:, h, :], 0, MLA_QK, qb, MLA_QK ** -0.5, vals, fin, kv_up))
        o2_buf = [rope_tmp[:, 0:128], rope_tmp[:, 128:256]]
        o2_free = [None, None]
        o1_tick = {}
        for h in range(DIFF_H):
            for qb in range(NT):
                for comp in range(2):
                    vals = [dv[:, k, h * P:(h + 1) * P] for k in range(qb + 1)]

                    def fin(p, inv, after, h=h, qb=qb, comp=comp):
                        dst = o_diff[:, qb, h * P:(h + 1) * P]
                        if comp == 0:
                            o1_tick[h, qb] = act(lambda e: e.activation(dst, p[:, 0:P], ACT.Copy, scale=inv), after)
                            return o1_tick[h, qb]
                        i = (h * NT + qb) % 2
                        t0 = act(lambda e: e.activation(o2_buf[i], p[:, 0:P], ACT.Copy, scale=inv), after, o2_free[i], t_qm, t_dk)
                        t1 = dve(lambda e: e.scalar_tensor_tensor(dst, o2_buf[i], lam_neg, dst, ALU.mult, ALU.add), t0, lam_ready, o1_tick[h, qb])
                        o2_free[i] = t1
                        return [t0, t1]
                    items.append(causal_item(dq_T[:, h, :], dk_T[:, h, :], comp * 64, comp * 64 + 64, qb, DIFF_D ** -0.5,
                                             vals, fin, dv_ready))
        att_done = attention(items, [xn], [lambda j=j: gate_panel(j) for j in range(2, 8)])

        tot = stat_col(NT * DIFF_H)
        tks = []
        for t in range(NT):
            for h in range(DIFF_H):
                i = t * DIFF_H + h
                v = o_diff[:, t, h * P:(h + 1) * P]
                tks.append(dve(lambda e, v=v, i=i: e.tensor_tensor_reduce(rope_tmp[:, 256:384], v, v, 1.0, 0.0, ALU.mult, ALU.add, tot[:, i:i + 1]),
                               att_done, tks[-1:] if tks else None))
        r, t1 = inverse_rms(tot, DIFF_V, tks)
        t_r = dve(lambda e: e.tensor_scalar(r, r, 1.0 - LAMBDA_INIT, None, ALU.mult), t1)
        odn = []
        for t in range(NT):
            for h in range(DIFF_H):
                i = t * DIFF_H + h
                v = o_diff[:, t, h * P:(h + 1) * P]
                odn.append(dve(lambda e, v=v, i=i: e.scalar_tensor_tensor(v, v, r[:, i:i + 1], subln, ALU.mult, ALU.mult), t_r, (s_sub, 16)))

        oa_T, ob_T = pair("oa", 4), pair("ob", 4)
        blocks4 = [(c * P, P) for c in range(4)]
        oa_ready = turned(o_mla, lambda i, n: pair_view(oa_T, i, n), blocks4, att_done)
        gates_ready = [act(lambda e, c=c: e.activation(gates_T[:, c, :], gates_T[:, c, :], ACT.Sigmoid, bias=col("b_gate", c)), gates_raw, cols_in)
                       for j in range(4) for c in (2 * j, 2 * j + 1, 8 + 2 * j, 9 + 2 * j)]
        ob_ready = turned(o_diff, lambda i, n: pair_view(ob_T, i, n), blocks4, odn)

        merged = by_chunk(place("merged", 2048))
        merged_T = pair("merged", DC)
        merged_ready = []
        for j in range(4):
            m = merged[:, 2 * j:2 * j + 2, :]
            ga, gb = gates_T[:, 2 * j:2 * j + 2, :], gates_T[:, 8 + 2 * j:10 + 2 * j, :]
            ta = feature_major(oa_T, oa_ready, 4, "w_b_mla", lambda p, tk, m=m, ga=ga, j=j: dve(lambda e: e.tensor_tensor(m, p, ga, ALU.mult), tk, gates_ready[4 * j:4 * j + 4]))
            tb = feature_major(ob_T, ob_ready, 4, "w_b_diff", lambda p, tk, gb=gb, j=j: dve(lambda e: e.tensor_tensor(gb, p, gb, ALU.mult), tk, gates_ready[4 * j:4 * j + 4]))
            t1 = dve(lambda e, m=m, gb=gb: e.tensor_tensor(m, m, gb, ALU.add), ta, tb)
            mv = pair_view(merged_T, 2 * j, 2)
            t2 = round_hi(mv.hi, m, t1)
            merged_ready.append([t2, rest_lo(mv.lo, m, mv.hi, t2, t1)])

        x2 = []
        for j in range(2):
            def ev(t, p, tk, j=j):
                v = xr[:, t, 512 * j:512 * (j + 1)]
                return dve(lambda e: e.tensor_tensor(v, p, v, ALU.add), tk, xn)
            x2.append(token_major(merged_T, merged_ready, DC, "w_out", 512, ev))

        hn = normed_T(xr, act_T, col("norm_ffn_g", 0, 8), None, x2, cols_in, tmp_free=att_done)
        ada = {"x": place("ada_x", 6 * D), "c": place("ada_c", 2 * D)}
        ada_tick = {}

        def ada_block(i):
            cb, rb = i // 2, i % 2
            blk = use("ada_w")[0]
            for k in range(4):
                for who, base in (("x", 0), ("c", DC)):
                    if who == "c" and cb >= 4:
                        continue
                    acc = ada[who][:, cb * 512:(cb + 1) * 512]
                    s = cs[:, base + rb * 4 + k:base + rb * 4 + k + 1]
                    w = blk.view[:, k, :]
                    if rb == 0 and k == 0:
                        tk = dve(lambda e, acc=acc, w=w, s=s: e.tensor_scalar(acc, w, s, None, ALU.mult), blk.arrived, t_cs, x2)
                    else:
                        tk = dve(lambda e, acc=acc, w=w, s=s: e.scalar_tensor_tensor(acc, w, s, acc, ALU.mult, ALU.add),
                                 blk.arrived, ada_tick[who, cb])
                    ada_tick[who, cb] = tk
            blk.released = tk

        hid_raw = [by_chunk(place(f"hid{i}", 512, F32, OFF["hid"] + 1024 * i)) for i in range(HID_BUFS)]
        hid_pair = [Pair(by_chunk(place(f"hid_hi{i}", 512, F32R, OFF["hid"] + 1024 * i + 512)),
                         by_chunk(place(f"hid_lo{i}", 512, F32R, OFF["hid"] + 1024 * i))) for i in range(HID_BUFS)]
        hid_free = [None] * HID_BUFS

        def split_hid(i, tk):
            t0 = round_hi(hid_pair[i].hi, hid_raw[i], tk)
            return [t0, rest_lo(hid_pair[i].lo, hid_raw[i], hid_pair[i].hi, t0, tk)]

        acc = [take() for _ in range(4)]
        n_units = FFN // UNIT
        hid_ready = {}
        for u in range(n_units + 1):
            if u < n_units:
                i = u % HID_BUFS
                hr = hid_raw[i]
                t0 = feature_major(act_T, hn, DC, "w_gate", lambda p, tk, hr=hr, i=i: act(lambda e: e.activation(hr, p, ACT.Silu), tk, hid_free[i]))
                t1 = feature_major(act_T, hn, DC, "w_up", lambda p, tk, hr=hr: dve(lambda e: e.tensor_tensor(hr, p, hr, ALU.mult), tk, t0))
                hid_ready[u] = split_hid(i, t1)
            if u >= 1:
                i = (u - 1) % HID_BUFS
                down_tick = hid_free[i] = rows_onto(acc, hid_pair[i], hid_ready[u - 1], "w_down", u == 1, u == n_units)
            if u < n_units:
                for b in ADA_AT[u]:
                    ada_block(b)
        x3 = []
        for half_ in range(2):
            for t in range(NT):
                bank, _ = acc[2 * half_ + t]
                v = xr[:, t, half_ * 512:(half_ + 1) * 512]
                tk = dve(lambda e, v=v, bank=bank: e.tensor_tensor(v, bank[:, :], v, ALU.add), down_tick, hn)
                give(bank, tk)
                x3.append(tk)

        def final_norm(xv, junk, src_ready, gain_blk):
            ticks = []
            for t in range(NT):
                total, t0 = squares(xv[:, t, :], junk[:, t, :], src_ready, (act, dve)[t % 2])
                r, t1 = inverse_rms(total, D, t0)
                ticks.append(dve(lambda e, t=t, r=r: e.scalar_tensor_tensor(xv[:, t, :], xv[:, t, :], r, gain_blk.view[:, 0, :], ALU.mult, ALU.mult),
                                 t1, t0, gain_blk.arrived))
            gain_blk.released = ticks[-1]
            return ticks

        x4 = final_norm(xr, xs, [x3, hn], use("norm_final_g")[0])

        mod = place("mod", 6 * DC)
        mcol = {n: mod[:, i * DC:(i + 1) * DC] for i, n in enumerate(("sh1", "sc1", "csh1", "csc1", "sh2", "sc2"))}
        ada_done = list(ada_tick.values())
        mod_ready = {}
        for name, who, part in (("csh1", "c", 0), ("csc1", "c", 1), ("sh1", "x", 0), ("sc1", "x", 1), ("sh2", "x", 3), ("sc2", "x", 4)):
            tks = []
            for half_ in range(2):
                bank, was = take()
                for j in range(4):
                    o = part * D + (half_ * 4 + j) * P
                    tk = turn(bank[:, j * P:(j + 1) * P], ada[who][:, o:o + P], was, ada_done, signal=(j == 3))
                ev = dve(lambda e, bank=bank, name=name, half_=half_: e.tensor_reduce(
                    mcol[name][:, half_ * 4:half_ * 4 + 4], bank[:, :].rearrange("p (j t) -> p j t", j=4), AXX, ALU.add), tk)
                give(bank, ev)
                tks.append(ev)
            bias = col("ada_b", part * DC, DC)
            tk = dve(lambda e, name=name, bias=bias: e.tensor_tensor(mcol[name], mcol[name], bias, ALU.add), tks)
            if "sc" in name:
                gain = col("norm2_g" if name == "sc2" else "norm1_g", 0, DC)
                tk = dve(lambda e, name=name, gain=gain: e.scalar_tensor_tensor(mcol[name], mcol[name], 1.0, gain, ALU.add, ALU.mult), tk)
            mod_ready[name] = tk
        g1row, g2row = place("g1row", D), place("g2row", D)
        grow_ready = {}
        for part, dst, src in ((2, g1row, "ada_b_g1"), (5, g2row, "ada_b_g2")):
            bias = use(src)[0]
            tks = []
            for half_ in range(2):
                bank, was = take()
                tk = mm(bank[:, :], ones, ada["x"][:, part * D + half_ * 512:part * D + (half_ + 1) * 512], True, True, was, ada_done, signal=True)
                ev = dve(lambda e, bank=bank, dst=dst, bias=bias, half_=half_: e.tensor_tensor(
                    dst[:, half_ * 512:(half_ + 1) * 512], bank[:, :], bias.view[:, 0, half_ * 512:(half_ + 1) * 512], ALU.add), tk, bias.arrived)
                give(bank, ev)
                tks.append(ev)
            bias.released = tks[-1]
            grow_ready[part] = tks
        mods_done = [list(grow_ready.values()), list(mod_ready.values())]

        ctx_T = pair("ctx", DC)
        ctx_blk = use("ctx")[0]
        hc = normed_T(ctx_blk.view, ctx_T, mcol["csc1"], mcol["csh1"], ctx_blk.arrived,
                      [mod_ready["csc1"], mod_ready["csh1"]], tmp_free=x4)
        ctx_blk.released = hc
        hx = normed_T(xr, act_T, mcol["sc1"], mcol["sh1"], x4, [mod_ready["sc1"], mod_ready["sh1"]], tmp_free=hc)

        zx, zc = token_buf("zx", 2048), token_buf("zc", 1024)
        zx_ready, zc_ready = {}, {}

        def both_major(j):
            opened = {("x", t): take() for t in range(NT)}
            if j >= 2:
                opened.update({("c", t): take() for t in range(NT)})
            for b in range(DC // 2):
                blk = use("w_in2")[0]
                ticks = {}
                for part in ("hi", "lo"):
                    for key, (bank, was) in opened.items():
                        who, t = key
                        x, rdy = (act_T, hx) if who == "x" else (ctx_T, hc)
                        for k in range(2):
                            w = part_of(blk, part)[:, k, :]
                            c = 2 * b + k
                            if part == "hi":
                                mm(bank[:, :], x.hi[:, c, t * P:(t + 1) * P], w, b == 0 and k == 0, False, was, rdy, blk.hi_ready)
                                mm(bank[:, :], x.lo[:, c, t * P:(t + 1) * P], w, False, False)
                            else:
                                ticks[key] = mm(bank[:, :], x.hi[:, c, t * P:(t + 1) * P], w, False, c == DC - 1, blk.lo_ready, signal=(k == 1))
                blk.released = ticks[list(opened)[-1]]
            for key, (bank, _) in opened.items():
                who, t = key
                dst = zx[:, t, 512 * j:512 * j + 512] if who == "x" else zc[:, t, 512 * (j - 2):512 * (j - 1)]
                ev = copy(dst, bank[:, :], ticks[key], down_tick)
                give(bank, ev)
                (zx_ready if who == "x" else zc_ready).setdefault(j, []).append(ev)

        part_of = lambda blk, part: blk.hi if part == "hi" else blk.lo
        q_T, k_T, kc_T = (by_chunk(place(n, 1024)) for n in ("q_T", "k_T", "kc_T"))
        for j in (1, 2, 3):
            both_major(j)

        na_ready = []
        for src, c0, dst, rdy in ((zx, 512, q_T, zx_ready[1]), (zx, 1024, k_T, zx_ready[2]), (zc, 0, kc_T, zc_ready[2])):
            na_ready.append(turned(src, lambda i, n, dst=dst: dst[:, i:i + n, :], [(c0 + c * P, P) for c in range(4)], rdy))

        attn = token_buf("attn", 512)
        items = []
        scale = NA_D ** -0.5
        bias_blk = {}
        for h in range(NA_H):
            for qb in range(NT):
                lo = (h % 2) * 64

                def scores(bank, after, h=h, qb=qb, lo=lo):
                    if h % 4 == 0 and qb == 0:
                        bias_blk[h // 4] = use("na_bias")[0]
                    q = q_T[lo:lo + 64, h // 2, qb * P:(qb + 1) * P]
                    mm(bank[0][:, 0:T], q, k_T[lo:lo + 64, h // 2, :], True, True, after, na_ready)
                    return mm(bank[1][:, 0:T], q, kc_T[lo:lo + 64, h // 2, :], True, True, signal=True)

                def masked(bank, buf, after, h=h, qb=qb):
                    hb = bias_blk[h // 4]
                    o = ((h % 4) * NT + qb) * T
                    t0 = dve(lambda e: e.scalar_tensor_tensor(buf[:, 0:T], bank[0][:, 0:T], scale, hb.view[:, 0, o:o + T], ALU.mult, ALU.add), after, hb.arrived)
                    hb.released = t0
                    return [t0, act(lambda e: e.activation(buf[:, T:2 * T], bank[1][:, 0:T], ACT.Copy, scale=scale), after)]

                def fin(p, inv, after, h=h, qb=qb, lo=lo):
                    return act(lambda e: e.activation(attn[:, qb, h * 64:(h + 1) * 64], p[:, lo:lo + 64], ACT.Copy, scale=inv), after)
                o = h // 2 * P
                vals = [zx[:, k, 1536 + o:1536 + o + P] for k in range(NT)] + [zc[:, k, 512 + o:512 + o + P] for k in range(NT)]
                items.append(dict(n=2 * T, banks=2, scores=scores, masked=masked, values=vals, finish=fin, values_ready=[zx_ready[3], zc_ready[3]]))
        def pooled_columns():
            both_major(0)

        attn_done = attention(items, [hx], [pooled_columns])
        mix_T = pair("mix", DC)
        mix_ready = []
        mix_ready.append(turned(attn, lambda i, n: pair_view(mix_T, 4 + i, n), blocks4, attn_done, mods_done))

        band_blk, pw_blk = use("band")[0], use("pool_w")[0]
        band = band_blk.view[:, 0, :].rearrange("p (k g t) -> p k g t", k=NT, g=4)
        pooled_T = by_chunk(place("pooled_T", 1024))
        for g in range(4):
            bank, was = take()
            for k in range(NT):
                tk = mm(bank[:, 0:T], zx[:, k, g * P:(g + 1) * P], band[:, k, g, :], k == 0, k == NT - 1,
                        was, zx_ready[0], band_blk.arrived, signal=(k == NT - 1))
            band_blk.released = tk
            ev = copy(pooled_T[:, g, :], bank[:, 0:T], tk)
            give(bank, ev)
            bank, was = take()
            tk = mm(bank[:, 0:T], pw_blk.view[:, 0, g * P:(g + 1) * P], pooled_T[:, g, :], True, True, was, ev, pw_blk.arrived, signal=True)
            pw_blk.released = tk
            t0 = act(lambda e, g=g, bank=bank: e.activation(mix_T.hi[:, g, :], bank[:, 0:T], ACT.Copy, scale=col("pool_scale", g)), tk, mods_done)
            ev = dve(lambda e, g=g, bank=bank: e.scalar_tensor_tensor(mix_T.lo[:, g, :], bank[:, 0:T], col("pool_scale", g), mix_T.hi[:, g, :].bitcast(F32),
                                                                      ALU.mult, ALU.subtract), t0, tk)
            give(bank, ev)
            mix_ready.append([t0, ev])

        x5 = []
        gated = place("gated", 1024)
        for j in range(2):
            def ev(t, p, tk, j=j):
                c0 = 512 * j
                tmp_ = gated[:, t * 512:(t + 1) * 512]
                t0 = dve(lambda e: e.tensor_tensor(tmp_, p, g1row[:, c0:c0 + 512], ALU.mult), tk, grow_ready[2], attn_done, x5)
                v = xr[:, t, c0:c0 + 512]
                x5.append(pool(lambda e: e.tensor_tensor(v, tmp_, v, ALU.add), t0, hx))
                return t0
            token_major(mix_T, mix_ready, DC, "w_out2", 512, ev)
        sp(lambda e: e.dma_start(parked_x.rearrange("(t p) d -> p t d", p=P), xr).then_inc(s_park, 16), x5, signal=0)
        sp(lambda e: e.dma_start(parked_g2, g2row).then_inc(s_park, 16), grow_ready[5], signal=0)
        parked = (s_park, 32)
        dram_ready["parked_x"] = dram_ready["parked_g2"] = parked

        h2 = normed_T(xr, act_T, mcol["sc2"], mcol["sh2"], x5, [mod_ready["sc2"], mod_ready["sh2"]], tmp_free=attn_done)

        pq_T = by_chunk(place("pq_T", 4096))
        pq_ready = []
        for j in range(8):
            def ev(p, tk, j=j):
                pq_ready.append(copy(pq_T[:, 2 * j:2 * j + 2, :], p, tk, attn_done))
                return pq_ready[-1]
            feature_major(act_T, h2, DC, "peer_wq", ev)

        keys = use("keys_T")[0]
        s_all = place("s", 4096).rearrange("p (t g n) -> p t g n", t=NT, g=16)
        s_ready = [[], []]
        for t in range(NT):
            for g4 in range(4):
                bank, was = take()
                for j in range(4):
                    g = 4 * g4 + j
                    tk = mm(bank[:, j * P:(j + 1) * P], pq_T[:, g, t * P:(t + 1) * P], keys.view[:, 0, g * P:(g + 1) * P], True, True,
                            was, pq_ready, keys.arrived, signal=(j == 3))
                ev = act(lambda e, t=t, g4=g4, bank=bank: e.activation(s_all[:, t, 4 * g4:4 * g4 + 4, :],
                                                                        bank[:, :].rearrange("p (j n) -> p j n", j=4), ACT.Copy), tk, x5)
                give(bank, ev)
                s_ready[t].append(ev)
        keys.released = tk

        s_work = place("s_work", 2048).rearrange("p (g n) -> p g n", g=16)
        v12w, i12w = place("v12", 256), place("i12", 256, U32)
        v12, i12 = (w.rearrange("p (g k) -> p g k", g=16) for w in (v12w, i12w))
        v4, i4 = (w.rearrange("p (h w k) -> p h w k", h=PE_H, w=2) for w in (v12w, i12w))
        i12f = place("i12f", 256).rearrange("p (h w k) -> p h w k", h=PE_H, w=2)
        cand = place("cand", 2048).rearrange("p (h k) -> p h k", h=PE_H)
        cand_work = place("cand_work", 2048).rearrange("p (h k) -> p h k", h=PE_H)
        eq = place("eq", 2048).rearrange("p (h k a) -> p h k a", h=PE_H, a=TOPK)
        tv = place("tv", 3 * 128)
        topv, abf = tv[:, 0:128].rearrange("p (h k) -> p h k", h=PE_H), tv[:, 128:384]
        topi, ab = place("topi", 128, U32), place("ab", 2 * 128, U32)
        pick = place("pick", 384).rearrange("p (w n) -> p w n", w=3)
        gs = stat_col(2 * PE_H)
        best = stat_col(PE_H)

        def top16(values, work, vals, idx, after):
            n = values.shape[1]
            for g in range(n):
                t0 = dve(lambda e, g=g: e.max(vals[:, g, 0:8], values[:, g, :]), after)
            for g in range(n):
                t1 = dve(lambda e, g=g: e.match_replace(work[:, g, :], vals[:, g, 0:8], values[:, g, :], LOWEST), t0)
            for g in range(n):
                dve(lambda e, g=g: e.max_index(idx[:, g, 0:8], vals[:, g, 0:8], values[:, g, :]), t0)
            for g in range(n):
                t2 = dve(lambda e, g=g: e.max(vals[:, g, 8:16], work[:, g, :]), t1)
            for g in range(n):
                t3 = dve(lambda e, g=g: e.max_index(idx[:, g, 8:16], vals[:, g, 8:16], work[:, g, :]), t2)
            return t3

        picks_ready = []
        last = None
        iota16 = iota[:, 0:TOPK]
        for t in range(NT):
            t0 = top16(s_all[:, t], s_work, v12, i12, [s_ready[t], last, x5])
            t1 = dve(lambda e: e.tensor_copy(i12f, i4), t0)
            for h in range(PE_H):
                tk = dve(lambda e, h=h: e.tensor_tensor(cand[:, h, :].rearrange("p (a b) -> p a b", a=TOPK),
                                                        v4[:, h, 0, :].unsqueeze(2).to_broadcast([P, TOPK, TOPK]),
                                                        v4[:, h, 1, :].unsqueeze(1).to_broadcast([P, TOPK, TOPK]), ALU.add), t0)
            t2 = top16(cand, cand_work, topv, topi.rearrange("p (h k) -> p h k", h=PE_H), tk)
            dve(lambda e: e.tensor_scalar(ab[:, 0:128], topi, 4, None, ALU.logical_shift_right), t2)
            t3 = dve(lambda e: e.tensor_scalar(ab[:, 128:256], topi, 15, None, ALU.bitwise_and), t2)
            t4 = dve(lambda e: e.tensor_copy(abf, ab), t3, t1)
            eq_flat = eq.rearrange("p h k a -> p (h k) a")
            for w in range(2):
                e0 = dve(lambda e, w=w: e.tensor_tensor(eq_flat, abf[:, w * 128:(w + 1) * 128].unsqueeze(2).to_broadcast([P, 128, TOPK]),
                                                        iota16.unsqueeze(1).to_broadcast([P, 128, TOPK]), ALU.is_equal), t4, last)
                e1 = dve(lambda e, w=w: e.tensor_tensor(eq, eq, i12f[:, :, w, :].unsqueeze(2).to_broadcast([P, PE_H, TOPK, TOPK]), ALU.mult), e0)
                t4 = dve(lambda e, w=w: e.tensor_reduce(pick[:, w, :], eq_flat, AXX, ALU.add), e1)
            u0 = dve(lambda e: e.tensor_copy(best, topv[:, :, 0]), t2, last)
            u1 = dve(lambda e: e.tensor_tensor(topv, topv, best.unsqueeze(2).to_broadcast([P, PE_H, TOPK]), ALU.subtract), u0)
            u2 = act(lambda e: e.activation(topv, topv, ACT.Exp), u1)
            u3 = dve(lambda e: e.tensor_reduce(gs[:, 0:PE_H], topv, AXX, ALU.add), u2)
            u4 = dve(lambda e: e.reciprocal(gs[:, PE_H:], gs[:, 0:PE_H]), u3)
            u5 = dve(lambda e: e.tensor_tensor(pick[:, 2, :].rearrange("p (h k) -> p h k", h=PE_H), topv,
                                               gs[:, PE_H:].unsqueeze(2).to_broadcast([P, PE_H, TOPK]), ALU.mult), u4)
            bank, was = take()
            for w in range(3):
                tk = turn(bank[:, w * P:(w + 1) * P], pick[:, w, :], was, t4, u5, signal=(w == 2))
            last = dve(lambda e, t=t, bank=bank: e.tensor_copy(pick_T.rearrange("p (w t) -> p w t", w=3)[:, :, t * P:(t + 1) * P],
                                                               bank[:, 0:3 * P].rearrange("p (w t) -> p w t", w=3)), tk)
            give(bank, last)
            picks_ready.append(last)

        Gw = place("G", G_WORDS)
        Gv = by_chunk(Gw)
        pT = pick_T.rearrange("p (w t) -> p w t", w=3)
        TG = 4
        hot_free = [picks_ready, picks_ready]
        hot = place("hot", 2048, F32, OFF["hid"])
        hot_a = [hot[:, i * 512:(i + 1) * 512].rearrange("p (t n) -> p t n", n=P) for i in range(2)]
        hot_b = [hot[:, 1024 + i * 512:1024 + (i + 1) * 512].rearrange("p (t n) -> p t n", n=P) for i in range(2)]
        g_ready = []
        for q in range(T // TG):
            A_, B_ = hot_a[q % 2], hot_b[q % 2]
            bank, was = take()
            for j in range(TG):
                tok = q * TG + j
                dve(lambda e, j=j, tok=tok, A_=A_: e.tensor_scalar(A_[:, j, :], iota, pT[:, 0, tok:tok + 1], None, ALU.is_equal), hot_free[q % 2])
                tk = dve(lambda e, j=j, tok=tok, B_=B_: e.tensor_scalar(B_[:, j, :], iota, pT[:, 1, tok:tok + 1], pT[:, 2, tok:tok + 1], ALU.is_equal, ALU.mult))
            for j in range(TG):
                m = mm(bank[:, j * P:(j + 1) * P], B_[:, j, :], A_[:, j, :], True, True, was, tk, signal=(j == TG - 1))
            hot_free[q % 2] = m
            src = bank[:, :].rearrange("p (t i) -> p i t", t=TG)
            dst = Gv[:, :, q * TG:(q + 1) * TG]
            ev = act(lambda e, src=src, dst=dst: e.activation(dst, src, ACT.Copy), m, picks_ready, parked, h2)
            give(bank, ev)
            g_ready.append(ev)

        acc = [take() for _ in range(4)]
        hid_free = [m] * HID_BUFS
        for u in range(N_UNITS + V_LAG):
            if u < N_UNITS:
                i = u % HID_BUFS
                hr = hid_raw[i]
                t0 = feature_major(act_T, h2, DC, "peer_uT", lambda p, tk, hr=hr, i=i: act(lambda e: e.activation(hr, p, ACT.Gelu), tk, hid_free[i]))
                t1 = dve(lambda e, hr=hr, u=u: e.tensor_tensor(hr, hr, Gv[:, 2 * u:2 * u + 2, :], ALU.mult), t0, g_ready)
                hid_ready[u] = split_hid(i, t1)
            if u >= V_LAG:
                v = u - V_LAG
                fin_tick = hid_free[v % HID_BUFS] = rows_onto(acc, hid_pair[v % HID_BUFS], hid_ready[v], "peer_v", v == 0, v == N_UNITS - 1)

        x_blk, g2_blk, fg_blk = use("parked_x")[0], use("parked_g2")[0], use("final_g")[0]
        x6 = []
        for half_ in range(2):
            for t in range(NT):
                bank, _ = acc[2 * half_ + t]
                tmp_ = Gw[:, (2 * half_ + t) * 512:(2 * half_ + t + 1) * 512]
                t0 = dve(lambda e, bank=bank, tmp_=tmp_, half_=half_: e.tensor_tensor(tmp_, bank[:, :], g2_blk.view[:, 0, half_ * 512:(half_ + 1) * 512], ALU.mult),
                         fin_tick, g2_blk.arrived, t1)
                give(bank, t0)
                v = x_blk.view[:, t, half_ * 512:(half_ + 1) * 512]
                x6.append(dve(lambda e, v=v, tmp_=tmp_: e.tensor_tensor(v, v, tmp_, ALU.add), t0, x_blk.arrived))
        done = final_norm(x_blk.view, Gw[:, 2048:4096].rearrange("p (t d) -> p t d", t=NT), x6, fg_blk)
        assert taken[0] == len(plan)
        for t in range(NT):
            act(lambda e, t=t: e.dma_start(out.rearrange("(t p) d -> p t d", p=P)[:, t, :], x_blk.view[:, t, :]).then_inc(s_out, 16), done[t], signal=0)
        act(lambda e: e.wait_ge(s_out, 16 * NT), signal=0)

        with nc.Block() as block:
            @block.sync
            def _(eng):
                sp.play(eng)

            @block.scalar
            def _(eng):
                act.play(eng)

            @block.vector
            def _(eng):
                dve.play(eng)

            @block.gpsimd
            def _(eng):
                pool.play(eng)

            @block.tensor
            def _(eng):
                pe.play(eng)


def constants():
    c = np.zeros((P, N_CONST), np.float32)
    c[:, K_IDENT:K_IDENT + P] = np.eye(P)
    c[:, K_ONES:K_ONES + P] = 1
    c[:, K_IOTA:K_IOTA + P] = np.arange(P)
    c[:, K_MASK + P:K_MASK + 2 * P] = np.where(np.arange(P)[None, :] <= np.arange(P)[:, None], 0, MASKED)
    for o, half, rot in ((0, HALF_M, ROPE), (HALF_M, HALF_D, DIFF_ROT)):
        c[:, K_FREQ + o:K_FREQ + o + half] = np.exp(np.float32(-math.log(THETA)) * np.arange(half, dtype=np.float32) * np.float32(2.0 / rot))
    return c


def pooling_band():
    t = np.arange(T)
    band = np.zeros((T, 4, T), np.float64)
    for g, w in enumerate(POOL_WINDOWS):
        lo, hi = np.clip(t - w // 2, 0, T), np.clip(t + w // 2, 0, T)
        inside = (t[:, None] >= lo[None, :]) & (t[:, None] < hi[None, :])
        band[:, g, :] = inside / (hi - lo)[None, :] - np.eye(T)
    return np.ascontiguousarray(band.astype(np.float32).reshape(NT, P, 4, T).transpose(1, 0, 2, 3).reshape(P, -1))


def window_bias(rpb):
    row, colm = np.arange(T) // GRID_W, np.arange(T) % GRID_W
    kh = min(NA_KH_MAX, ROWS)
    r0 = np.clip(row - kh // 2, 0, ROWS - kh)
    c0 = np.clip(colm - NA_KW // 2, 0, GRID_W - NA_KW)
    ok = ((row[None, :] >= r0[:, None]) & (row[None, :] < (r0 + kh)[:, None])
          & (colm[None, :] >= c0[:, None]) & (colm[None, :] < (c0 + NA_KW)[:, None]))
    ro = np.clip(row[None, :] - row[:, None] + NA_KH_MAX - 1, 0, 2 * NA_KH_MAX - 2)
    co = np.clip(colm[None, :] - colm[:, None] + NA_KW - 1, 0, 2 * NA_KW - 2)
    b = rpb[:, ro, co]
    b[:, ~ok] = MASKED
    return np.ascontiguousarray(b.reshape(NA_H, NT, P, T).transpose(2, 0, 1, 3).reshape(P, -1))


def kernel(**inputs):
    import concourse.bacc as bacc
    from concourse.bass_utils import run_bass_kernel_spmd

    v = {k: np.asarray(x) for k, x in inputs.items()}
    by_col = lambda x: x.reshape(-1, P).T
    arrays = {
        "x": v["x"][0],
        "pos": v["positions"].reshape(NT, P).T,
        "const": constants(),
        "cols": np.concatenate([by_col(v[n]) for n in (
            "norm_mix_g", "mla_q_norm_g", "mla_kv_norm_g", "b_gate", "norm_ffn_g", "c_2", "c_ctx_2", "norm1_g_2",
            "norm2_g_2", "pool_scale_2", "ada_b_2")], axis=1),
        "lam": np.concatenate([v[n].reshape(-1) for n in ("diff_lambda_q1", "diff_lambda_k1", "diff_lambda_q2", "diff_lambda_k2")]),
        "subln": v["diff_subln_g"][0],
        "w_in": v["w_in"][0], "w_uq": v["mla_w_uq"][0], "w_ukv": v["mla_w_ukv"][0],
        "w_b_mla": v["w_branch_mla"][0], "w_b_diff": v["w_branch_diff"][0], "w_out": v["w_out"][0],
        "w_gate": v["w_ffn_gate"][0], "w_up": v["w_ffn_up"][0], "w_down": v["w_ffn_down"][0],
        "norm_final_g": v["norm_final_g"],
        "ctx": v["ctx_2"][0], "ada_w": v["ada_w_2"][0],
        "ada_b_g1": v["ada_b_2"][0, 2 * D:3 * D], "ada_b_g2": v["ada_b_2"][0, 5 * D:6 * D],
        "w_in2": v["w_in_2"][0], "na_bias": window_bias(v["na_rpb_2"][0].copy()), "band": pooling_band(),
        "pool_w": v["pool_w_2"][0].transpose(1, 0, 2).reshape(P, -1), "w_out2": v["w_out_2"][0],
        "peer_wq": v["peer_wq_2"][0], "keys_T": v["peer_keys_2"][0].transpose(3, 0, 1, 2).reshape(P, -1),
        "peer_uT": v["peer_u_2"][0].T, "peer_v": v["peer_v_2"][0], "final_g": v["final_g_2"],
    }
    arrays = {k: np.ascontiguousarray(x) for k, x in arrays.items()}
    nc = bacc.Bacc("TRN2", target_bir_lowering=False, num_devices=1)
    aps = {k: nc.dram_tensor(k, x.shape, mybir.dt.from_np(x.dtype), kind="ExternalInput").ap() for k, x in arrays.items()}
    out = nc.dram_tensor("y", (T, D), F32, kind="ExternalOutput").ap()
    parked_x = nc.dram_tensor("parked_x", (T, D), F32, kind="Internal").ap()
    parked_g2 = nc.dram_tensor("parked_g2", (P, D), F32, kind="Internal").ap()
    build(nc, aps, out, parked_x, parked_g2)
    r = run_bass_kernel_spmd(nc, [arrays], core_ids=[0])
    return r.results[0]["y"].reshape(1, T, D)
```

```python
import math

import numpy as np

import concourse.bass as bass
from concourse import mybir
from concourse.alu_op_type import AluOpType as ALU

F32 = mybir.dt.float32
F32R = mybir.dt.float32r
U32 = mybir.dt.uint32
I32 = mybir.dt.int32
ACT = mybir.ActivationFunctionType
AXX = mybir.AxisListType.X

P = 128
D = 1024
T = 256
NT = T // P
DC = D // P
EPS = 1e-6
THETA = 500000.0
MLA_H, NOPE, ROPE, MLA_V, Q_RANK, KV_RANK = 8, 64, 32, 64, 384, 256
MLA_QK = NOPE + ROPE
DIFF_H, DIFF_D, DIFF_ROT = 4, 64, 16
DIFF_V = 2 * DIFF_D
LAT = Q_RANK + KV_RANK + ROPE
FFN = 2816
LAMBDA_INIT = 0.8 - 0.6 * math.exp(-0.3 * 0)
NA_H, NA_D, GRID_W, NA_KW, NA_KH_MAX = 8, 64, 64, 16, 8
ROWS = T // GRID_W
POOL_WINDOWS = (2, 4, 8, 16)
D_POOL = 512
PE_H, NKEYS, TOPK = 8, 128, 16
MASKED = -1e30
LOWEST = -3.4e38

COLS = {}
_at = 0
for _name, _n in (("norm_mix_g", 8), ("q_norm_g", 3), ("kv_norm_g", 2), ("b_gate", 16), ("norm_ffn_g", 8),
                  ("c", 8), ("c_ctx", 8), ("norm1_g", 8), ("norm2_g", 8), ("pool_scale", 4), ("ada_b", 48)):
    COLS[_name] = (_at, _n)
    _at += _n
N_COLS = _at
K_IDENT, K_ONES, K_IOTA, K_MASK, K_FREQ = 0, 128, 256, 384, 640
HALF_M, HALF_D = ROPE // 2, DIFF_ROT // 2
N_FREQ = HALF_M + HALF_D
N_CONST = K_FREQ + N_FREQ

RING_SLOTS = 5
BLOCK = 1024
SLOT = 2 * BLOCK
POOL_SHARE = dict(peer_uT_early=1, w_in2_ctx=1, w_gate=2, w_up=2, w_down=2, peer_wq=1)
AHEAD = 3
UNIT = 256
HID_BUFS = 3
ADA_BUFS, ADA_LATE_BUFS = 5, 2
SELECT_ORDER = "HDHHDHDHHDHDHEDEDEEDEDEE"
CTX_UNIT = 8

G_WORDS = NKEYS * T
SBUF_BASE = 16512
OFF = dict(
    gates_T=0, dq=4096, dk=5120, dv=6144, lat=7168, qm=8512, kv=10048, km=12096, lat_hi=13632, lat_lo=14912,
    qm_T=16192, km_T=18240, dq_T=20288, dk_T=21312, o_mla=22336, o_diff=23360,
    xres=24384, xs=26432, score_bufs=26432, prob_T=28480, rope_tmp=29504, rope=30016, small=30304, posi=30688, turns=30696,
    oa_hi=7168, oa_lo=8192, ob_hi=9216, ob_lo=10240, merged=16192, merged_hi=12096, merged_lo=14144,
    ada_x=0, ada_c=6144, ada_bufs=(18432, 20480, 12288, 14336, 16384, 8192, 10240),
    ctx_hi=8192, ctx_lo=10240, zx=12288, zc=16384, q_T=18432, k_T=19456, kc_T=20480, attn=21504, pooled_T=22528,
    mix_hi=0, mix_lo=2048, g1row=31744, g2row=30720, gated=18432, band=6144, pool_w=23552, shifted=28480,
    s=0, cand=4096, pq_T=8192, eq=12288, s_work=14336, cand_work=14848, v12=18432, i12=18944, i12f=19456, abf=19968, keys_T=20480,
    topv=15360, topi=15616, ab=15872, pick=16384, weight=16896,
    early=(22528, 23040, 23552),
    G=0, act_hi=32768, act_lo=34816, ring=36864, hid=36864 + 5 * 2048, const=50176, cols=50840, mod=50968, stat=51024, pick_T=51520,
)


class Lane:

    def __init__(self, name, sem):
        self.name, self.sem, self.count, self.steps = name, sem, 0, []

    def __call__(self, issue, *after, signal=True):
        self.steps.append((issue, frozen(after), signal))
        self.count += signal
        return (self.sem, self.count) if signal else None

    def play(self, eng):
        passed = {}
        for issue, after, signal in self.steps:
            for tick in flat(after):
                sem, value = tick
                if passed.get(id(sem), 0) < value:
                    eng.wait_ge(sem, value)
                    passed[id(sem)] = value
            ins = issue(eng)
            if signal is True:
                ins.then_inc(self.sem, 1)


def frozen(ticks):
    return tuple(frozen(t) for t in ticks) if isinstance(ticks, (list, tuple)) else ticks


def flat(ticks):
    for t in ticks:
        if t is None:
            continue
        if isinstance(t, Block):
            yield from flat((t.released,))
        elif isinstance(t, tuple) and len(t) == 2 and not isinstance(t[1], (tuple, list)) and t[1] is not None:
            yield t
        else:
            yield from flat(t)


class Block:

    def __init__(self, name):
        self.name, self.released = name, None


class Pair:

    def __init__(self, hi, lo):
        self.hi, self.lo = hi, lo


def build(nc, a, out, parked_x, parked_g2, parked_units):
    from contextlib import ExitStack
    ctx = ExitStack()
    with ctx:
        sem = lambda name: ctx.enter_context(nc.semaphore(name))

        def place(name, words, dt=F32, offset=None):
            o = OFF[name] if offset is None else offset
            return nc.alloc_sbuf_tensor_at("sb_" + name, [P, words], dt, offset=SBUF_BASE + 4 * o)[:, :]

        banks = [ctx.enter_context(nc.psum_tensor(f"bank{i}", [P, 512], F32)) for i in range(8)]
        const, cols, stat, pick_T = place("const", N_CONST), place("cols", N_COLS), place("stat", 490), place("pick_T", 3 * T)
        xres, posi = place("xres", NT * D), place("posi", NT, I32)

        pe, act, dve, pool, sp = (Lane(n, sem(f"{n}_done")) for n in ("pe", "act", "dve", "pool", "sp"))
        slot_sem = [sem(f"slot{i}_arrived") for i in range(RING_SLOTS)]
        s_ada = [sem(f"ada{i}_arrived") for i in range(ADA_BUFS + ADA_LATE_BUFS)]
        s_early = [sem(f"early{i}_stored") for i in range(3)]
        s_hid = [sem(f"hid{i}_arrived") for i in range(HID_BUFS)]
        s_x = [sem(f"x{t}_arrived") for t in range(NT)]
        s_const, s_cols, s_pos, s_lam, s_sub, s_park, s_keys, s_band, s_pool_w, s_out = (
            sem(n) for n in ("const_arrived", "cols_arrived", "pos_arrived", "lam_arrived",
                             "subln_arrived", "parked", "keys_arrived", "band_arrived", "pool_w_arrived", "out_stored"))

        plan = []

        def by_chunks(w, r0, kc, c0, n):
            return w[r0:r0 + kc * P, c0:c0 + n].rearrange("(c p) n -> p c n", p=P)

        def plan_panel(name, rows, c0, n):
            step = 2 if n > UNIT else 4
            for k0 in range(0, rows // P, step):
                kc = min(step, rows // P - k0)
                plan.append((name, by_chunks(a[name.removesuffix("_ctx").removesuffix("_early")], k0 * P, kc, c0, n), kc, n, True))

        def plan_rows(name, r0):
            for c0 in (0, 512):
                plan.append((name, by_chunks(a[name], r0, 2, c0, 512), 2, 512, True))

        def plan_plain(name, src, kc, n):
            plan.append((name, src, kc, n, False))

        for c0 in (0, LAT // 2):
            plan_panel("w_in", D, c0, LAT // 2)
        for j in range(3):
            plan_panel("w_in", D, LAT + 512 * j, 512)
        for c0 in (0, 384):
            plan_panel("w_uq", Q_RANK, c0, 384)
        for c0 in (0, 512):
            plan_panel("w_ukv", KV_RANK, c0, 512)
        for j in range(8):
            plan_panel("w_in", D, LAT + 1536 + UNIT * j, UNIT)
        for j in range(4):
            plan_panel("w_b_mla", 512, UNIT * j, UNIT)
        for j in range(4):
            plan_panel("w_b_diff", 512, UNIT * j, UNIT)
        for j in range(2):
            plan_panel("w_out", D, 512 * j, 512)
        for u in range(FFN // UNIT):
            plan_panel("w_gate", D, UNIT * u, UNIT)
            plan_panel("w_up", D, UNIT * u, UNIT)
            if u:
                plan_rows("w_down", UNIT * (u - 1))
            if u == CTX_UNIT:
                plan_plain("ctx", a["ctx"].rearrange("(t p) d -> p t d", p=P), 2, D)
        plan_rows("w_down", FFN - UNIT)
        for j in (2, 3):
            plan_panel("w_in2_ctx", D, 512 * j, 512)
        plan.insert(len(plan) - 5, ("norm_final_g", a["norm_final_g"].partition_broadcast(P), 1, D, False))
        for j in (1, 2, 3):
            plan_panel("w_in2", D, 512 * j, 512)
        def plan_bias(q):
            plan_plain("na_bias", a["na_bias"][:, q * BLOCK:(q + 1) * BLOCK], 1, BLOCK)

        plan_bias(0)
        plan_panel("w_in2", D, 0, 512)
        plan.insert(len(plan) - 1, ("na_bias", a["na_bias"][:, BLOCK:2 * BLOCK], 1, BLOCK, False))
        plan_bias(2)
        plan_bias(3)
        for name in ("ada_b_g1", "ada_b_g2"):
            plan_plain(name, a[name].partition_broadcast(P), 1, D)
        for j in range(2):
            plan_panel("w_out2", D, 512 * j, 512)
        for j in range(8):
            plan_panel("peer_wq", D, UNIT * j, UNIT)
        N_UNITS = NKEYS * NKEYS // UNIT
        EARLY = SELECT_ORDER.count("E")
        V_LAG = HID_BUFS - 1
        order = [v for e in range(EARLY) for v in (EARLY + e, e)] + list(range(2 * EARLY, N_UNITS))
        for e in range(EARLY):
            plan_panel("peer_uT_early", D, UNIT * e, UNIT)
        for i in range(N_UNITS + V_LAG):
            if i < N_UNITS and order[i] >= EARLY:
                plan_panel("peer_uT", D, UNIT * order[i], UNIT)
            if i >= V_LAG:
                plan_rows("peer_v", UNIT * order[i - V_LAG])
        plan_plain("parked_x", parked_x.rearrange("(t p) d -> p t d", p=P), 2, D)
        plan_plain("parked_g2", parked_g2, 1, D)
        plan_plain("final_g", a["final_g"].partition_broadcast(P), 1, D)

        ring = [dict(full=place(f"slot{i}", SLOT, F32, OFF["ring"] + i * SLOT),
                     raw=place(f"raw{i}", BLOCK, F32, OFF["ring"] + i * SLOT),
                     lo=place(f"lo{i}", BLOCK, F32R, OFF["ring"] + i * SLOT),
                     hi=place(f"hi{i}", BLOCK, F32R, OFF["ring"] + i * SLOT + BLOCK)) for i in range(RING_SLOTS)]
        issued, taken, n_split = [], [0], [0]
        dram_ready = {}

        def issue(i):
            name, src, kc, n, split = plan[i]
            s = i % RING_SLOTS
            cut = lambda t: t[:, 0:kc * n].rearrange("p (c n) -> p c n", c=kc)
            blk = Block(name)
            before = issued[i - RING_SLOTS] if i >= RING_SLOTS else None
            dst = ring[s]["raw" if split else "full"]
            view = cut(dst) if len(src.shape) == 3 else dst[:, 0:n]
            blk.arrived = (slot_sem[s], 16 * (i // RING_SLOTS + 1))
            sp(lambda e: e.dma_start(view, src).then_inc(slot_sem[s], 16), before, dram_ready.get(name), signal=0)
            if split:
                w = kc * n
                raw, hi, lo = dst[:, 0:w], ring[s]["hi"][:, 0:w], ring[s]["lo"][:, 0:w]
                blk.hi_ready = act(lambda e: e.activation(hi, raw, ACT.Copy), blk.arrived)
                n_split[0] += 1
                lane = pool if n_split[0] % POOL_SHARE.get(name, 4) == 0 else dve
                blk.lo_ready = lane(lambda e: e.tensor_tensor(lo, raw, hi.bitcast(F32), ALU.subtract), blk.hi_ready, blk.arrived)
                blk.hi, blk.lo = cut(ring[s]["hi"]), cut(ring[s]["lo"])
            else:
                blk.view = cut(dst)
            issued.append(blk)

        def use(name, count=1):
            out_ = []
            for _ in range(count):
                i = taken[0]
                taken[0] += 1
                while len(issued) <= min(i + AHEAD, len(plan) - 1):
                    n = len(issued)
                    if n > i and n >= RING_SLOTS and issued[n - RING_SLOTS].released is None:
                        break
                    issue(n)
                assert issued[i].name == name, (issued[i].name, name)
                out_.append(issued[i])
            return out_

        free = [(b, None) for b in banks]

        def take():
            return free.pop(0)

        def give(b, tick):
            free.append((b, tick))

        n_stat = [0]

        def stat_col(n=1):
            o = n_stat[0]
            n_stat[0] += n
            assert n_stat[0] <= 490
            return stat[:, o:o + n]

        def col(name, c, n=1):
            o, m = COLS[name]
            assert c + n <= m
            return cols[:, o + c:o + c + n]

        ident = const[:, K_IDENT:K_IDENT + P]
        ones = const[:, K_ONES:K_ONES + P]
        iota = const[:, K_IOTA:K_IOTA + P]
        mask = const[:, K_MASK:K_MASK + 2 * P]
        freq = const[:, K_FREQ:K_FREQ + N_FREQ]

        def by_chunk(t, w=T):
            return t.rearrange("p (c t) -> p c t", t=w)

        def token_buf(name, width):
            return place(name, NT * width).rearrange("p (t d) -> p t d", t=NT)

        def mm(dst, lhsT, rhs, start, stop, *after, signal=False, shared=False):
            return pe(lambda e: e.matmul(dst, lhsT, rhs, start=start, stop=stop, skip_group_check=shared), *after, signal=signal)

        def turn(dst, src, *after, signal=False):
            n = src.shape[0]
            return pe(lambda e: e.transpose(dst, src, ident[0:n, 0:n]), *after, signal=signal)

        def round_hi(hi, src, *after):
            return act(lambda e: e.activation(hi, src, ACT.Copy), *after)

        def rest_lo(lo, src, hi, *after):
            return dve(lambda e: e.tensor_tensor(lo, src, hi.bitcast(F32), ALU.subtract), *after)

        xr = xres.rearrange("p (t d) -> p t d", t=NT)
        for t, lane in enumerate((sp, act)):
            lane(lambda e, t=t: e.dma_start(xr[:, t, :], a["x"][t * P:(t + 1) * P, :]).then_inc(s_x[t], 16), signal=0)
        x_in = [(s_x[t], 16) for t in range(NT)]
        for lane, dst, src, s in ((sp, const, a["const"], s_const), (act, cols[:, 0:N_COLS], a["cols"], s_cols), (pool, posi, a["pos"], s_pos)):
            lane(lambda e, dst=dst, src=src, s=s: e.dma_start(dst, src).then_inc(s, 16), signal=0)
        const_in, cols_in, pos_in = (s_const, 16), (s_cols, 16), (s_pos, 16)
        small = place("small", 384)
        lam_rows = small[:, 0:4 * DIFF_D]
        subln = small[:, 256:256 + DIFF_V]
        pool(lambda e: e.dma_start(lam_rows, a["lam"].partition_broadcast(P)).then_inc(s_lam, 16), signal=0)
        pool(lambda e: e.dma_start(subln, a["subln"].partition_broadcast(P)).then_inc(s_sub, 16), signal=0)
        xs = token_buf("xs", D)

        half = stat_col()
        half_set = pool(lambda e: e.memset(half, -0.5))

        def run(steps):
            while True:
                try:
                    next(steps)
                except StopIteration as end:
                    return end.value

        def some_steps(steps, n):
            return [lambda: next(steps, None)] * n

        def inverse_rms(total, width, after):
            n = total.shape[1]
            mean, r = stat_col(n), stat_col(n)
            t0 = dve(lambda e: e.tensor_scalar(mean, total, 1.0 / width, EPS, ALU.mult, ALU.add), after)
            hb = half if n == 1 else half.to_broadcast([P, n])
            t1 = pool(lambda e: e.tensor_tensor(r, mean, hb, ALU.pow), t0, half_set)
            return r, t1

        def squares(src, junk, after, lane):
            total = stat_col()
            if lane is act:
                return total, act(lambda e: e.activation(junk, src, ACT.Square, accum_out=total), after)
            return total, dve(lambda e: e.tensor_tensor_reduce(junk, src, src, 1.0, 0.0, ALU.mult, ALU.add, total), after)

        shifted = place("shifted", 1024)
        shift_free = [None, None]

        def by_tile(ticks):
            return [[panel[t] for panel in ticks] for t in range(NT)]

        def normed_T(*what, **more):
            return run(norm_steps(*what, **more))

        def norm_steps(src, dst, gain, shift, after, gain_ready, tmp_free=None):
            scaled = [[], []]
            for t in range(NT):
                lane = (act, dve)[t % 2]
                total, t0 = squares(src[:, t, :], xs[:, t, :], [after[t] if isinstance(after, list) and len(after) == NT else after, tmp_free], lane)
                r, t1 = inverse_rms(total, D, t0)
                for h_, cut_ in enumerate((slice(0, D // 2), slice(D // 2, D))):
                    v, o = src[:, t, cut_], xs[:, t, cut_]
                    if lane is act:
                        scaled[h_].append(act(lambda e, v=v, o=o, r=r: e.activation(o, v, ACT.Copy, scale=r), t1, t0))
                    else:
                        scaled[h_].append(dve(lambda e, v=v, o=o, r=r: e.tensor_scalar(o, v, r, None, ALU.mult), t1, t0))
            yield
            done = []
            for c2 in range(DC // 2):
                bank, was = take()
                for j in range(2):
                    for t in range(NT):
                        c = 2 * c2 + j
                        tk = turn(bank[:, j * T + t * P:j * T + (t + 1) * P], xs[:, t, c * P:(c + 1) * P],
                                  was, scaled[2 * c // DC], const_in, signal=(j == 1 and t == NT - 1))
                if shift is None:
                    tk = [tk]
                    for j in range(2):
                        c = 2 * c2 + j
                        tk.append(act(lambda e, c=c, j=j, bank=bank: e.activation(dst.hi[:, c, :], bank[:, j * T:(j + 1) * T], ACT.Copy, scale=gain[:, c:c + 1]),
                                      tk[0], gain_ready))
                    for j in range(2):
                        c = 2 * c2 + j
                        lo = dve(lambda e, c=c, j=j, bank=bank: e.scalar_tensor_tensor(
                            dst.lo[:, c, :], bank[:, j * T:(j + 1) * T], gain[:, c:c + 1], dst.hi[:, c, :].bitcast(F32), ALU.mult, ALU.subtract), tk, gain_ready)
                    give(bank, lo)
                else:
                    buf = shifted[:, c2 % 2 * 512:(c2 % 2 + 1) * 512]
                    for j in range(2):
                        c = 2 * c2 + j
                        ev = act(lambda e, c=c, j=j, bank=bank, buf=buf: e.activation(buf[:, j * T:(j + 1) * T], bank[:, j * T:(j + 1) * T], ACT.Identity,
                                                                                    bias=shift[:, c:c + 1], scale=gain[:, c:c + 1]),
                                 tk, gain_ready, shift_free[c2 % 2])
                    give(bank, ev)
                    bv = by_chunk(buf)
                    hi_, lo_ = dst.hi[:, 2 * c2:2 * c2 + 2, :], dst.lo[:, 2 * c2:2 * c2 + 2, :]
                    t0 = dve(lambda e, hi_=hi_, bv=bv: e.tensor_copy(hi_, bv), ev)
                    lo = rest_lo(lo_, bv, hi_, t0)
                    shift_free[c2 % 2] = lo
                done.append([tk, lo])
            return done

        def ready_at(ready, chunk, kc):
            return ready[chunk // 2] if isinstance(ready, list) and len(ready) == DC // 2 and kc == DC else ready

        def token_steps(x, ready, kc, name, n, evacuate):
            opened = [take() for _ in range(NT)]
            n_blk = (kc + 1) // 2
            ticks = [None] * NT
            for b in range(n_blk):
                blk = use(name)[0]
                k0, kb = 2 * b, min(2, kc - 2 * b)
                for t in range(NT):
                    bank, was = opened[t]
                    for k in range(kb):
                        for part in (x.hi, x.lo):
                            mm(bank[:, 0:n], part[:, k0 + k, t * P:(t + 1) * P], blk.hi[:, k, :], b == 0 and k == 0 and part is x.hi, False,
                               was, ready_at(ready, k0 + k, kc), blk.hi_ready)
                for t in range(NT):
                    bank, was = opened[t]
                    for k in range(kb):
                        ticks[t] = mm(bank[:, 0:n], x.hi[:, k0 + k, t * P:(t + 1) * P], blk.lo[:, k, :], False, b == n_blk - 1 and k == kb - 1,
                                      blk.lo_ready, signal=(k == kb - 1))
                blk.released = ticks[NT - 1]
                if b < n_blk - 1:
                    yield
            res = []
            for t in range(NT):
                bank, _ = opened[t]
                ev = evacuate(t, bank[:, 0:n], ticks[t])
                give(bank, ev)
                res.append(ev)
            return res

        def feature_steps(x, ready, kc, name, evacuate):
            bank, was = take()
            n_blk = (kc + 3) // 4
            for b in range(n_blk):
                blk = use(name)[0]
                k0, kb = 4 * b, min(4, kc - 4 * b)
                for j in range(2):
                    for k in range(kb):
                        for part in (x.hi, x.lo):
                            mm(bank[:, j * T:(j + 1) * T], blk.hi[:, k, j * P:(j + 1) * P], part[:, k0 + k, :],
                               b == 0 and j == 0 and k == 0 and part is x.hi, False, was, ready_at(ready, k0 + k, kc), blk.hi_ready, shared=True)
                for j in range(2):
                    for k in range(kb):
                        end = j == 1 and k == kb - 1
                        tk = mm(bank[:, j * T:(j + 1) * T], blk.lo[:, k, j * P:(j + 1) * P], x.hi[:, k0 + k, :],
                                False, end and b == n_blk - 1, blk.lo_ready, signal=end, shared=True)
                blk.released = tk
                if b < n_blk - 1:
                    yield
            ev = evacuate(by_chunk(bank[:, 0:2 * T]), tk)
            give(bank, ev)
            return ev

        def token_major(*panel):
            return run(token_steps(*panel))

        def feature_major(*panel):
            return run(feature_steps(*panel))

        def rows_onto(acc, hid, ready, name, first, last):
            done = []
            for half_ in range(2):
                blk = use(name)[0]
                for t in range(NT):
                    bank, was = acc[2 * half_ + t]
                    for k in range(2):
                        for part in (hid.hi, hid.lo):
                            mm(bank[:, :], part[:, k, t * P:(t + 1) * P], blk.hi[:, k, :], first and k == 0 and part is hid.hi, False,
                               was, ready, blk.hi_ready)
                for t in range(NT):
                    bank, _ = acc[2 * half_ + t]
                    for k in range(2):
                        tk = mm(bank[:, :], hid.hi[:, k, t * P:(t + 1) * P], blk.lo[:, k, :], False, last and k == 1,
                                blk.lo_ready, signal=(k == 1))
                    done.append(tk)
                blk.released = tk
            return done

        flip = [0]

        def copy(dst, src, *after):
            flip[0] += 1
            if flip[0] % 2:
                return act(lambda e: e.activation(dst, src, ACT.Copy), *after)
            return dve(lambda e: e.tensor_copy(dst, src), *after)

        def turned(src, dst_of, blocks_of_cols, ready, *after):
            ticks = []
            for i0 in range(0, len(blocks_of_cols), 2):
                group = blocks_of_cols[i0:i0 + 2]
                bank, was = take()
                for j, (c0, n) in enumerate(group):
                    for t in range(NT):
                        tk = turn(bank[0:n, j * T + t * P:j * T + (t + 1) * P], src[:, t, c0:c0 + n], was, ready, *after,
                                  signal=(j == len(group) - 1 and t == NT - 1))
                n = group[0][1]
                dst, got = dst_of(i0, len(group)), by_chunk(bank[0:n, 0:len(group) * T])
                if isinstance(dst, Pair):
                    t0 = round_hi(dst.hi, got, tk)
                    ev = rest_lo(dst.lo, got, dst.hi, t0, tk)
                    ticks.append([t0, ev])
                else:
                    ev = copy(dst[0:n], got, tk)
                    ticks.append(ev)
                give(bank, ev)
            return ticks

        def pair_view(x, i, n):
            return Pair(x.hi[:, i:i + n, :], x.lo[:, i:i + n, :])

        def pair(name, chunks_):
            hi, lo = (place(f"{name}_{w}", chunks_ * T, F32R) for w in ("hi", "lo"))
            return Pair(by_chunk(hi), by_chunk(lo))

        score_bufs, prob_T = place("score_bufs", 2048), place("prob_T", 1024)
        sb_ring = [score_bufs[:, i * 512:(i + 1) * 512] for i in range(4)]
        pt_ring = [prob_T[:, i * 512:(i + 1) * 512] for i in range(2)]
        att_stats = stat_col(12)
        stat_free = [None] * 4

        def attention(items, ready, meanwhile=()):
            N = len(items)
            meanwhile = list(meanwhile)
            steps, run = len(meanwhile), 0
            out_ticks = []
            buf_free, pt_free = [ready] * 4, [ready] * 2
            for i in range(N + 3):
                if i < N:
                    it = items[i]
                    opened = [take() for _ in range(it["banks"])]
                    tk = it["scores"]([b for b, _ in opened], [was for _, was in opened] + [ready])
                    buf = sb_ring[i % 4][:, 0:it["n"]]
                    it["buf"] = buf
                    msk = it["masked"]([b for b, _ in opened], buf, [tk, buf_free[i % 4]])
                    for (b, _), m_ in zip(opened, msk):
                        give(b, m_)
                    nmax, tot, inv = (att_stats[:, 3 * (i % 4) + j:3 * (i % 4) + j + 1] for j in range(3))
                    t1 = dve(lambda e, buf=buf, nmax=nmax: e.tensor_reduce(nmax, buf, AXX, ALU.max, negate=True), msk, stat_free[i % 4])
                    it["inv"], it["nmax"], it["tot"], it["max"] = inv, nmax, tot, [t1, msk]
                if i >= 1 and i - 1 < N:
                    it = items[i - 1]
                    it["exp"] = act(lambda e, buf=it["buf"], nmax=it["nmax"], tot=it["tot"]: e.activation(buf, buf, ACT.Exp, bias=nmax, accum_out=tot), it["max"])
                if i >= 2 and i - 2 < N:
                    it = items[i - 2]
                    kc = it["n"] // P
                    bank, was = take()
                    for k in range(kc):
                        tk = turn(bank[:, k * P:(k + 1) * P], it["buf"][:, k * P:(k + 1) * P], was, it["exp"], signal=(k == kc - 1))
                    buf_free[(i - 2) % 4] = tk
                    pt = pt_ring[i % 2][:, 0:it["n"]]
                    it["pt"] = pt
                    it["ptt"] = copy(pt, bank[:, 0:it["n"]], tk, pt_free[i % 2])
                    give(bank, it["ptt"])
                    it["invt"] = dve(lambda e, inv=it["inv"], tot=it["tot"]: e.reciprocal(inv, tot), it["exp"])
                if i >= 3:
                    it = items[i - 3]
                    bank, was = take()
                    kc = it["n"] // P
                    for k in range(kc):
                        tk = mm(bank[:, 0:P], it["pt"][:, k * P:(k + 1) * P], it["values"][k], k == 0, k == kc - 1,
                                was, it["ptt"], it["values_ready"], signal=(k == kc - 1))
                    pt_free[(i - 3) % 2] = tk
                    ev = it["finish"](bank, it["inv"], [tk, it["invt"]])
                    stat_free[(i - 3) % 4] = ev
                    give(bank, ev)
                    out_ticks.append(ev)
                while meanwhile and run * (N + 1) < (i + 1) * steps:
                    meanwhile.pop(0)()
                    run += 1
            return out_ticks

        act_T = pair("act", DC)
        x_norm = norm_steps(xr, act_T, col("norm_mix_g", 0, 8), None, x_in, cols_in)
        next(x_norm)
        issue(0)
        xn = run(x_norm)

        rope_tmp = place("rope_tmp", 512)
        rope_last = [None]

        def rope(v, c0, heads, stride, half_n, f0, after):
            ticks = []
            for t in range(NT):
                w = v[:, t, 0:heads * stride].rearrange("p (h s) -> p h s", s=stride)
                x1, x2 = w[:, :, c0:c0 + half_n], w[:, :, c0 + half_n:c0 + 2 * half_n]
                co = cos_t[:, t * N_FREQ + f0:t * N_FREQ + f0 + half_n].unsqueeze(1).to_broadcast([P, heads, half_n])
                si = sin_t[:, t * N_FREQ + f0:t * N_FREQ + f0 + half_n].unsqueeze(1).to_broadcast([P, heads, half_n])
                n = heads * half_n
                tm = [rope_tmp[:, i * 128:i * 128 + n].rearrange("p (h s) -> p h s", s=half_n) for i in range(4)]
                tt = lambda o, x, y, op, *af: pool(lambda e: e.tensor_tensor(o, x, y, op), *af)
                tt(tm[0], x1, co, ALU.mult, after, rope_ready, rope_last[0])
                tt(tm[1], x2, si, ALU.mult)
                tt(tm[2], x2, co, ALU.mult)
                a1 = tt(tm[3], x1, si, ALU.mult)
                tt(x1, tm[0], tm[1], ALU.subtract, a1)
                rope_last[0] = tt(x2, tm[2], tm[3], ALU.add, a1)
                ticks.append(rope_last[0])
            return ticks

        lat = token_buf("lat", LAT)
        lat_ready = []
        for c0 in (0, LAT // 2):
            lat_ready.append(token_major(act_T, xn, DC, "w_in", LAT // 2, lambda t, p, tk, c0=c0: copy(lat[:, t, c0:c0 + LAT // 2], p, tk)))

        posf = stat_col(NT)
        t_pos = dve(lambda e: e.tensor_copy(posf, posi), pos_in)
        nf = NT * N_FREQ
        rope_w = place("rope", 6 * nf)
        turns = place("turns", nf, I32)
        ang, red, tmp, sin_t, cos_t, nturn = (rope_w[:, i * nf:(i + 1) * nf] for i in range(6))
        tk = None
        for t in range(NT):
            tk = dve(lambda e, t=t: e.tensor_scalar(ang[:, t * N_FREQ:(t + 1) * N_FREQ], freq, posf[:, t:t + 1], None, ALU.mult),
                     t_pos, const_in)
        TWO_PI = 2 * math.pi
        c1 = 6.28125
        c2 = float(np.float32(np.round((TWO_PI - c1) * 2**21) / 2**21))
        c3 = TWO_PI - c1 - c2
        tk = dve(lambda e: e.tensor_scalar(turns, ang, 1.0 / TWO_PI, None, ALU.mult), tk)
        tk = dve(lambda e: e.tensor_copy(nturn, turns), tk)
        tk = dve(lambda e: e.scalar_tensor_tensor(red, nturn, -c1, ang, ALU.mult, ALU.add), tk)
        for c in (c2, c3):
            tk = dve(lambda e, c=c: e.scalar_tensor_tensor(red, nturn, -c, red, ALU.mult, ALU.add), tk)

        def wrap(v, tk):
            tk = dve(lambda e: e.tensor_scalar(tmp, v, math.pi, -TWO_PI, ALU.is_gt, ALU.mult), tk)
            tk = dve(lambda e: e.tensor_tensor(v, v, tmp, ALU.add), tk)
            tk = dve(lambda e: e.tensor_scalar(tmp, v, -math.pi, TWO_PI, ALU.is_lt, ALU.mult), tk)
            tk = dve(lambda e: e.tensor_tensor(v, v, tmp, ALU.add), tk)
            return dve(lambda e: e.tensor_scalar(v, v, 3.1415925, -3.1415925, ALU.min, ALU.max), tk)

        tk = wrap(red, tk)
        t_sin = act(lambda e: e.activation(sin_t, red, ACT.Sin), tk)
        tk = dve(lambda e: e.tensor_scalar(ang, red, math.pi / 2, None, ALU.add), tk)
        tk = wrap(ang, tk)
        rope_ready = [act(lambda e: e.activation(cos_t, ang, ACT.Sin), tk), t_sin]

        lam_s, lam_e, lam_neg = stat_col(2), stat_col(2), stat_col()
        lam_junk = stat_col(DIFF_D)
        for i in range(2):
            tk = dve(lambda e, i=i: e.tensor_tensor_reduce(lam_junk, lam_rows[:, 2 * i * DIFF_D:(2 * i + 1) * DIFF_D],
                                                           lam_rows[:, (2 * i + 1) * DIFF_D:(2 * i + 2) * DIFF_D],
                                                           1.0, 0.0, ALU.mult, ALU.add, lam_s[:, i:i + 1]), (s_lam, 16), tk)
        tk = act(lambda e: e.activation(lam_e, lam_s, ACT.Exp), tk)
        tk = dve(lambda e: e.tensor_scalar(lam_neg, lam_e[:, 1:2], -LAMBDA_INIT, None, ALU.add), tk)
        lam_ready = dve(lambda e: e.tensor_tensor(lam_neg, lam_neg, lam_e[:, 0:1], ALU.subtract), tk)

        cs = stat_col(2 * DC)
        t_cs = act(lambda e: e.activation(cs, cols[:, COLS["c"][0]:COLS["c"][0] + 2 * DC], ACT.Silu), cols_in)

        kpe = lat[:, :, Q_RANK + KV_RANK:LAT]
        t_kpe = rope(kpe, 0, 1, ROPE, HALF_M, 0, lat_ready)

        dq, dk, dv = (token_buf(n, 512) for n in ("dq", "dk", "dv"))
        km = token_buf("km", 768)
        lat_T = pair("lat", 5)
        got = []
        for j, dst in enumerate((dq, dk, dv)):
            got.append(token_major(act_T, xn, DC, "w_in", 512, lambda t, p, tk, dst=dst: copy(dst[:, t, :], p, tk)))
            if j == 0:
                lat_scaled = []
                for t in range(NT):
                    for j2, (c0, n) in enumerate(((0, Q_RANK), (Q_RANK, KV_RANK))):
                        total, t0 = squares(lat[:, t, c0:c0 + n], km[:, t, j2 * 384:j2 * 384 + n], lat_ready, (act, dve)[j2])
                        r, t1 = inverse_rms(total, n, t0)
                        lat_scaled.append(dve(lambda e, t=t, c0=c0, n=n, r=r: e.tensor_scalar(lat[:, t, c0:c0 + n], lat[:, t, c0:c0 + n], r, None, ALU.mult), t1, t0))
            if j != 1:
                continue
            lat_T_ready = []
            g0 = COLS["q_norm_g"][0]
            for c in range(5):
                bank, was = take()
                for t in range(NT):
                    tk = turn(bank[:, t * P:(t + 1) * P], lat[:, t, c * P:(c + 1) * P], was, lat_scaled, signal=(t == NT - 1))
                g = cols[:, g0 + c:g0 + c + 1]
                t0 = act(lambda e, c=c, bank=bank, g=g: e.activation(lat_T.hi[:, c, :], bank[:, 0:T], ACT.Copy, scale=g), tk)
                ev = dve(lambda e, c=c, bank=bank, g=g: e.scalar_tensor_tensor(lat_T.lo[:, c, :], bank[:, 0:T], g, lat_T.hi[:, c, :].bitcast(F32),
                                                                               ALU.mult, ALU.subtract), t0, tk)
                give(bank, ev)
                lat_T_ready.append([t0, ev])
        t_dq = rope(dq, 0, 8, DIFF_D, HALF_D, HALF_M, got[0])
        t_dk = rope(dk, 0, 8, DIFF_D, HALF_D, HALF_M, got[1])
        dv_ready = got[2]

        qm, kv = token_buf("qm", 768), token_buf("kv", 1024)
        q_up = []
        for c0 in (0, 384):
            q_up.append(token_major(pair_view(lat_T, 0, 3), lat_T_ready, 3, "w_uq", 384, lambda t, p, tk, c0=c0: copy(qm[:, t, c0:c0 + 384], p, tk)))
        t_qm = rope(qm, NOPE, MLA_H, MLA_QK, HALF_M, 0, q_up)
        kv_up = []
        for c0 in (0, 512):
            kv_up.append(token_major(pair_view(lat_T, 3, 2), lat_T_ready, 2, "w_ukv", 512, lambda t, p, tk, c0=c0: copy(kv[:, t, c0:c0 + 512], p, tk)))
        km_ready = []
        for t in range(NT):
            kv_h = kv[:, t, :].rearrange("p (h s) -> p h s", s=2 * NOPE)
            km_h = km[:, t, :].rearrange("p (h s) -> p h s", s=MLA_QK)
            km_ready.append(dve(lambda e, o=km_h, i=kv_h: e.tensor_copy(o[:, :, 0:NOPE], i[:, :, 0:NOPE]), kv_up, lat_scaled))
            km_ready.append(pool(lambda e, o=km_h, t=t: e.tensor_copy(o[:, :, NOPE:MLA_QK], kpe[:, t, :].unsqueeze(1).to_broadcast([P, MLA_H, ROPE])), t_kpe, lat_scaled))

        gates_T = by_chunk(place("gates_T", 4096))
        gates_raw = []

        def gate_panel(j):
            def ev(p, tk):
                gates_raw.append(copy(gates_T[:, 2 * j:2 * j + 2, :], p, tk))
                return gates_raw[-1]
            return feature_steps(act_T, xn, DC, "w_in", ev)

        for j in range(2):
            run(gate_panel(j))

        qm_T, km_T = (by_chunk(place(n, 2048)) for n in ("qm_T", "km_T"))
        dq_T, dk_T = (by_chunk(place(n, 1024)) for n in ("dq_T", "dk_T"))
        att_ready = []
        for src, dst, blocks_, rdy in ((qm, qm_T, [(h * MLA_QK, MLA_QK) for h in range(MLA_H)], t_qm),
                                       (km, km_T, [(h * MLA_QK, MLA_QK) for h in range(MLA_H)], km_ready),
                                       (dq, dq_T, [(h * P, P) for h in range(DIFF_H)], t_dq),
                                       (dk, dk_T, [(h * P, P) for h in range(DIFF_H)], t_dk)):
            att_ready.append(turned(src, lambda i, n, dst=dst: dst[:, i:i + n, :], blocks_, rdy))

        o_mla, o_diff = token_buf("o_mla", 512), token_buf("o_diff", 512)
        oa_T, ob_T = pair("oa", 4), pair("ob", 4)
        blocks4 = [(c * P, P) for c in range(4)]
        mla_done, oa_ready = [], []
        items = []

        def causal_item(qT, kT, lo, hi, qb, scale, values, finish, vready):
            n = (qb + 1) * P
            m = mask[:, 2 * P - n:2 * P]

            def scores(bank, after):
                return mm(bank[0][:, 0:n], qT[lo:hi, qb * P:(qb + 1) * P], kT[lo:hi, 0:n], True, True, after, att_ready, signal=True)

            def masked(bank, buf, after):
                return [dve(lambda e: e.scalar_tensor_tensor(buf, bank[0][:, 0:n], scale, m, ALU.mult, ALU.add), after)]
            return dict(n=n, banks=1, scores=scores, masked=masked, values=values, finish=finish, values_ready=vready)

        for h in range(MLA_H):
            for qb in range(NT):
                vals = [kv[:, k, h * 128:(h + 1) * 128] for k in range(qb + 1)]

                def fin(p, inv, after, h=h, qb=qb):
                    mla_done.append(act(lambda e: e.activation(o_mla[:, qb, h * 64:(h + 1) * 64], p[:, NOPE:NOPE + MLA_V], ACT.Copy, scale=inv), after))
                    return mla_done[-1]
                items.append(causal_item(qm_T[:, h, :], km_T[:, h, :], 0, MLA_QK, qb, MLA_QK ** -0.5, vals, fin, kv_up))
        o2_buf = [rope_tmp[:, 0:128], rope_tmp[:, 128:256]]
        o2_free = [None, None]
        o1_tick = {}
        for h in range(DIFF_H):
            for qb in range(NT):
                for comp in range(2):
                    vals = [dv[:, k, h * P:(h + 1) * P] for k in range(qb + 1)]

                    def fin(p, inv, after, h=h, qb=qb, comp=comp):
                        dst = o_diff[:, qb, h * P:(h + 1) * P]
                        if comp == 0:
                            o1_tick[h, qb] = act(lambda e: e.activation(dst, p[:, 0:P], ACT.Copy, scale=inv), after)
                            return o1_tick[h, qb]
                        i = (h * NT + qb) % 2
                        t0 = act(lambda e: e.activation(o2_buf[i], p[:, 0:P], ACT.Copy, scale=inv), after, o2_free[i], t_qm, t_dk)
                        t1 = dve(lambda e: e.scalar_tensor_tensor(dst, o2_buf[i], lam_neg, dst, ALU.mult, ALU.add), t0, lam_ready, o1_tick[h, qb])
                        o2_free[i] = t1
                        return [t0, t1]
                    items.append(causal_item(dq_T[:, h, :], dk_T[:, h, :], comp * 64, comp * 64 + 64, qb, DIFF_D ** -0.5,
                                             vals, fin, dv_ready))

        def beside_attention():
            for j in range(2, 8):
                for _ in gate_panel(j):
                    yield
                yield
            for i in (0, 2):
                assert len(mla_done) == MLA_H * NT
                oa_ready.extend(turned(o_mla, lambda _, n, i=i: pair_view(oa_T, i, n), blocks4[i:i + 2], mla_done, att_ready))
                yield

        att_done = attention(items, [xn], some_steps(beside_attention(), 14))

        tot = stat_col(NT * DIFF_H)
        tks = []
        for t in range(NT):
            for h in range(DIFF_H):
                i = t * DIFF_H + h
                v = o_diff[:, t, h * P:(h + 1) * P]
                tks.append(dve(lambda e, v=v, i=i: e.tensor_tensor_reduce(rope_tmp[:, 256:384], v, v, 1.0, 0.0, ALU.mult, ALU.add, tot[:, i:i + 1]),
                               att_done, tks[-1:] if tks else None))
        r, t1 = inverse_rms(tot, DIFF_V, tks)
        t_r = dve(lambda e: e.tensor_scalar(r, r, 1.0 - LAMBDA_INIT, None, ALU.mult), t1)
        odn = []
        for t in range(NT):
            for h in range(DIFF_H):
                i = t * DIFF_H + h
                v = o_diff[:, t, h * P:(h + 1) * P]
                odn.append(dve(lambda e, v=v, i=i: e.scalar_tensor_tensor(v, v, r[:, i:i + 1], subln, ALU.mult, ALU.mult), t_r, (s_sub, 16)))

        gates_ready = [act(lambda e, c=c: e.activation(gates_T[:, c, :], gates_T[:, c, :], ACT.Sigmoid, bias=col("b_gate", c)), gates_raw, cols_in)
                       for j in range(4) for c in (2 * j, 2 * j + 1, 8 + 2 * j, 9 + 2 * j)]

        merged = by_chunk(place("merged", 2048))
        merged_T = pair("merged", DC)
        merged_ready = []
        ms = [merged[:, 2 * j:2 * j + 2, :] for j in range(4)]
        gate_of = [(gates_T[:, 2 * j:2 * j + 2, :], gates_T[:, 8 + 2 * j:10 + 2 * j, :]) for j in range(4)]
        first_part = []
        for j, m in enumerate(ms):
            first_part.append(feature_major(oa_T, oa_ready, 4, "w_b_mla", lambda p, tk, m=m, ga=gate_of[j][0], j=j: dve(
                lambda e: e.tensor_tensor(m, p, ga, ALU.mult), tk, gates_ready[4 * j:4 * j + 4], att_done)))
        ob_ready = turned(o_diff, lambda i, n: pair_view(ob_T, i, n), blocks4, odn)
        for j, m in enumerate(ms):
            gb = gate_of[j][1]
            tb = feature_major(ob_T, ob_ready, 4, "w_b_diff", lambda p, tk, gb=gb, j=j: dve(lambda e: e.tensor_tensor(gb, p, gb, ALU.mult), tk, gates_ready[4 * j:4 * j + 4]))
            t1 = dve(lambda e, m=m, gb=gb: e.tensor_tensor(m, m, gb, ALU.add), first_part[j], tb)
            mv = pair_view(merged_T, 2 * j, 2)
            t2 = round_hi(mv.hi, m, t1)
            merged_ready.append([t2, rest_lo(mv.lo, m, mv.hi, t2, t1)])

        x2 = []
        for j in range(2):
            def ev(t, p, tk, j=j):
                v = xr[:, t, 512 * j:512 * (j + 1)]
                return dve(lambda e: e.tensor_tensor(v, p, v, ALU.add), tk, xn)
            x2.append(token_major(merged_T, merged_ready, DC, "w_out", 512, ev))

        hn = normed_T(xr, act_T, col("norm_ffn_g", 0, 8), None, by_tile(x2), cols_in, tmp_free=att_done)
        ada = {"x": place("ada_x", 6 * D), "c": place("ada_c", 2 * D)}
        ada_tick = {}

        N_ADA, N_EARLY, HALF_C = 6 * D // 512 * 2, 6 * D // 512, DC // 2
        ada_bufs = [place(f"ada_w{i}", 2048, F32, o).rearrange("p (c n) -> p c n", n=512) for i, o in enumerate(OFF["ada_bufs"])]
        ada_was = [[att_done, oa_ready]] * 2 + [x2] * 3
        ada_used = {}

        def ada_slot(i):
            if i < N_EARLY:
                return i % ADA_BUFS, i // ADA_BUFS, i - ADA_BUFS
            n = i - N_EARLY
            return ADA_BUFS + n % ADA_LATE_BUFS, n // ADA_LATE_BUFS, i - ADA_LATE_BUFS

        def load_ada(i):
            b, nth, before = ada_slot(i)
            lane = sp if i < N_EARLY else pool
            lane(lambda e: e.dma_start(ada_bufs[b], by_chunks(a["ada_w"], i % 2 * 512, HALF_C, i // 2 * 512, 512)).then_inc(s_ada[b], 16),
               ada_used[before] if nth else ada_was[b], signal=0)

        def ada_steps(first, end, bufs):
            for i in range(first, end):
                b, nth, _ = ada_slot(i)
                for k in range(HALF_C):
                    if k == (0 if bufs == 2 else 2) and first + bufs <= i + bufs - 1 < end:
                        load_ada(i + bufs - 1)
                    for who, base in (("x", 0), ("c", DC)):
                        cb = i // 2
                        if who == "c" and cb >= 4:
                            continue
                        acc = ada[who][:, cb * 512:(cb + 1) * 512]
                        o = base + i % 2 * HALF_C + k
                        s, w = cs[:, o:o + 1], ada_bufs[b][:, k, :]
                        arrived = (s_ada[b], 16 * (nth + 1))
                        if k == 0 and i % 2 == 0:
                            tk = dve(lambda e, acc=acc, w=w, s=s: e.tensor_scalar(acc, w, s, None, ALU.mult), arrived, t_cs, x2)
                        else:
                            tk = dve(lambda e, acc=acc, w=w, s=s: e.scalar_tensor_tensor(acc, w, s, acc, ALU.mult, ALU.add),
                                     arrived, ada_tick[who, cb])
                        ada_tick[who, cb] = ada_used[i] = tk
                        yield

        hid_raw = [by_chunk(place(f"hid{i}", 512, F32, OFF["hid"] + 1024 * i)) for i in range(HID_BUFS)]
        hid_pair = [Pair(by_chunk(place(f"hid_hi{i}", 512, F32R, OFF["hid"] + 1024 * i + 512)),
                         by_chunk(place(f"hid_lo{i}", 512, F32R, OFF["hid"] + 1024 * i))) for i in range(HID_BUFS)]
        hid_free = [None] * HID_BUFS

        def split_hid(i, tk):
            t0 = round_hi(hid_pair[i].hi, hid_raw[i], tk)
            return [t0, rest_lo(hid_pair[i].lo, hid_raw[i], hid_pair[i].hi, t0, tk)]

        mod = place("mod", 6 * DC)
        mcol = {n: mod[:, i * DC:(i + 1) * DC] for i, n in enumerate(("sh1", "sc1", "csh1", "csc1", "sh2", "sc2"))}
        mod_ready, grow_ready = {}, {}
        g1row, g2row = place("g1row", D), place("g2row", D)

        def summed(who, part):
            return [ada_tick[who, 2 * part], ada_tick[who, 2 * part + 1]]

        def mod_columns(name, who, part):
            tks = []
            for half_ in range(2):
                bank, was = take()
                for j in range(4):
                    o = part * D + (half_ * 4 + j) * P
                    tk = turn(bank[:, j * P:(j + 1) * P], ada[who][:, o:o + P], was, summed(who, part), signal=(j == 3))
                ev = dve(lambda e, bank=bank, half_=half_: e.tensor_reduce(
                    mcol[name][:, half_ * 4:half_ * 4 + 4], bank[:, :].rearrange("p (j t) -> p j t", j=4), AXX, ALU.add), tk)
                give(bank, ev)
                tks.append(ev)
            bias = col("ada_b", part * DC, DC)
            tk = dve(lambda e: e.tensor_tensor(mcol[name], mcol[name], bias, ALU.add), tks)
            if "sc" in name:
                gain = col("norm2_g" if name == "sc2" else "norm1_g", 0, DC)
                tk = dve(lambda e: e.scalar_tensor_tensor(mcol[name], mcol[name], 1.0, gain, ALU.add, ALU.mult), tk)
            mod_ready[name] = tk

        def gate_row(part, dst, src):
            bias = use(src)[0]
            tks = []
            for half_ in range(2):
                bank, was = take()
                tk = mm(bank[:, :], ones, ada["x"][:, part * D + half_ * 512:part * D + (half_ + 1) * 512], True, True, was, summed("x", part), signal=True)
                ev = dve(lambda e, bank=bank, half_=half_: e.tensor_tensor(
                    dst[:, half_ * 512:(half_ + 1) * 512], bank[:, :], bias.view[:, 0, half_ * 512:(half_ + 1) * 512], ALU.add), tk, bias.arrived)
                give(bank, ev)
                tks.append(ev)
            bias.released = tks[-1]
            grow_ready[part] = tks

        EARLY_MODS = {3 * (CTX_UNIT - 1) + i: m for i, m in enumerate((("csh1", "c", 0), ("csc1", "c", 1), ("sh1", "x", 0), ("sc1", "x", 1)))}
        ctx_T = pair("ctx", DC)

        acc = [take() for _ in range(4)]
        n_units = FFN // UNIT
        hid_ready = {}
        for i in range(ADA_BUFS):
            load_ada(i)
        ada_left = ada_steps(0, N_EARLY, ADA_BUFS)
        ADA_STEPS = HALF_C * (N_EARLY + 8)
        ada_done_steps = [0]

        def ada_some(u, third):
            while ada_done_steps[0] * 3 * (CTX_UNIT - 1) < (3 * u + third + 1) * ADA_STEPS and ada_done_steps[0] < ADA_STEPS:
                next(ada_left)
                ada_done_steps[0] += 1
            if 3 * u + third in EARLY_MODS:
                mod_columns(*EARLY_MODS[3 * u + third])

        for u in range(n_units + 1):
            if u < n_units:
                i = u % HID_BUFS
                hr = hid_raw[i]
                t0 = feature_major(act_T, hn, DC, "w_gate", lambda p, tk, hr=hr, i=i: act(lambda e: e.activation(hr, p, ACT.Silu), tk, hid_free[i]))
                ada_some(u, 0)
                t1 = feature_major(act_T, hn, DC, "w_up", lambda p, tk, hr=hr: dve(lambda e: e.tensor_tensor(hr, p, hr, ALU.mult), tk, t0))
                hid_ready[u] = split_hid(i, t1)
                ada_some(u, 1)
            if u >= 1:
                i = (u - 1) % HID_BUFS
                down_tick = hid_free[i] = rows_onto(acc, hid_pair[i], hid_ready[u - 1], "w_down", u == 1, u == n_units)
            ada_some(u, 2)
            if u == CTX_UNIT:
                ctx_blk = use("ctx")[0]
                ctx_norm = norm_steps(ctx_blk.view, ctx_T, mcol["csc1"], mcol["csh1"], ctx_blk.arrived,
                                      [mod_ready["csc1"], mod_ready["csh1"]], tmp_free=[hn, att_done])
                next(ctx_norm)
                ctx_blk.released = [(act.sem, act.count), (dve.sem, dve.count)]
            if u == CTX_UNIT + 1:
                hc = run(ctx_norm)
        x3 = []
        for half_ in range(2):
            for t in range(NT):
                bank, _ = acc[2 * half_ + t]
                v = xr[:, t, half_ * 512:(half_ + 1) * 512]
                tk = dve(lambda e, v=v, bank=bank: e.tensor_tensor(v, bank[:, :], v, ALU.add), down_tick[2 * half_ + t], hn)
                give(bank, tk)
                x3.append(tk)

        zx, zc = token_buf("zx", 2048), token_buf("zc", 1024)
        zx_ready, zc_ready = {}, {}
        ada_done = list(ada_tick.values())

        def mixed(dst, c0, x, rdy, name, ready_by, j):
            def ev(t, p, tk):
                ready_by.setdefault(j, []).append(copy(dst[:, t, c0:c0 + 512], p, tk, ada_done, down_tick))
                return ready_by[j][-1]
            return token_steps(x, rdy, DC, name, 512, ev)

        def context_panels():
            for j in (2, 3):
                yield from mixed(zc, 512 * (j - 2), ctx_T, hc, "w_in2_ctx", zc_ready, j)
                yield

        def final_norm(xv, junk, src_ready, gain_blk):
            ticks = []
            for t in range(NT):
                total, t0 = squares(xv[:, t, :], junk[:, t, :], src_ready, (act, dve)[t % 2])
                r, t1 = inverse_rms(total, D, t0)
                ticks.append(dve(lambda e, t=t, r=r: e.scalar_tensor_tensor(xv[:, t, :], xv[:, t, :], r, gain_blk.view[:, 0, :], ALU.mult, ALU.mult),
                                 t1, t0, gain_blk.arrived))
            gain_blk.released = ticks[-1]
            return ticks

        band = place("band", 2048)
        pool_w = place("pool_w", 512)
        sp(lambda e: e.dma_start(band, a["band"]).then_inc(s_band, 16), mod_ready["csh1"], mod_ready["csc1"], signal=0)
        sp(lambda e: e.dma_start(pool_w, a["pool_w"]).then_inc(s_pool_w, 16), ob_ready, signal=0)
        band = band.rearrange("p (k g t) -> p k g t", k=NT, g=4)
        panels = context_panels()
        for _ in range(3):
            next(panels)
        x4 = final_norm(xr, xs, [x3, hn, hc], use("norm_final_g")[0])
        run(panels)
        ada_was += [zc_ready[2] + zc_ready[3]] * ADA_LATE_BUFS
        for i in range(ADA_LATE_BUFS):
            load_ada(N_EARLY + i)
        ada_left = ada_steps(N_EARLY, N_ADA, ADA_LATE_BUFS)

        def ada_more(n):
            for _ in range(n):
                next(ada_left)

        hx = normed_T(xr, act_T, mcol["sc1"], mcol["sh1"], x4, [mod_ready["sc1"], mod_ready["sh1"], down_tick], tmp_free=hc)
        q_T, k_T, kc_T = (by_chunk(place(n, 1024)) for n in ("q_T", "k_T", "kc_T"))
        na_ready = []

        def head_rows(src, c0, dst, rdy):
            na_ready.append(turned(src, lambda i, n: dst[:, i:i + n, :], [(c0 + c * P, P) for c in range(4)], rdy))

        head_rows(zc, 0, kc_T, zc_ready[2])
        for j in (1, 2, 3):
            for i, _ in enumerate(mixed(zx, 512 * j, act_T, hx, "w_in2", zx_ready, j)):
                if j > 1:
                    ada_more(3)
                if j == 3 and i == 1:
                    head_rows(zx, 1024, k_T, zx_ready[2])
            if j == 2:
                head_rows(zx, 512, q_T, zx_ready[1])

        attn = token_buf("attn", 512)
        items = []
        scale = NA_D ** -0.5
        bias_blk = {}
        for h in range(NA_H):
            for qb in range(NT):
                lo = (h % 2) * 64

                def scores(bank, after, h=h, qb=qb, lo=lo):
                    if h % 2 == 0 and qb == 0:
                        bias_blk[h // 2] = use("na_bias")[0]
                    q = q_T[lo:lo + 64, h // 2, qb * P:(qb + 1) * P]
                    mm(bank[0][:, 0:T], q, k_T[lo:lo + 64, h // 2, :], True, True, after, na_ready)
                    return mm(bank[1][:, 0:T], q, kc_T[lo:lo + 64, h // 2, :], True, True, signal=True)

                def masked(bank, buf, after, h=h, qb=qb):
                    hb = bias_blk[h // 2]
                    o = ((h % 2) * NT + qb) * T
                    t0 = dve(lambda e: e.scalar_tensor_tensor(buf[:, 0:T], bank[0][:, 0:T], scale, hb.view[:, 0, o:o + T], ALU.mult, ALU.add), after, hb.arrived)
                    if h % 2 and qb == NT - 1:
                        hb.released = t0
                    return [t0, act(lambda e: e.activation(buf[:, T:2 * T], bank[1][:, 0:T], ACT.Copy, scale=scale), after)]

                def fin(p, inv, after, h=h, qb=qb, lo=lo):
                    return act(lambda e: e.activation(attn[:, qb, h * 64:(h + 1) * 64], p[:, lo:lo + 64], ACT.Copy, scale=inv), after)
                o = h // 2 * P
                vals = [zx[:, k, 1536 + o:1536 + o + P] for k in range(NT)] + [zc[:, k, 512 + o:512 + o + P] for k in range(NT)]
                items.append(dict(n=2 * T, banks=2, scores=scores, masked=masked, values=vals, finish=fin, values_ready=[zx_ready[3], zc_ready[3]]))

        mix_T = act_T
        mix_ready = []
        pooled_T = by_chunk(place("pooled_T", 1024))

        def pooled_group(g):
            bank, was = take()
            for k in range(NT):
                tk = mm(bank[:, 0:T], zx[:, k, g * P:(g + 1) * P], band[:, k, g, :], k == 0, k == NT - 1,
                        was, zx_ready[0], (s_band, 16), signal=(k == NT - 1))
            ev = copy(pooled_T[:, g, :], bank[:, 0:T], tk, ada_done)
            give(bank, ev)
            bank2, was = take()
            tk = mm(bank2[:, 0:T], pool_w[:, g * P:(g + 1) * P], pooled_T[:, g, :], True, True, was, ev, (s_pool_w, 16), signal=True)
            t0 = act(lambda e: e.activation(mix_T.hi[:, g, :], bank2[:, 0:T], ACT.Copy, scale=col("pool_scale", g)), tk)
            ev = dve(lambda e: e.scalar_tensor_tensor(mix_T.lo[:, g, :], bank2[:, 0:T], col("pool_scale", g), mix_T.hi[:, g, :].bitcast(F32),
                                                      ALU.mult, ALU.subtract), t0, tk)
            give(bank2, ev)
            mix_ready.append([t0, ev])

        def beside():
            for i, _ in enumerate(mixed(zx, 0, act_T, hx, "w_in2", zx_ready, 0)):
                ada_more(4)
                yield
                if i == 2:
                    yield
            ada_more(4)
            yield
            for g in range(4):
                pooled_group(g)
                if g < 3:
                    ada_more(4)
                else:
                    run(ada_left)
                yield
            for m in (("sh2", "x", 3), ("sc2", "x", 4)):
                mod_columns(*m)
                yield
            gate_row(2, g1row, "ada_b_g1")
            yield
            gate_row(5, g2row, "ada_b_g2")

        attn_done = attention(items, [hx], some_steps(beside(), 13))
        mix_ready = [mix_ready[0:2], mix_ready[2:4]] + turned(attn, lambda i, n: pair_view(mix_T, 4 + i, n), blocks4, attn_done)

        x5 = []
        gated = place("gated", 1024)
        for j in range(2):
            def ev(t, p, tk, j=j):
                c0 = 512 * j
                tmp_ = gated[:, t * 512:(t + 1) * 512]
                t0 = dve(lambda e: e.tensor_tensor(tmp_, p, g1row[:, c0:c0 + 512], ALU.mult), tk, grow_ready[2], attn_done, x5[t::NT])
                v = xr[:, t, c0:c0 + 512]
                x5.append((pool, dve)[j](lambda e: e.tensor_tensor(v, tmp_, v, ALU.add), t0, hx))
                return t0
            token_major(mix_T, mix_ready, DC, "w_out2", 512, ev)
        sp(lambda e: e.dma_start(parked_x.rearrange("(t p) d -> p t d", p=P), xr).then_inc(s_park, 16), x5, signal=0)
        sp(lambda e: e.dma_start(parked_g2, g2row).then_inc(s_park, 16), grow_ready[5], signal=0)
        parked = (s_park, 32)
        dram_ready["parked_x"] = dram_ready["parked_g2"] = parked

        h2 = normed_T(xr, act_T, mcol["sc2"], mcol["sh2"], [x5[t::NT] for t in range(NT)], [mod_ready["sc2"], mod_ready["sh2"]], tmp_free=attn_done)

        pq_T = by_chunk(place("pq_T", 4096))
        keys_T = place("keys_T", 2048)
        sp(lambda e: e.dma_start(keys_T, a["keys_T"]).then_inc(s_keys, 16), mix_ready, attn_done, signal=0)
        keys_in = (s_keys, 16)
        TW = 2 * NT
        s_all = place("s", 4096).rearrange("p (h g n) -> p h g n", h=PE_H, g=TW)
        s_work = place("s_work", 512).rearrange("p (g n) -> p g n", g=TW)
        v12 = place("v12", 512).rearrange("p (h t w k) -> p h t w k", h=PE_H, t=NT, w=2)
        i12 = place("i12", 512, U32).rearrange("p (h g k) -> p h g k", h=PE_H, g=TW)
        i12f = place("i12f", 512).rearrange("p (h g k) -> p h g k", h=PE_H, g=TW)
        cand = place("cand", 4096).rearrange("p (h t k) -> p h t k", h=PE_H, t=NT)
        cand_work = place("cand_work", 512).rearrange("p (t k) -> p t k", t=NT)
        eq = place("eq", 2048).rearrange("p (b g k a) -> p b g k a", b=2, g=TW, a=TOPK)
        topv = place("topv", 256).rearrange("p (g k) -> p g k", k=TOPK)
        topi = place("topi", 256, U32).rearrange("p (g k) -> p g k", k=TOPK)
        ab = place("ab", 512, U32).rearrange("p (h t w k) -> p h t w k", h=PE_H, t=NT, w=2)
        abf = place("abf", 512).rearrange("p (h g k) -> p h g k", h=PE_H, g=TW)
        pick = place("pick", 512).rearrange("p (g h k) -> p g h k", g=TW, h=PE_H)
        weight = place("weight", 256).rearrange("p (t h k) -> p t h k", t=NT, h=PE_H)
        best, total16, inv16 = (stat_col(NT * PE_H) for _ in range(3))
        iota16 = iota[:, 0:TOPK]

        def top16(rows, after):
            for x, _, vals, _ in rows:
                t0 = dve(lambda e, x=x, vals=vals: e.max(vals[:, 0:8], x), after)
            for x, work, vals, _ in rows:
                t1 = dve(lambda e, x=x, work=work, vals=vals: e.match_replace(work, vals[:, 0:8], x, LOWEST), t0)
            for x, _, vals, idx in rows:
                dve(lambda e, x=x, vals=vals, idx=idx: e.max_index(idx[:, 0:8], vals[:, 0:8], x), t0)
            for _, work, vals, _ in rows:
                t2 = dve(lambda e, work=work, vals=vals: e.max(vals[:, 8:16], work), t1)
            for _, work, vals, idx in rows:
                t3 = dve(lambda e, work=work, vals=vals, idx=idx: e.max_index(idx[:, 8:16], vals[:, 8:16], work), t2)
            return t3

        sel = {}

        def score_head(h):
            def ev(p, tk):
                sel["q", h] = act(lambda e: e.activation(pq_T[:, 2 * h:2 * h + 2, :], p, ACT.Copy), tk, attn_done)
                return sel["q", h]
            feature_major(act_T, h2, DC, "peer_wq", ev)
            bank, was = take()
            for t in range(NT):
                for w in range(2):
                    o = (2 * t + w) * P
                    tk = mm(bank[:, o:o + P], pq_T[:, 2 * h + w, t * P:(t + 1) * P], keys_T[:, (2 * h + w) * P:(2 * h + w + 1) * P], True, True,
                            was, sel["q", h], keys_in, signal=(t == NT - 1 and w == 1))
            sel["s", h] = act(lambda e: e.activation(s_all[:, h], bank[:, :].rearrange("p (g n) -> p g n", g=TW), ACT.Copy), tk, x5)
            give(bank, sel["s", h])

        def best_keys(h):
            sel["keys", h] = top16([(s_all[:, h, g, :], s_work[:, g, :], v12[:, h, g // 2, g % 2, :], i12[:, h, g, :]) for g in range(TW)],
                                   [sel["s", h], x5])
            sel["i12f", h] = dve(lambda e: e.tensor_copy(i12f[:, h], i12[:, h]), sel["keys", h])
            sel["cand", h] = pool(lambda e: e.tensor_tensor(cand[:, h].rearrange("p t (a b) -> p t a b", a=TOPK),
                                                            v12[:, h, :, 0, :].unsqueeze(3).to_broadcast([P, NT, TOPK, TOPK]),
                                                            v12[:, h, :, 1, :].unsqueeze(2).to_broadcast([P, NT, TOPK, TOPK]), ALU.add), sel["keys", h])

        def best_pairs(h):
            t0 = top16([(cand[:, h, t, :], cand_work[:, t, :], topv[:, NT * h + t, :], topi[:, NT * h + t, :]) for t in range(NT)],
                       sel["cand", h])
            sel["topv", h] = t0
            ti = topi[:, NT * h:NT * (h + 1), :]
            dve(lambda e: e.tensor_scalar(ab[:, h, :, 0, :], ti, 4, None, ALU.logical_shift_right), t0)
            t1 = dve(lambda e: e.tensor_scalar(ab[:, h, :, 1, :], ti, 15, None, ALU.bitwise_and), t0)
            sel["ab", h] = dve(lambda e: e.tensor_copy(abf[:, h], ab[:, h].rearrange("p t w k -> p (t w) k")), t1)

        def match_places(h, lane):
            v = eq[:, h % 2]
            t0 = dve(lambda e: e.tensor_tensor(v, abf[:, h].unsqueeze(3).to_broadcast([P, TW, TOPK, TOPK]),
                                               iota16.unsqueeze(1).unsqueeze(1).to_broadcast([P, TW, TOPK, TOPK]), ALU.is_equal),
                     sel["ab", h], sel.get(("pick", h - 2)))
            sel["eq", h] = lane(lambda e: e.tensor_tensor(v, v, i12f[:, h].unsqueeze(2).to_broadcast([P, TW, TOPK, TOPK]), ALU.mult),
                                t0, sel["i12f", h])

        def sum_places(h):
            sel["pick", h] = dve(lambda e: e.tensor_reduce(pick[:, :, h, :], eq[:, h % 2], AXX, ALU.add), sel["eq", h])

        early_buf = [place(f"early{i}", 512, F32, o) for i, o in enumerate(OFF["early"])]
        early_done = {}

        def early_unit(e_):
            b, nth = e_ % len(early_buf), e_ // len(early_buf)
            buf = early_buf[b]
            stored = (s_early[b], 16 * nth) if nth else None
            t0 = feature_major(act_T, h2, DC, "peer_uT_early", lambda p, tk: act(lambda e: e.activation(by_chunk(buf), p, ACT.Gelu), tk, stored, attn_done, mix_ready))
            sp(lambda e: e.dma_start(parked_units[e_], buf).then_inc(s_early[b], 16), t0, signal=0)
            early_done[e_] = (s_early[b], 16 * (nth + 1))

        def select_head(h):
            if h < PE_H:
                best_keys(h)
            if h >= 2:
                sum_places(h - 2)
            if h >= 1:
                best_pairs(h - 1)
                if h == PE_H:
                    exponentials()
                match_places(h - 1, pool if h < PE_H else dve)

        def exponentials():
            tops = [sel["topv", h] for h in range(PE_H)]
            u0 = dve(lambda e: e.tensor_copy(best, topv[:, :, 0]), tops)
            u1 = dve(lambda e: e.tensor_tensor(topv, topv, best.unsqueeze(2).to_broadcast([P, NT * PE_H, TOPK]), ALU.subtract), u0)
            sel["exp"] = act(lambda e: e.activation(topv, topv, ACT.Exp), u1)

        count = dict(H=0, D=0, E=0)
        for what in SELECT_ORDER:
            {"H": score_head, "D": select_head, "E": early_unit}[what](count[what])
            count[what] += 1
        sum_places(PE_H - 1)
        u3 = dve(lambda e: e.tensor_reduce(total16, topv, AXX, ALU.add), sel["exp"])
        u4 = dve(lambda e: e.reciprocal(inv16, total16), u3)
        u5 = dve(lambda e: e.tensor_tensor(weight.rearrange("p t h k -> p h t k"), topv.rearrange("p (h t) k -> p h t k", t=NT),
                                           inv16.rearrange("p (h t) -> p h t", t=NT).unsqueeze(3).to_broadcast([P, PE_H, NT, TOPK]), ALU.mult), u4)
        picks_ready = []
        keys_picked = [sel["pick", h] for h in range(PE_H)]
        for t in range(NT):
            bank, was = take()
            for w, src in enumerate((pick[:, 2 * t], pick[:, 2 * t + 1], weight[:, t])):
                tk = turn(bank[:, w * P:(w + 1) * P], src.rearrange("p h k -> p (h k)"), was, keys_picked, u5, signal=(w == 2))
            ev = dve(lambda e, t=t, bank=bank: e.tensor_copy(pick_T.rearrange("p (w t) -> p w t", w=3)[:, :, t * P:(t + 1) * P],
                                                             bank[:, 0:3 * P].rearrange("p (w t) -> p w t", w=3)), tk)
            give(bank, ev)
            picks_ready.append(ev)

        Gw = place("G", G_WORDS)
        Gv = by_chunk(Gw)
        pT = pick_T.rearrange("p (w t) -> p w t", w=3)
        TG = 4
        hot_free = [picks_ready] * HID_BUFS
        hot = [place(f"hot{i}", 1024, F32, OFF["hid"] + 1024 * i).rearrange("p (w t n) -> p w t n", w=2, n=P) for i in range(HID_BUFS)]
        g_ready = []
        for q in range(T // TG):
            toks = slice(q * TG, (q + 1) * TG)
            bank, was = take()
            t0 = dve(lambda e, q=q, toks=toks: e.tensor_tensor(hot[q % HID_BUFS], iota.unsqueeze(1).unsqueeze(1).to_broadcast([P, 2, TG, P]),
                                                               pT[:, 0:2, toks].unsqueeze(3).to_broadcast([P, 2, TG, P]), ALU.is_equal), hot_free[q % HID_BUFS])
            tk = pool(lambda e, q=q, toks=toks: e.tensor_tensor(hot[q % HID_BUFS][:, 1], hot[q % HID_BUFS][:, 1], pT[:, 2, toks].unsqueeze(2).to_broadcast([P, TG, P]), ALU.mult), t0)
            for j in range(TG):
                m = mm(bank[:, j * P:(j + 1) * P], hot[q % HID_BUFS][:, 1, j, :], hot[q % HID_BUFS][:, 0, j, :], True, True, was, tk, signal=(j == TG - 1))
            hot_free[q % HID_BUFS] = m
            src = bank[:, :].rearrange("p (t i) -> p i t", t=TG)
            dst = Gv[:, :, toks]
            ev = act(lambda e, src=src, dst=dst: e.activation(dst, src, ACT.Copy), m, picks_ready, parked, h2, list(early_done.values()))
            give(bank, ev)
            g_ready.append(ev)

        acc = [take() for _ in range(4)]
        hid_free = [m] * HID_BUFS
        load_count = [0] * HID_BUFS
        for at in range(N_UNITS + V_LAG):
            if at < N_UNITS:
                i, u = at % HID_BUFS, order[at]
                hr = hid_raw[i]
                if u >= EARLY:
                    t0 = feature_major(act_T, h2, DC, "peer_uT", lambda p, tk, hr=hr, i=i: act(lambda e: e.activation(hr, p, ACT.Gelu), tk, hid_free[i]))
                else:
                    t0 = (s_hid[i], 16 * load_count[i])
                t1 = dve(lambda e, hr=hr, u=u: e.tensor_tensor(hr, hr, Gv[:, 2 * u:2 * u + 2, :], ALU.mult), t0, g_ready)
                hid_ready[at] = split_hid(i, t1)
            if at >= V_LAG:
                v = at - V_LAG
                fin_tick = hid_free[v % HID_BUFS] = rows_onto(acc, hid_pair[v % HID_BUFS], hid_ready[v], "peer_v", v == 0, v == N_UNITS - 1)
            if at + 1 < N_UNITS and order[at + 1] < EARLY:
                i, u = (at + 1) % HID_BUFS, order[at + 1]
                sp(lambda e, i=i, u=u: e.dma_start(hid_raw[i], parked_units[u].rearrange("p (c t) -> p c t", t=T)).then_inc(s_hid[i], 16),
                   hid_free[i], early_done[u], signal=0)
                load_count[i] += 1

        x_blk, g2_blk, fg_blk = use("parked_x")[0], use("parked_g2")[0], use("final_g")[0]
        x6 = []
        for half_ in range(2):
            for t in range(NT):
                bank, _ = acc[2 * half_ + t]
                tmp_ = Gw[:, (2 * half_ + t) * 512:(2 * half_ + t + 1) * 512]
                t0 = dve(lambda e, bank=bank, tmp_=tmp_, half_=half_: e.tensor_tensor(tmp_, bank[:, :], g2_blk.view[:, 0, half_ * 512:(half_ + 1) * 512], ALU.mult),
                         fin_tick[2 * half_ + t], g2_blk.arrived, t1)
                give(bank, t0)
                v = x_blk.view[:, t, half_ * 512:(half_ + 1) * 512]
                x6.append((pool, dve)[half_](lambda e, v=v, tmp_=tmp_: e.tensor_tensor(v, v, tmp_, ALU.add), t0, x_blk.arrived))
        done = final_norm(x_blk.view, Gw[:, 2048:4096].rearrange("p (t d) -> p t d", t=NT), x6, fg_blk)
        assert taken[0] == len(plan)
        for t in range(NT):
            act(lambda e, t=t: e.dma_start(out.rearrange("(t p) d -> p t d", p=P)[:, t, :], x_blk.view[:, t, :]).then_inc(s_out, 16), done[t], signal=0)
        act(lambda e: e.wait_ge(s_out, 16 * NT), signal=0)

        with nc.Block() as block:
            @block.sync
            def _(eng):
                sp.play(eng)

            @block.scalar
            def _(eng):
                act.play(eng)

            @block.vector
            def _(eng):
                dve.play(eng)

            @block.gpsimd
            def _(eng):
                pool.play(eng)

            @block.tensor
            def _(eng):
                pe.play(eng)


def constants():
    c = np.zeros((P, N_CONST), np.float32)
    c[:, K_IDENT:K_IDENT + P] = np.eye(P)
    c[:, K_ONES:K_ONES + P] = 1
    c[:, K_IOTA:K_IOTA + P] = np.arange(P)
    c[:, K_MASK + P:K_MASK + 2 * P] = np.where(np.arange(P)[None, :] <= np.arange(P)[:, None], 0, MASKED)
    for o, half, rot in ((0, HALF_M, ROPE), (HALF_M, HALF_D, DIFF_ROT)):
        c[:, K_FREQ + o:K_FREQ + o + half] = np.exp(np.float32(-math.log(THETA)) * np.arange(half, dtype=np.float32) * np.float32(2.0 / rot))
    return c


def pooling_band():
    t = np.arange(T)
    band = np.zeros((T, 4, T), np.float64)
    for g, w in enumerate(POOL_WINDOWS):
        lo, hi = np.clip(t - w // 2, 0, T), np.clip(t + w // 2, 0, T)
        inside = (t[:, None] >= lo[None, :]) & (t[:, None] < hi[None, :])
        band[:, g, :] = inside / (hi - lo)[None, :] - np.eye(T)
    return np.ascontiguousarray(band.astype(np.float32).reshape(NT, P, 4, T).transpose(1, 0, 2, 3).reshape(P, -1))


def window_bias(rpb):
    row, colm = np.arange(T) // GRID_W, np.arange(T) % GRID_W
    kh = min(NA_KH_MAX, ROWS)
    r0 = np.clip(row - kh // 2, 0, ROWS - kh)
    c0 = np.clip(colm - NA_KW // 2, 0, GRID_W - NA_KW)
    ok = ((row[None, :] >= r0[:, None]) & (row[None, :] < (r0 + kh)[:, None])
          & (colm[None, :] >= c0[:, None]) & (colm[None, :] < (c0 + NA_KW)[:, None]))
    ro = np.clip(row[None, :] - row[:, None] + NA_KH_MAX - 1, 0, 2 * NA_KH_MAX - 2)
    co = np.clip(colm[None, :] - colm[:, None] + NA_KW - 1, 0, 2 * NA_KW - 2)
    b = rpb[:, ro, co]
    b[:, ~ok] = MASKED
    return np.ascontiguousarray(b.reshape(NA_H, NT, P, T).transpose(2, 0, 1, 3).reshape(P, -1))


def kernel(**inputs):
    import concourse.bacc as bacc
    from concourse.bass_utils import run_bass_kernel_spmd

    v = {k: np.asarray(x) for k, x in inputs.items()}
    by_col = lambda x: x.reshape(-1, P).T
    arrays = {
        "x": v["x"][0],
        "pos": v["positions"].reshape(NT, P).T,
        "const": constants(),
        "cols": np.concatenate([by_col(v[n]) for n in (
            "norm_mix_g", "mla_q_norm_g", "mla_kv_norm_g", "b_gate", "norm_ffn_g", "c_2", "c_ctx_2", "norm1_g_2",
            "norm2_g_2", "pool_scale_2", "ada_b_2")], axis=1),
        "lam": np.concatenate([v[n].reshape(-1) for n in ("diff_lambda_q1", "diff_lambda_k1", "diff_lambda_q2", "diff_lambda_k2")]),
        "subln": v["diff_subln_g"][0],
        "w_in": v["w_in"][0], "w_uq": v["mla_w_uq"][0], "w_ukv": v["mla_w_ukv"][0],
        "w_b_mla": v["w_branch_mla"][0], "w_b_diff": v["w_branch_diff"][0], "w_out": v["w_out"][0],
        "w_gate": v["w_ffn_gate"][0], "w_up": v["w_ffn_up"][0], "w_down": v["w_ffn_down"][0],
        "norm_final_g": v["norm_final_g"],
        "ctx": v["ctx_2"][0], "ada_w": v["ada_w_2"][0],
        "ada_b_g1": v["ada_b_2"][0, 2 * D:3 * D], "ada_b_g2": v["ada_b_2"][0, 5 * D:6 * D],
        "w_in2": v["w_in_2"][0], "na_bias": window_bias(v["na_rpb_2"][0].copy()), "band": pooling_band(),
        "pool_w": v["pool_w_2"][0].transpose(1, 0, 2).reshape(P, -1), "w_out2": v["w_out_2"][0],
        "peer_wq": v["peer_wq_2"][0], "keys_T": v["peer_keys_2"][0].transpose(3, 0, 1, 2).reshape(P, -1),
        "peer_uT": v["peer_u_2"][0].T, "peer_v": v["peer_v_2"][0], "final_g": v["final_g_2"],
    }
    arrays = {k: np.ascontiguousarray(x) for k, x in arrays.items()}
    nc = bacc.Bacc("TRN2", target_bir_lowering=False, num_devices=1)
    aps = {k: nc.dram_tensor(k, x.shape, mybir.dt.from_np(x.dtype), kind="ExternalInput").ap() for k, x in arrays.items()}
    out = nc.dram_tensor("y", (T, D), F32, kind="ExternalOutput").ap()
    parked_x = nc.dram_tensor("parked_x", (T, D), F32, kind="Internal").ap()
    parked_g2 = nc.dram_tensor("parked_g2", (P, D), F32, kind="Internal").ap()
    parked_units = nc.dram_tensor("parked_units", (max(1, SELECT_ORDER.count("E")), P, 2 * T), F32, kind="Internal").ap()
    build(nc, aps, out, parked_x, parked_g2, parked_units)
    r = run_bass_kernel_spmd(nc, [arrays], core_ids=[0])
    return r.results[0]["y"].reshape(1, T, D)
```
